# Optimizing a Trainium2 kernel written in Bass

```python
import math
import jax, jax.numpy as jnp
from jax import lax
import numpy as np

D_MODEL = 1024
BATCH = 1
SEQ = 256
DEPTH = 2

CHUNK = 64
QBLOCK = 128
EPS = 1e-6
NEG_INF = -1e30

LRU_WIDTH = 512
LRU_HEADS = 8
LRU_HEAD_DIM = LRU_WIDTH // LRU_HEADS
CONV_WIDTH = 4
LRU_C = 8.0

MLA_HEADS = 8
MLA_Q_LORA = 384
MLA_KV_LORA = 256
MLA_NOPE = 64
MLA_ROPE = 32
MLA_V = 64
ROPE_BASE = 10000.0

FOX_HEADS = 8
FOX_HEAD_DIM = 64
FOX_WIDTH = FOX_HEADS * FOX_HEAD_DIM

N_BRANCH = 3
D_FF = ((8 * D_MODEL // 3 + 255) // 256) * 256
PLE_DIM = 256

SPLIT_SIZES = (
    LRU_WIDTH,
    LRU_WIDTH,
    MLA_Q_LORA,
    MLA_KV_LORA + MLA_ROPE,
    FOX_WIDTH,
    FOX_WIDTH,
    FOX_WIDTH,
    FOX_HEADS,
    N_BRANCH * D_MODEL,
)
D_IN = 2 * LRU_WIDTH + MLA_Q_LORA + MLA_KV_LORA + MLA_ROPE + 3 * FOX_WIDTH + FOX_HEADS + N_BRANCH * D_MODEL


def rmsnorm(x, g):
    xf = x.astype(jnp.float32)
    y = xf * lax.rsqrt(jnp.mean(xf * xf, axis=-1, keepdims=True) + EPS)
    return (y * g.astype(jnp.float32)).astype(x.dtype)

def split_columns(z):
    idx = []
    acc = 0
    for s in SPLIT_SIZES[:-1]:
        acc += s
        idx.append(acc)
    return jnp.split(z, idx, axis=-1)

def rope(x, cos, sin):
    half = x.shape[-1] // 2
    x1, x2 = x[..., :half], x[..., half:]
    c = cos[None, :, None, :].astype(x.dtype)
    s = sin[None, :, None, :].astype(x.dtype)
    return jnp.concatenate([x1 * c - x2 * s, x2 * c + x1 * s], axis=-1)

def block_attention(q, k, v, scale, unit, decay=None):
    B, S, H, Dk = q.shape
    nb = S // QBLOCK
    q_blocks = q.reshape(B, nb, QBLOCK, H, Dk).transpose(1, 0, 2, 3, 4)
    key_unit = jnp.arange(S) // unit
    decay_t = None if decay is None else decay.transpose(0, 2, 1)

    def one_block(args):
        ib, q_blk = args
        s = jnp.einsum('bqhd,bkhd->bhqk', q_blk, k, preferred_element_type=jnp.float32) * scale
        if decay_t is not None:
            dq = lax.dynamic_slice_in_dim(decay_t, ib * QBLOCK, QBLOCK, axis=2)
            s = s + dq[:, :, :, None] - decay_t[:, :, None, :]
        q_unit = (ib * QBLOCK + jnp.arange(QBLOCK)) // unit
        mask = q_unit[:, None] >= key_unit[None, :]
        s = jnp.where(mask[None, None], s, NEG_INF)
        pr = jax.nn.softmax(s, axis=-1)
        return jnp.einsum('bhqk,bkhd->bqhd', pr.astype(v.dtype), v)

    out = lax.map(one_block, (jnp.arange(nb), q_blocks))
    return out.transpose(1, 0, 2, 3, 4).reshape(B, S, H, v.shape[-1])

def _lru_combine(left, right):
    a1, b1 = left
    a2, b2 = right
    return a1 * a2, a2 * b1 + b2

def rglru_branch(u, u_gate, conv_w, conv_b, wa, ba, wx, bx, lam):
    B, S, W = u.shape
    up = jnp.pad(u, ((0, 0), (CONV_WIDTH - 1, 0), (0, 0)))
    xc = conv_b + up[:, 0:S] * conv_w[0]
    for kk in range(1, CONV_WIDTH):
        xc = xc + up[:, kk:kk + S] * conv_w[kk]
    xh = xc.reshape(B, S, LRU_HEADS, LRU_HEAD_DIM)
    r = jax.nn.sigmoid(jnp.einsum('bshi,hij->bshj', xh, wa).reshape(B, S, W) + ba)
    ig = jax.nn.sigmoid(jnp.einsum('bshi,hij->bshj', xh, wx).reshape(B, S, W) + bx)
    log_a = -LRU_C * r.astype(jnp.float32) * jax.nn.softplus(-lam.astype(jnp.float32))
    a = jnp.exp(log_a)
    b = jnp.sqrt(-jnp.expm1(2.0 * log_a)) * (ig * xc).astype(jnp.float32)
    _, h = lax.associative_scan(_lru_combine, (a, b), axis=1)
    return h.astype(u.dtype) * jax.nn.gelu(u_gate)

def mla_branch(c_q, ckv_rope, q_norm, wuq, kv_norm, wukv, cos, sin):
    B, S, _ = c_q.shape
    q = (rmsnorm(c_q, q_norm) @ wuq).reshape(B, S, MLA_HEADS, MLA_NOPE + MLA_ROPE)
    q_nope, q_rope = q[..., :MLA_NOPE], q[..., MLA_NOPE:]
    c_kv, k_rope = ckv_rope[..., :MLA_KV_LORA], ckv_rope[..., MLA_KV_LORA:]
    kv = (rmsnorm(c_kv, kv_norm) @ wukv).reshape(B, S, MLA_HEADS, MLA_NOPE + MLA_V)
    k_nope, v = kv[..., :MLA_NOPE], kv[..., MLA_NOPE:]
    q_rope = rope(q_rope, cos, sin)
    k_rope = rope(k_rope[:, :, None, :], cos, sin)
    q_full = jnp.concatenate([q_nope, q_rope], axis=-1)
    k_full = jnp.concatenate([k_nope, jnp.broadcast_to(k_rope, (B, S, MLA_HEADS, MLA_ROPE))], axis=-1)
    o = block_attention(q_full, k_full, v, (MLA_NOPE + MLA_ROPE) ** -0.5, CHUNK)
    return o.reshape(B, S, MLA_HEADS * MLA_V)

def fox_branch(fq, fk, fv, f_logit, bf):
    B, S, _ = fq.shape
    q = fq.reshape(B, S, FOX_HEADS, FOX_HEAD_DIM)
    k = fk.reshape(B, S, FOX_HEADS, FOX_HEAD_DIM)
    v = fv.reshape(B, S, FOX_HEADS, FOX_HEAD_DIM)
    log_f = jax.nn.log_sigmoid((f_logit + bf).astype(jnp.float32))
    cum = jnp.cumsum(log_f, axis=1)
    o = block_attention(q, k, v, FOX_HEAD_DIM ** -0.5, 1, decay=cum)
    return o.reshape(B, S, FOX_WIDTH)

def first_inputs(seed: int = 0) -> dict:
    key = jax.random.key(seed)
    ks = jax.random.split(key, 32)

    def nrm(k, shape, scale):
        return jax.random.normal(k, shape, jnp.float32) * scale

    def gain(k, shape):
        return 1.0 + 0.05 * jax.random.normal(k, shape, jnp.float32)

    u = jax.random.uniform(ks[10], (DEPTH, LRU_WIDTH), jnp.float32, 0.9, 0.999)
    a = u ** (1.0 / LRU_C)
    lru_lambda = jnp.log(a) - jnp.log1p(-a)

    return {
        "x": nrm(ks[0], (BATCH, SEQ, D_MODEL), 1.0),
        "p": nrm(ks[1], (DEPTH, BATCH, SEQ, PLE_DIM), 1.0),
        "mix_norm": gain(ks[2], (DEPTH, D_MODEL)),
        "w_in": nrm(ks[3], (DEPTH, D_MODEL, D_IN), D_MODEL ** -0.5),
        "gate_b": nrm(ks[4], (DEPTH, N_BRANCH * D_MODEL), 0.1),
        "conv_w": nrm(ks[5], (DEPTH, CONV_WIDTH, LRU_WIDTH), CONV_WIDTH ** -0.5),
        "conv_b": nrm(ks[6], (DEPTH, LRU_WIDTH), 0.1),
        "lru_wa": nrm(ks[7], (DEPTH, LRU_HEADS, LRU_HEAD_DIM, LRU_HEAD_DIM), LRU_HEAD_DIM ** -0.5),
        "lru_ba": nrm(ks[8], (DEPTH, LRU_WIDTH), 0.1),
        "lru_wx": nrm(ks[9], (DEPTH, LRU_HEADS, LRU_HEAD_DIM, LRU_HEAD_DIM), LRU_HEAD_DIM ** -0.5),
        "lru_bx": nrm(ks[11], (DEPTH, LRU_WIDTH), 0.1),
        "lru_lambda": lru_lambda,
        "mla_q_norm": gain(ks[12], (DEPTH, MLA_Q_LORA)),
        "mla_wuq": nrm(ks[13], (DEPTH, MLA_Q_LORA, MLA_HEADS * (MLA_NOPE + MLA_ROPE)), MLA_Q_LORA ** -0.5),
        "mla_kv_norm": gain(ks[14], (DEPTH, MLA_KV_LORA)),
        "mla_wukv": nrm(ks[15], (DEPTH, MLA_KV_LORA, MLA_HEADS * (MLA_NOPE + MLA_V)), MLA_KV_LORA ** -0.5),
        "fox_bf": jax.random.uniform(ks[16], (DEPTH, FOX_HEADS), jnp.float32, 1.0, 5.0),
        "w_br_a": nrm(ks[17], (DEPTH, LRU_WIDTH, D_MODEL), LRU_WIDTH ** -0.5),
        "w_br_b": nrm(ks[18], (DEPTH, MLA_HEADS * MLA_V, D_MODEL), (MLA_HEADS * MLA_V) ** -0.5),
        "w_br_c": nrm(ks[19], (DEPTH, FOX_WIDTH, D_MODEL), FOX_WIDTH ** -0.5),
        "w_o": nrm(ks[20], (DEPTH, D_MODEL, D_MODEL), D_MODEL ** -0.5),
        "ffn_norm": gain(ks[21], (DEPTH, D_MODEL)),
        "w_gate_up": nrm(ks[22], (DEPTH, D_MODEL, 2 * D_FF), D_MODEL ** -0.5),
        "w_down": nrm(ks[23], (DEPTH, D_FF, D_MODEL), D_FF ** -0.5),
        "ple_norm": gain(ks[24], (DEPTH, D_MODEL)),
        "w_ple_gate": nrm(ks[25], (DEPTH, D_MODEL, D_MODEL), D_MODEL ** -0.5),
        "w_ple": nrm(ks[26], (DEPTH, PLE_DIM, D_MODEL), PLE_DIM ** -0.5),
        "final_norm": gain(ks[27], (D_MODEL,)),
    }

def first_block(x, p, mix_norm, w_in, gate_b, conv_w, conv_b, lru_wa, lru_ba, lru_wx, lru_bx, lru_lambda,
              mla_q_norm, mla_wuq, mla_kv_norm, mla_wukv, fox_bf, w_br_a, w_br_b, w_br_c, w_o,
              ffn_norm, w_gate_up, w_down, ple_norm, w_ple_gate, w_ple, final_norm):
    B, S, D = x.shape
    pos = jnp.arange(S, dtype=jnp.float32)
    inv_freq = ROPE_BASE ** (-jnp.arange(0, MLA_ROPE, 2, dtype=jnp.float32) / MLA_ROPE)
    ang = pos[:, None] * inv_freq[None, :]
    cos, sin = jnp.cos(ang), jnp.sin(ang)

    for i in range(DEPTH):
        h = rmsnorm(x, mix_norm[i])
        z = h @ w_in[i]
        u_rnn, u_gelu, c_q, ckv_rope, fq, fk, fv, f_logit, gate_logit = split_columns(z)
        y_a = rglru_branch(u_rnn, u_gelu, conv_w[i], conv_b[i], lru_wa[i], lru_ba[i],
                           lru_wx[i], lru_bx[i], lru_lambda[i]) @ w_br_a[i]
        y_b = mla_branch(c_q, ckv_rope, mla_q_norm[i], mla_wuq[i], mla_kv_norm[i],
                         mla_wukv[i], cos, sin) @ w_br_b[i]
        y_c = fox_branch(fq, fk, fv, f_logit, fox_bf[i]) @ w_br_c[i]
        g = jax.nn.sigmoid(gate_logit + gate_b[i]).reshape(B, S, N_BRANCH, D)
        merged = g[:, :, 0] * y_a + g[:, :, 1] * y_b + g[:, :, 2] * y_c
        x = x + merged @ w_o[i]
        hf = rmsnorm(x, ffn_norm[i]) @ w_gate_up[i]
        x = x + (jax.nn.silu(hf[..., :D_FF]) * hf[..., D_FF:]) @ w_down[i]
        pg = jax.nn.sigmoid(rmsnorm(x, ple_norm[i]) @ w_ple_gate[i])
        x = x + pg * (p[i] @ w_ple[i])
    return rmsnorm(x, final_norm)


GRID_W = 64
CTX_LEN = 256
N_MIXERS = 3
POOL_WINDOWS = (2, 4, 8, 16)
POOL_GROUPS = 4
POOL_GW = D_MODEL // POOL_GROUPS
HEAD_DIM = 128
N_HEADS = D_MODEL // HEAD_DIM
N_KV_HEADS = N_HEADS // 2
QKV_WIDTH = (N_HEADS + 2 * N_KV_HEADS) * HEAD_DIM
Q_BLOCK = 128
CHUNK_2 = 128
GMLP_HALF = 2 * D_MODEL
GMLP_GROUPS = 8
GMLP_GW = GMLP_HALF // GMLP_GROUPS
D_FF_2 = 4 * D_MODEL


def n_layers_of(kind):
    return len(range(kind, DEPTH, N_MIXERS))

def rms_norm(x, g):
    xf = x.astype(jnp.float32)
    y = xf * lax.rsqrt(jnp.mean(xf * xf, axis=-1, keepdims=True) + EPS)
    return (y * g.astype(jnp.float32)).astype(x.dtype)

def layer_norm(x, g, b):
    xf = x.astype(jnp.float32)
    mu = jnp.mean(xf, axis=-1, keepdims=True)
    xc = xf - mu
    y = xc * lax.rsqrt(jnp.mean(xc * xc, axis=-1, keepdims=True) + EPS)
    return (y * g.astype(jnp.float32) + b.astype(jnp.float32)).astype(x.dtype)

def modulate(h, shift, scale):
    return h * (1 + scale[:, None, :]) + shift[:, None, :]

def pool_mix(h, w, scale):
    B, L, D = h.shape
    hf = h.astype(jnp.float32)
    cs = jnp.concatenate([jnp.zeros((B, 1, D), jnp.float32), jnp.cumsum(hf, axis=1)], axis=1)
    csg = cs.reshape(B, L + 1, POOL_GROUPS, POOL_GW)
    hg = hf.reshape(B, L, POOL_GROUPS, POOL_GW)
    pos = jnp.arange(L)
    outs = []
    for g, win in enumerate(POOL_WINDOWS):
        lo = jnp.clip(pos - win // 2, 0, L)
        hi = jnp.clip(pos + win - win // 2, 0, L)
        s = jnp.take(csg[:, :, g], hi, axis=1) - jnp.take(csg[:, :, g], lo, axis=1)
        cnt = (hi - lo).astype(jnp.float32)[None, :, None]
        outs.append(s / cnt - hg[:, :, g])
    p = jnp.stack(outs, axis=2).astype(h.dtype)
    y = jnp.einsum("blgc,gcd->blgd", p, w).reshape(B, L, D)
    return y * scale

def axial_rope_tables(L):
    rows_n = L // GRID_W
    row = jnp.repeat(jnp.arange(rows_n), GRID_W).astype(jnp.float32)
    col = jnp.tile(jnp.arange(GRID_W), rows_n).astype(jnp.float32)
    half = HEAD_DIM // 2
    inv = ROPE_BASE ** (-jnp.arange(0, half, 2, dtype=jnp.float32) / half)
    ang_r = row[:, None] * inv[None, :]
    ang_c = col[:, None] * inv[None, :]
    return jnp.cos(ang_r), jnp.sin(ang_r), jnp.cos(ang_c), jnp.sin(ang_c)

def rotate(x, cos, sin):
    x1, x2 = jnp.split(x, 2, axis=-1)
    cos = cos[None, :, None, :]
    sin = sin[None, :, None, :]
    return jnp.concatenate([x1 * cos - x2 * sin, x1 * sin + x2 * cos], axis=-1)

def apply_axial_rope(x, tables):
    cr, sr, cc, scol = tables
    xf = x.astype(jnp.float32)
    xr, xc = jnp.split(xf, 2, axis=-1)
    return jnp.concatenate([rotate(xr, cr, sr), rotate(xc, cc, scol)], axis=-1).astype(x.dtype)

def gqa_core(q, k, v):
    B, Lq = q.shape[0], q.shape[1]
    G = N_HEADS // N_KV_HEADS
    qg = q.reshape(B, Lq, N_KV_HEADS, G, HEAD_DIM)
    s = jnp.einsum("bqkgd,bskd->bkgqs", qg, k).astype(jnp.float32) * (HEAD_DIM ** -0.5)
    p = jax.nn.softmax(s, axis=-1).astype(v.dtype)
    o = jnp.einsum("bkgqs,bskd->bqkgd", p, v)
    return o.reshape(B, Lq, N_HEADS * HEAD_DIM)

def qkv_proj(h, w_qkv, q_g, k_g):
    B, L, _ = h.shape
    qkv = h @ w_qkv
    q, k, v = jnp.split(qkv, [N_HEADS * HEAD_DIM, (N_HEADS + N_KV_HEADS) * HEAD_DIM], axis=-1)
    q = rms_norm(q.reshape(B, L, N_HEADS, HEAD_DIM), q_g)
    k = rms_norm(k.reshape(B, L, N_KV_HEADS, HEAD_DIM), k_g)
    v = v.reshape(B, L, N_KV_HEADS, HEAD_DIM)
    return q, k, v

def attn_mix(h_ctx, h_lat, w_qkv, w_o, q_g, k_g, ctx_out):
    B, S, _ = h_lat.shape
    qc, kc, vc = qkv_proj(h_ctx, w_qkv, q_g, k_g)
    ql, kl, vl = qkv_proj(h_lat, w_qkv, q_g, k_g)
    tables = axial_rope_tables(S)
    ql = apply_axial_rope(ql, tables)
    kl = apply_axial_rope(kl, tables)
    k_all = jnp.concatenate([kc, kl], axis=1)
    v_all = jnp.concatenate([vc, vl], axis=1)
    nb = S // Q_BLOCK
    qb = ql.reshape(B, nb, Q_BLOCK, N_HEADS, HEAD_DIM).transpose(1, 0, 2, 3, 4)
    ob = lax.map(lambda qq: gqa_core(qq, k_all, v_all), qb)
    y_lat = ob.transpose(1, 0, 2, 3).reshape(B, S, N_HEADS * HEAD_DIM) @ w_o
    y_ctx = gqa_core(qc, kc, vc) @ w_o if ctx_out else None
    return y_ctx, y_lat

def gmlp_mix(h, w_in, ln_g, ln_b, ws, bs, w_out):
    B, L, _ = h.shape
    z = jax.nn.gelu(h @ w_in)
    u, v = jnp.split(z, 2, axis=-1)
    v = layer_norm(v, ln_g, ln_b)
    vg = v.reshape(B, L // CHUNK_2, CHUNK_2, GMLP_GROUPS, GMLP_GW)
    sv = jnp.einsum("gqp,bnpgc->bnqgc", ws, vg) + bs.T[None, None, :, :, None]
    return (u * sv.reshape(B, L, GMLP_HALF)) @ w_out

def sq_relu_mlp(h, w1, w2):
    return jnp.square(jax.nn.relu(h @ w1)) @ w2

def second_inputs(seed: int = 0) -> dict:
    key = jax.random.key(seed)
    ks = jax.random.split(key, 24)
    f32 = jnp.float32
    D = D_MODEL
    nP, nA, nG = n_layers_of(0), n_layers_of(1), n_layers_of(2)

    def nrm(k, shape, s):
        return jax.random.normal(k, shape, f32) * s

    return {
        "x": nrm(ks[0], (BATCH, SEQ, D), 1.0),
        "c": nrm(ks[1], (BATCH, D), 1.0),
        "ctx": nrm(ks[2], (BATCH, CTX_LEN, D), 1.0),
        "c_ctx": nrm(ks[3], (D,), 1.0),
        "ada_w": nrm(ks[4], (DEPTH, D, 6 * D), 0.5 * D ** -0.5),
        "ada_b": nrm(ks[5], (DEPTH, 6 * D), 0.02),
        "norm_g": 1.0 + nrm(ks[6], (DEPTH, 2, D), 0.02),
        "mlp_w1": nrm(ks[7], (DEPTH, D, D_FF_2), D ** -0.5),
        "mlp_w2": nrm(ks[8], (DEPTH, D_FF_2, D), D_FF_2 ** -0.5),
        "pool_w": nrm(ks[9], (nP, POOL_GROUPS, POOL_GW, POOL_GW), POOL_GW ** -0.5),
        "pool_scale": 1.0 + nrm(ks[10], (nP, D), 0.02),
        "attn_w_qkv": nrm(ks[11], (nA, D, QKV_WIDTH), D ** -0.5),
        "attn_w_o": nrm(ks[12], (nA, N_HEADS * HEAD_DIM, D), (N_HEADS * HEAD_DIM) ** -0.5),
        "attn_q_g": 1.0 + nrm(ks[13], (nA, HEAD_DIM), 0.02),
        "attn_k_g": 1.0 + nrm(ks[14], (nA, HEAD_DIM), 0.02),
        "gm_w_in": nrm(ks[15], (nG, D, 2 * GMLP_HALF), D ** -0.5),
        "gm_ln_g": 1.0 + nrm(ks[16], (nG, GMLP_HALF), 0.02),
        "gm_ln_b": nrm(ks[17], (nG, GMLP_HALF), 0.02),
        "gm_ws": nrm(ks[18], (nG, GMLP_GROUPS, CHUNK_2, CHUNK_2), CHUNK_2 ** -0.5),
        "gm_bs": nrm(ks[19], (nG, GMLP_GROUPS, CHUNK_2), 0.02),
        "gm_w_out": nrm(ks[20], (nG, GMLP_HALF, D), GMLP_HALF ** -0.5),
        "final_g": 1.0 + nrm(ks[21], (D,), 0.02),
    }

def second_block(x, c, ctx, c_ctx, ada_w, ada_b, norm_g, mlp_w1, mlp_w2, pool_w, pool_scale,
              attn_w_qkv, attn_w_o, attn_q_g, attn_k_g, gm_w_in, gm_ln_g, gm_ln_b, gm_ws, gm_bs,
              gm_w_out, final_g):
    last_ctx_read = max([i for i in range(DEPTH) if i % N_MIXERS == 1], default=-1)
    s_lat = jax.nn.silu(c)
    s_ctx = jax.nn.silu(c_ctx)[None, :]
    h_lat, h_ctx = x, ctx
    for i in range(DEPTH):
        kind, j = i % N_MIXERS, i // N_MIXERS
        ctx_in = i <= last_ctx_read
        ctx_out = i < last_ctx_read
        sh1, sc1, g1, sh2, sc2, g2 = jnp.split(s_lat @ ada_w[i] + ada_b[i], 6, axis=-1)
        a_l = modulate(rms_norm(h_lat, norm_g[i, 0]), sh1, sc1)
        if ctx_in:
            csh1, csc1, cg1, csh2, csc2, cg2 = jnp.split(s_ctx @ ada_w[i] + ada_b[i], 6, axis=-1)
            a_c = modulate(rms_norm(h_ctx, norm_g[i, 0]), csh1, csc1)
        y_c = None
        if kind == 0:
            y_l = pool_mix(a_l, pool_w[j], pool_scale[j])
            if ctx_out:
                y_c = pool_mix(a_c, pool_w[j], pool_scale[j])
        elif kind == 1:
            y_c, y_l = attn_mix(a_c, a_l, attn_w_qkv[j], attn_w_o[j], attn_q_g[j], attn_k_g[j], ctx_out)
        else:
            y_l = gmlp_mix(a_l, gm_w_in[j], gm_ln_g[j], gm_ln_b[j], gm_ws[j], gm_bs[j], gm_w_out[j])
            if ctx_out:
                y_c = gmlp_mix(a_c, gm_w_in[j], gm_ln_g[j], gm_ln_b[j], gm_ws[j], gm_bs[j], gm_w_out[j])
        h_lat = h_lat + g1[:, None, :] * y_l
        m_l = modulate(rms_norm(h_lat, norm_g[i, 1]), sh2, sc2)
        h_lat = h_lat + g2[:, None, :] * sq_relu_mlp(m_l, mlp_w1[i], mlp_w2[i])
        if ctx_out:
            h_ctx = h_ctx + cg1[:, None, :] * y_c
            m_c = modulate(rms_norm(h_ctx, norm_g[i, 1]), csh2, csc2)
            h_ctx = h_ctx + cg2[:, None, :] * sq_relu_mlp(m_c, mlp_w1[i], mlp_w2[i])
    return rms_norm(h_lat, final_g)


def setup_inputs(seed=0):
    out = dict(first_inputs(seed))
    for name, value in second_inputs(seed + 1).items():
        if name != "x":
            out[name + "_2"] = value
    return out


def reference(
    x, p, mix_norm, w_in, gate_b, conv_w, conv_b, lru_wa, lru_ba, lru_wx, lru_bx, lru_lambda,
    mla_q_norm, mla_wuq, mla_kv_norm, mla_wukv, fox_bf, w_br_a, w_br_b, w_br_c, w_o, ffn_norm,
    w_gate_up, w_down, ple_norm, w_ple_gate, w_ple, final_norm, c_2, ctx_2, c_ctx_2, ada_w_2,
    ada_b_2, norm_g_2, mlp_w1_2, mlp_w2_2, pool_w_2, pool_scale_2, attn_w_qkv_2, attn_w_o_2,
    attn_q_g_2, attn_k_g_2, gm_w_in_2, gm_ln_g_2, gm_ln_b_2, gm_ws_2, gm_bs_2, gm_w_out_2,
    final_g_2,
):
    x = first_block(
        x, p, mix_norm, w_in, gate_b, conv_w, conv_b, lru_wa, lru_ba, lru_wx, lru_bx,
        lru_lambda, mla_q_norm, mla_wuq, mla_kv_norm, mla_wukv, fox_bf, w_br_a, w_br_b, w_br_c,
        w_o, ffn_norm, w_gate_up, w_down, ple_norm, w_ple_gate, w_ple, final_norm,
    )
    return second_block(
        x, c_2, ctx_2, c_ctx_2, ada_w_2, ada_b_2, norm_g_2, mlp_w1_2, mlp_w2_2, pool_w_2,
        pool_scale_2, attn_w_qkv_2, attn_w_o_2, attn_q_g_2, attn_k_g_2, gm_w_in_2, gm_ln_g_2,
        gm_ln_b_2, gm_ws_2, gm_bs_2, gm_w_out_2, final_g_2,
    )


_drawn_inputs = setup_inputs


def setup_inputs(seed=0):
    import zlib

    import numpy as np

    out = dict(_drawn_inputs(seed))
    spreads = {}
    factors = {'gate_b': 3.213,
     'lru_ba': 8.0,
     'lru_bx': 4.426,
     'mla_q_norm': 8.0,
     'mla_kv_norm': 7.271,
     'ple_norm': 5.149,
     'ctx_2': 4.014,
     'norm_g_2': 4.357,
     'pool_scale_2': 8.0,
     'attn_q_g_2': 23.6,
     'attn_k_g_2': 26.09,
     'final_g_2': 8.28}
    for name, (base, spread) in spreads.items():
        noise = np.random.default_rng([zlib.crc32(name.encode()), seed]).standard_normal(out[name].shape)
        drawn = base * np.exp(spread * noise) if base else spread * noise
        out[name] = __import__('jax').numpy.asarray(drawn.astype(out[name].dtype))
    for name, factor in factors.items():
        out[name] = (out[name] * factor).astype(out[name].dtype)
    return out
```

```python
from contextlib import ExitStack

import numpy as np

import concourse.bass as bass
from concourse import mybir

F32 = mybir.dt.float32
F32R = mybir.dt.float32r
ALU = mybir.AluOpType
ACT = mybir.ActivationFunctionType
AXX = mybir.AxisListType.X

P = 128
D = 1024
S = 256
DEPTH = 2
KT = D // P
LRU_T = 512 // P
CONV = 4
Q_LORA_T = 384 // P
KV_LORA_T = 256 // P
HEADS = 8
D_FF = 2816
FF_T = D_FF // P
HALF_T = FF_T // 2
PLE_T = 256 // P
EPS = 1e-6
MLA_SCALE = 96.0 ** -0.5
FOX_SCALE = 64.0 ** -0.5
GELU_C = (2.0 / np.pi) ** 0.5
BIG = 1.0e30

CHUNK_ATOMS = 10
RING = 4
CH = CHUNK_ATOMS * P
AHEAD = 3

PAR = {}
_n = 0
for _name, _w in (("mix_g", 8), ("gate_b", 24), ("conv_w", 16), ("conv_b", 4), ("ba", 4), ("bx", 4), ("lam", 4),
                  ("q_g", 3), ("kv_g", 2), ("ffn_g", 8), ("ple_g", 8), ("bf", 1)):
    PAR[_name] = _n
    _n += _w
NPAR = _n

ATOMS_OF = {"ss": 0, "u": 8, "gl": 8, "cq": 8, "ckv": 8, "kr": 8, "col": 0, "wa": 1, "wx": 1, "rotk": 0,
            "fv": 32, "vm": 8, "kn": 2, "qn": 3, "qr": 3, "rotq": 0, "fl": 8, "fq": 8, "fk": 8, "g": 8, "y": 4,
            "wo": 8, "hg": 8, "hu": 8, "dn": 11, "pg": 8, "pp": 2}
BRANCH_TILES = [[t for n in range(8) for t in (("g", b, n), ("y", b, n))] for b in range(3)]
HEAD_TILES = (
    [("ss", "mix")] + [("u", j) for j in range(4)] + [("gl", j) for j in range(4)]
    + [("cq", j) for j in range(3)] + [("ckv", j) for j in range(2)] + [("kr", 0)]
    + [("ss", "q"), ("ss", "kv"), ("col", "mix")]
    + [("wa", j) for j in range(4)] + [("wx", j) for j in range(4)]
    + [("rotk", 0), ("fv", 0), ("fv", 1), ("col", "kv"), ("vm", 0), ("vm", 1)]
    + [("kn", j) for j in range(4)] + [("qn", j) for j in range(4)] + [("qr", 0), ("qr", 1)]
    + [("rotq", 0), ("rotq", 1)])
MLA_FILL = [("fl", 0)] + [("fq", j) for j in range(4)] + [("fk", j) for j in range(4)] + BRANCH_TILES[0][:7]
FOX_FILL = BRANCH_TILES[0][7:] + BRANCH_TILES[1][:7]
MID_TILES = BRANCH_TILES[1][7:] + BRANCH_TILES[2]
TAIL_TILES = (
    [("wo", n) for n in range(8)] + [("ss", "ffn")]
    + [t for h in range(2) for t in [u for j in range(HALF_T) for u in (("hg", h, j), ("hu", h, j))]
       + [("dn", h, n) for n in range(8)]]
    + [("ss", "ple")] + [t for n in range(8) for t in (("pg", n), ("pp", n))])
TILES = HEAD_TILES + MLA_FILL + FOX_FILL + MID_TILES + TAIL_TILES
TILE_NO = {t: i for i, t in enumerate(TILES)}
N_TILES = len(TILES)
N_BANKS = 4
TILES_PER_LAYER = -(-N_TILES // N_BANKS) * N_BANKS
SHARED = {("fv", 1), ("vm", 1)}


def first_atoms():
    at, out = 0, {}
    for t in TILES:
        if t in SHARED:
            out[t] = (out[(t[0], 0)][0], out[(t[0], 0)][1])
            continue
        out[t] = (at, at + ATOMS_OF[t[0]])
        at += ATOMS_OF[t[0]]
    return out, at


ATOM_SPAN, LAYER_ATOMS = first_atoms()
LAYER_CHUNKS = -(-LAYER_ATOMS // (CHUNK_ATOMS * RING)) * RING


def last_chunk(span):
    return max(span[1] - 1, 0) // CHUNK_ATOMS


MOD_T = 6 * D // P
MLP_T = 4 * D // P
QUARTERS = 4
QT = MLP_T // QUARTERS
KV_HEADS = 4
B2_ATOMS_ADA = DEPTH * MOD_T * KT
B2 = {}
_at = 0
for _name, _n in (("ada", B2_ATOMS_ADA), ("pool", 16), ("mlp0", 2 * MLP_T * KT), ("q", 64), ("k", 32), ("v", 32),
                  ("o", 64), ("mlp1", 2 * MLP_T * KT)):
    B2[_name] = _at
    _at += _n
B2_ATOMS = _at
B2_CHUNKS = -(-B2_ATOMS // (CHUNK_ATOMS * RING)) * RING
N_CHUNKS = DEPTH * LAYER_CHUNKS + B2_CHUNKS

ADA_GROUPS = MOD_T // 8


def mlp_tiles(l):
    return [t for q in range(QUARTERS) for t in [("w1", l, q, j) for j in range(QT)] + [("w2", l, q, n) for n in range(KT)]]


def staggered(name, n):
    out = []
    for j in range(n + 2):
        out += [(name, j)] if j < n else []
        out += [(name + "ss", j - 1)] if 0 <= j - 1 < n else []
        out += [(name + "rot", j - 2)] if j >= 2 else []
    return out


def ada_tiles():
    out = []
    for n in range(DEPTH * ADA_GROUPS):
        for i in range(4):
            out.append(("ada", n // ADA_GROUPS, n % ADA_GROUPS * 4 + i))
            if i == 0 and n:
                out.append(("turn", (n - 1) // ADA_GROUPS, (n - 1) % ADA_GROUPS))
    return out + [("turn", DEPTH - 1, ADA_GROUPS - 1)]


ATOMS_OF2 = {"ada": 16, "pool": 2, "w1": 8, "w2": 8, "q": 8, "k": 8, "v": 32, "o": 8}
TILES2 = (
    [("ss", "first")]
    + ada_tiles()
    + [("ss", 0, 0)] + [("pool", t) for t in range(KT)]
    + [("ss", 0, 1)] + mlp_tiles(0)
    + [("ss", 1, 0)] + staggered("q", 8) + staggered("k", KV_HEADS) + [("v", m) for m in range(4)]
    + [("o", n) for n in range(KT)]
    + [("ss", 1, 1)] + mlp_tiles(1) + [("ss", "last")])
TILE_NO2 = {t: i for i, t in enumerate(TILES2)}


def second_spans():
    at, out = 0, {}
    for t in TILES2:
        n = 0 if t[0] == "v" and t[1] else ATOMS_OF2.get(t[0], 0)
        if t[0] == "v" and t[1]:
            out[t] = out[("v", 0)]
            continue
        out[t] = (at, at + n)
        at += n
    assert at == B2_ATOMS, (at, B2_ATOMS)
    return out


ATOM_SPAN2 = second_spans()
FIRST_CHUNK2 = DEPTH * LAYER_CHUNKS
FIRST_TILE2 = DEPTH * TILES_PER_LAYER
FIRST_GEMM2 = DEPTH * N_TILES
SH1, SC1, G1, SH2, SC2, G2 = range(6)
GQA_SCALE = float(P) ** -0.5

PAR2 = {}
_n = 0
for _name, _w in (("cc", 16), ("ada_b", 96), ("norm_g", 32), ("pool_scale", 8), ("q_g", 1), ("k_g", 1),
                  ("final_g", 8), ("first_g", 8)):
    PAR2[_name] = _n
    _n += _w
NPAR2 = _n

CONST = {}
_n = 0
for _name, _w in (("ident", 128), ("ones", 256), ("mask_mla", 256), ("mask_fox", 256), ("cos", 256), ("sin", 256),
                  ("rot", 128), ("onehot", 8), ("sub", 2)):
    CONST[_name] = (_n, _w)
    _n += _w
NCONST = _n
CONST2 = {}
_n = 0
for _name, _w in (("cos", 256), ("sin", 256), ("rot", 128), ("inv_count", 4 * 256)):
    CONST2[_name] = (_n, _w)
    _n += _w
NCONST2 = _n


def shape_constants():
    c = np.zeros((P, NCONST), np.float32)

    def put(dst, table, name, value):
        at, w = table[name]
        dst[:, at:at + w] = value

    put(c, CONST, "ident", np.eye(P))
    put(c, CONST, "ones", 1.0)
    i = np.arange(P)
    for name, seen in (("mask_mla", i[:, None] // 64 >= i[None, :] // 64), ("mask_fox", i[:, None] >= i[None, :])):
        m = np.zeros((P, 256), np.float32)
        m[:, P:] = np.where(seen, 0.0, BIG)
        put(c, CONST, name, m)
    pos = np.arange(S, dtype=np.float32)
    inv = (np.float32(10000.0) ** (-np.arange(0, 32, 2, dtype=np.float32) / np.float32(32))).astype(np.float32)
    ang = pos[None, :] * inv[i % 16][:, None]
    put(c, CONST, "cos", np.cos(ang))
    put(c, CONST, "sin", np.sin(ang))

    def rotation(width):
        r = np.zeros((P, P), np.float32)
        for m in range(P):
            if m % (2 * width) < width:
                r[m + width, m] = -1.0
            else:
                r[m - width, m] = 1.0
        return r

    put(c, CONST, "rot", rotation(16))
    onehot = np.zeros((P, 8), np.float32)
    for base in (0, 32, 64, 96):
        onehot[base:base + 8] = np.eye(8)
    put(c, CONST, "onehot", onehot)
    put(c, CONST, "sub", np.stack([(i // 32) % 2 == 0, (i // 32) % 2 == 1], 1))
    d = np.zeros((P, NCONST2), np.float32)
    half = 64
    inv = (np.float32(10000.0) ** (-np.arange(0, half, 2, dtype=np.float32) / np.float32(half))).astype(np.float32)
    grid = np.where(i[:, None] < 64, (pos // 64)[None, :], (pos % 64)[None, :]).astype(np.float32)
    ang = grid * inv[i % 32][:, None]
    put(d, CONST2, "cos", np.cos(ang))
    put(d, CONST2, "sin", np.sin(ang))
    put(d, CONST2, "rot", rotation(32))
    t = np.arange(S)
    counts = [1.0 / (np.clip(t + w - w // 2, 0, S) - np.clip(t - w // 2, 0, S)) for w in (2, 4, 8, 16)]
    put(d, CONST2, "inv_count", np.concatenate(counts)[None, :])
    return c.astype(np.float32), d.astype(np.float32)


def tile_columns(w, k_tiles, col):
    return [w[k * P:(k + 1) * P, col:col + P] for k in range(k_tiles)]


def wide_columns(w, k_tiles, cols, width=2):
    return [w[k * P:(k + 1) * P, c + P * i:c + P * (i + 1)]
            for c in range(0, cols, width * P) for k in range(k_tiles) for i in range(width)]


def layer_atoms(a, lay):
    w_in = a["w_in"][lay]
    o_cq, o_ckv, o_fq = 1024, 1408, 1696
    o_fk, o_fv, o_fl, o_g = o_fq + 512, o_fq + 1024, o_fq + 1536, o_fq + 1544
    w_kr = np.tile(w_in[:, o_ckv + 256:o_fq], (1, 4))
    w_fl = np.zeros((D, P), np.float32)
    for base in (0, 32, 64, 96):
        w_fl[:, base:base + 8] = w_in[:, o_fl:o_g]
    wuq = a["mla_wuq"][lay].reshape(384, HEADS, 96)
    wukv = a["mla_wukv"][lay].reshape(256, HEADS, 128)
    w_qn = wuq[:, :, :64].reshape(384, 512)
    w_qr = wuq[:, [0, 2, 1, 3, 4, 6, 5, 7], 64:].reshape(384, 256)
    w_kn = wukv[:, :, :64].reshape(256, 512)
    w_vm = wukv[:, :, 64:].reshape(256, 512)

    def pair_diagonal(w, j):
        d = np.zeros((P, P), np.float32)
        d[:64, :64] = w[2 * j]
        d[64:, 64:] = w[2 * j + 1]
        return [d]

    out = []
    for t in TILES:
        if t in SHARED:
            continue
        kind, j = t[0], t[-1]
        if kind in ("u", "gl", "cq", "ckv", "fq", "fk"):
            base = {"u": 0, "gl": 512, "cq": o_cq, "ckv": o_ckv, "fq": o_fq, "fk": o_fk}[kind]
            out += tile_columns(w_in, KT, base + j * P)
        elif kind == "kr":
            out += tile_columns(w_kr, KT, 0)
        elif kind == "fl":
            out += tile_columns(w_fl, KT, 0)
        elif kind == "wa":
            out += pair_diagonal(a["lru_wa"][lay], j)
        elif kind == "wx":
            out += pair_diagonal(a["lru_wx"][lay], j)
        elif kind == "fv":
            out += wide_columns(w_in[:, o_fv:o_fv + 512], KT, 512)
        elif kind == "vm":
            out += wide_columns(w_vm, KV_LORA_T, 512)
        elif kind == "kn":
            out += tile_columns(w_kn, KV_LORA_T, j * P)
        elif kind == "qn":
            out += tile_columns(w_qn, Q_LORA_T, j * P)
        elif kind == "qr":
            out += tile_columns(w_qr, Q_LORA_T, j * P)
        elif kind == "g":
            out += tile_columns(w_in, KT, o_g + t[1] * D + j * P)
        elif kind == "y":
            out += tile_columns(a[("w_br_a", "w_br_b", "w_br_c")[t[1]]][lay], 4, j * P)
        elif kind == "wo":
            out += tile_columns(a["w_o"][lay], KT, j * P)
        elif kind == "hg":
            out += tile_columns(a["w_gate_up"][lay], KT, (t[1] * HALF_T + j) * P)
        elif kind == "hu":
            out += tile_columns(a["w_gate_up"][lay], KT, D_FF + (t[1] * HALF_T + j) * P)
        elif kind == "dn":
            out += tile_columns(a["w_down"][lay][t[1] * HALF_T * P:], HALF_T, j * P)
        elif kind == "pg":
            out += tile_columns(a["w_ple_gate"][lay], KT, j * P)
        elif kind == "pp":
            out += tile_columns(a["w_ple"][lay], PLE_T, j * P)
    assert len(out) == LAYER_ATOMS
    return out


def second_atoms(a):
    out = []
    for l in range(DEPTH):
        out += wide_columns(a["ada_w_2"][l], KT, 6 * D)
    for g in range(4):
        for j in range(2):
            out += tile_columns(a["pool_w_2"][0, g], 2, j * P)

    def mlp(l):
        o = []
        for q in range(QUARTERS):
            for j in range(QT):
                o += tile_columns(a["mlp_w1_2"][l], KT, (q * QT + j) * P)
            for n in range(KT):
                o += tile_columns(a["mlp_w2_2"][l][q * QT * P:], QT, n * P)
        return o

    out += mlp(0)
    qkv = a["attn_w_qkv_2"][0]
    for j in range(8):
        out += tile_columns(qkv, KT, j * P)
    for j in range(4):
        out += tile_columns(qkv, KT, 1024 + j * P)
    out += wide_columns(qkv[:, 1536:], KT, 512)
    for j in range(8):
        out += tile_columns(a["attn_w_o_2"][0], KT, j * P)
    out += mlp(1)
    assert len(out) == B2_ATOMS
    return out


def pack_stream(a):
    stream = np.zeros((N_CHUNKS, P, CHUNK_ATOMS, P), np.float32)
    first = 0
    for atoms, chunks in [(layer_atoms(a, l), LAYER_CHUNKS) for l in range(DEPTH)] + [(second_atoms(a), B2_CHUNKS)]:
        for n, atom in enumerate(atoms):
            stream[first + n // CHUNK_ATOMS, :, n % CHUNK_ATOMS] = atom
        first += chunks
    return stream.reshape(N_CHUNKS, P, CH)


def columns(v):
    return np.ascontiguousarray(np.asarray(v).reshape(-1, P).T)


def pack_parameters(a):
    par = np.zeros((P, DEPTH, NPAR), np.float32)
    for l in range(DEPTH):
        def put(name, v):
            c = columns(v)
            par[:, l, PAR[name]:PAR[name] + c.shape[1]] = c
        for name, src in (("mix_g", "mix_norm"), ("gate_b", "gate_b"), ("conv_w", "conv_w"), ("conv_b", "conv_b"),
                          ("ba", "lru_ba"), ("bx", "lru_bx"), ("lam", "lru_lambda"), ("q_g", "mla_q_norm"),
                          ("kv_g", "mla_kv_norm"), ("ffn_g", "ffn_norm"), ("ple_g", "ple_norm")):
            put(name, a[src][l])
        for base in (0, 32, 64, 96):
            par[base:base + 8, l, PAR["bf"]] = a["fox_bf"][l]
    par2 = np.zeros((P, NPAR2), np.float32)

    def put2(name, v, at=0):
        c = columns(v)
        par2[:, PAR2[name] + at:PAR2[name] + at + c.shape[1]] = c
    cc = np.stack([columns(a["c_ctx_2"]), columns(a["c_2"])], 2).reshape(P, 16)
    par2[:, PAR2["cc"]:PAR2["cc"] + 16] = cc
    put2("ada_b", a["ada_b_2"])
    put2("norm_g", a["norm_g_2"])
    put2("pool_scale", a["pool_scale_2"])
    put2("q_g", a["attn_q_g_2"])
    put2("k_g", a["attn_k_g_2"])
    put2("final_g", a["final_g_2"])
    put2("first_g", a["final_norm"])
    return par.reshape(P, DEPTH * NPAR), par2


def token_minor(x):
    t, f = x.shape
    return np.ascontiguousarray(x.T.reshape(f // P, P, t).transpose(1, 0, 2).reshape(P, (f // P) * t))


NORM_FIRST = {"mix": 0, "q": 8, "kv": 11, "ffn": 13, "ple": 21}
NORM_TILES = 29
NORM_NO = {"mix": 0, "q": 1, "kv": 2, "ffn": 3, "ple": 4}
N_NORMS = 5
UNITS = 32
PAIRS = 8
FREE_BANKS = N_BANKS
FREE_SLOTS = 3


def build(nc, ins, out):
    stream, x_in, ctx_in, p_in, par_in, par2_in, const_in, const2_in = ins
    ctx = ExitStack()
    with ctx:
        def sem(name):
            return ctx.enter_context(nc.semaphore(name))

        raw = [ctx.enter_context(nc.sbuf_tensor(f"raw{i}", [P, CH], F32)) for i in range(RING)]
        whi = [ctx.enter_context(nc.sbuf_tensor(f"whi{i}", [P, CH], F32R)) for i in range(RING)]
        wlo = [ctx.enter_context(nc.sbuf_tensor(f"wlo{i}", [P, CH], F32R)) for i in range(RING)]
        AR = ctx.enter_context(nc.sbuf_tensor("split_acts", [P, 16384], F32R))
        NAF = 21300
        AF = ctx.enter_context(nc.sbuf_tensor("acts", [P, NAF], F32))
        bank = [ctx.enter_context(nc.psum_tensor(f"bank{i}", [P, 512], F32)) for i in range(8)]
        o_bank, s_bank, t_bank = bank[4], [bank[5], bank[6]], bank[7]

        top = [NAF]
        low = [0]

        def keep(n):
            top[0] -= n
            return AF[:, top[0]:top[0] + n]

        def take(n):
            low[0] += n
            assert low[0] <= top[0], (low[0], top[0])
            return AF[:, low[0] - n:low[0]]

        const = keep(NCONST)
        par = keep(DEPTH * NPAR)
        par2 = keep(NPAR2)
        stat = keep(32)

        def C(name):
            at, w = CONST[name]
            return const[:, at:at + w]

        ident, ones = C("ident"), C("ones")
        eps_col = stat[:, 0:1]
        nmax = [stat[:, 2:3], stat[:, 3:4]]
        rsum = [stat[:, 4:5], stat[:, 5:6]]
        rinv = stat[:, 6:7]

        x = take(2048)
        rstd_x = take(256)
        rstd_q = take(256)
        rstd_kv = take(256)
        rcol = take(4)
        ugl = take(2060)
        u_pad = ugl[:, 0:1036]
        sq_lru = ugl[:, 0:1024]
        gl = ugl[:, 1036:2060]
        merged = ugl[:, 0:2048]
        lru = take(3584)
        xc, tr, ti, rec = lru[:, 0:1024], lru[:, 1024:2048], lru[:, 2048:3072], lru[:, 3072:3584]
        sqx = lru[:, 0:2048]
        krm = take(512)
        qn, kn, qr, vm = take(1024), take(1024), take(512), take(1024)
        fqk = take(2048)
        fq, fk = fqk[:, 0:1024], fqk[:, 1024:2048]
        c_raw, c_sq = fqk[:, 0:1280], fqk[:, 1280:2048]
        p_raw = fqk[:, 0:512]
        vf = take(1024)
        rk, lq, lh = take(256), take(256), take(512)
        att = take(2048 - 256)
        lg, pr, pt, o32 = att[:, 0:512], att[:, 512:1024], att[:, 1024:1536], att[:, 1536:1792]
        krz = lg[:, 0:256]
        th, hid, ut = att[:, 0:512], att[:, 512:1024], att[:, 1024:1280]
        gt = take(512)
        yt = take(256)
        cur = take(NPAR)
        hgb = take(24)
        m2sp = take(4)
        small = take(24)
        f_z, f_ab, f_den, f_s = (ti[:, i * 256:(i + 1) * 256] for i in range(4))
        f_s2, f_p = rec[:, 0:256], rec[:, 256:512]

        def Cp(name, j=0):
            return cur[:, PAR[name] + j:PAR[name] + j + 1]

        xa_hi, xa_lo = AR[:, 0:2048], AR[:, 2048:4096]
        xb_hi, xb_lo = AR[:, 4096:6144], AR[:, 6144:8192]
        lru_hi, lru_lo = AR[:, 8192:9216], AR[:, 9216:10240]
        cn_hi, cn_lo = AR[:, 10240:11520], AR[:, 11520:12800]
        mo_hi, mo_lo = AR[:, 10240:11264], AR[:, 11264:12288]
        xc_hi, xc_lo = AR[:, 12800:13824], AR[:, 13824:14848]
        fo_hi, fo_lo = AR[:, 12800:13824], AR[:, 13824:14848]
        h_hi, h_lo = AR[:, 8192:8192 + HALF_T * 256], AR[:, 8192 + HALF_T * 256:8192 + 2 * HALF_T * 256]
        p_hi, p_lo = AR[:, 13824:14336], AR[:, 14336:14848]
        branch_in = [(lru_hi, lru_lo), (mo_hi, mo_lo), (fo_hi, fo_lo)]

        def tile(a, t, n=256):
            return a[:, t * n:(t + 1) * n]

        low[0] = 2048
        h = take(4096)
        sq2 = take(4096)
        q2, k2 = sq2[:, 0:2048], sq2[:, 2048:4096]
        v2 = take(2048)
        pr2, pt2 = take(1024), take(1024)
        low[0] -= 2048
        rows = take(2048)
        low[0] -= 2048
        padded, sum_a, sum_b = take(1088), take(544), take(544)
        hsq = pr2
        tmp, squares, rstd2 = take(1024), take(1024), take(512)
        m32, var2 = squares[:, 0:512], squares[:, 512:1024]
        o32b = take(256)
        const2 = take(NCONST2)
        mod, gain, pool_gate, svec, turned = take(2 * 96), take(64), take(16), take(32), take(32)
        qg_scaled = take(1)
        m_hi, m_lo = AR[:, 0:4096], AR[:, 4096:8192]
        hid_hi, hid_lo = AR[:, 8192:12288], AR[:, 12288:16384]
        silu_c = AR[:, 8192:9216]
        oh_hi, oh_lo = AR[:, 8192:10240], AR[:, 12288:14336]

        def C2(name):
            at, w = CONST2[name]
            return const2[:, at:at + w]

        def mod_col(l, part, t, s):
            i = (l * MOD_T + part * KT + t) * 2 + s
            return mod[:, i:i + 1]

        def gain_col(l, i, t, s):
            c = ((l * 2 + i) * KT + t) * 2 + s
            return gain[:, c:c + 1]

        o_banks2 = (o_bank, bank[(FIRST_TILE2 + TILE_NO2[("o", 3)]) % N_BANKS])

        def sides(l, i):
            return (1,) if (l, i) == (1, 1) else (0, 1)

        def side(a, t, s):
            return a[:, t * 512 + s * 256:t * 512 + (s + 1) * 256]

        raw_in = [sem(f"raw_in{i}") for i in range(RING)]
        hi_ready = sem("hi_ready")
        lo_ready = sem("lo_ready")
        slots_used = sem("slots_used")
        gemm_done = sem("gemm_done")
        tiles_out = sem("tiles_out")
        start_in = sem("start_in")
        x_ready = sem("x_ready")
        par_ready = sem("par_ready")
        sq_ready = sem("sq_ready")
        nhi_ready = sem("nhi_ready")
        nlo_ready = sem("nlo_ready")
        sd_ready = sem("sd_ready")
        rstd_ready = sem("rstd_ready")
        lam_abs, lam_exp, m2sp_ready = sem("lam_abs"), sem("lam_exp"), sem("m2sp_ready")
        xc_begun, xc_done = sem("xc_begun"), sem("xc_done")
        gl_sq, gl_inner, gl_tanh = sem("gl_sq"), sem("gl_inner"), sem("gl_tanh")
        xchi_ready, xclo_ready = sem("xchi_ready"), sem("xclo_ready")
        lru_act = sem("lru_act")
        lru_done, lruhi_ready, lrulo_ready = sem("lru_done"), sem("lruhi_ready"), sem("lrulo_ready")
        mla_ready = sem("mla_ready")
        fl_abs, fl_exp, decay_ready, lh_ready = sem("fl_abs"), sem("fl_exp"), sem("decay_ready"), sem("lh_ready")
        s_done, lg_done, exp_done = sem("s_done"), sem("lg_done"), sem("exp_done")
        p_done, t_done, pt_done, pv_done = sem("p_done"), sem("t_done"), sem("pt_done"), sem("pv_done")
        o_out, ohi_ready, olo_ready = sem("o_out"), sem("ohi_ready"), sem("olo_ready")
        gate_tanh = sem("gate_tanh")
        merged_ready, mhi_ready, mlo_ready = sem("merged_ready"), sem("mhi_ready"), sem("mlo_ready")
        hid_ready, hhi_ready, hlo_ready = sem("hid_ready"), sem("hhi_ready"), sem("hlo_ready")
        ple_in, phi_ready, plo_ready = sem("ple_in"), sem("phi_ready"), sem("plo_ready")
        late_in = sem("late_in")
        h_ready = sem("h_ready")
        sq2_ready = sem("sq2_ready")
        sd2_ready = sem("sd2_ready")
        silu_act, silu_ready, rows_ready = sem("silu_act"), sem("silu_ready"), sem("rows_ready")
        scaled2, m_act, m_split = sem("scaled2"), sem("m_act"), sem("m_split")
        pooled, pooled_hi = sem("pooled"), sem("pooled_hi")
        act2_hi, act2_lo = sem("act2_hi"), sem("act2_lo")
        hsq_ready, hsd_ready, hn_ready = sem("hsq_ready"), sem("hsd_ready"), sem("hn_ready")
        qkv_ready = sem("qkv_ready")
        s2_done, max2_done, exp2_done, p2_done = sem("s2_done"), sem("max2_done"), sem("exp2_done"), sem("p2_done")
        t2_done, pt2_done, pv2_done = sem("t2_done"), sem("pt2_done"), sem("pv2_done")
        o2_out, o2_hi, o2_lo = sem("o2_out"), sem("o2_hi"), sem("o2_lo")
        result_ready = sem("result_ready")
        out_done = sem("out_done")
        N_GATES = 24 + FF_T + 8

        def gate_no(t):
            if t[0] == "g":
                return t[1] * 8 + t[2]
            return 24 + t[1] * HALF_T + t[2] if t[0] == "hg" else 24 + FF_T + t[1]

        block = ctx.enter_context(nc.Block())

        @block.sync
        def _(sp):
            def fetch(slot, index):
                sp.dma_start(raw[slot][:, :], stream[index]).then_inc(raw_in[slot], 16)

            sp.dma_start(par[:, :], par_in).then_inc(start_in, 16)
            sp.dma_start(x[:, :], x_in).then_inc(start_in, 16)
            sp.dma_start(const[:, :], const_in).then_inc(start_in, 16)
            for slot in range(RING):
                fetch(slot, slot)
            sp.dma_start(par2[:, :], par2_in).then_inc(start_in, 16)
            with sp.Fori(1, N_CHUNKS // RING) as r:
                for slot in range(RING):
                    sp.wait_ge(lo_ready, r * RING + (slot - RING + 1))
                    sp.dma_start(raw[slot][:, :], stream[bass.ds(r * RING + slot, 1)].rearrange("a p n -> (a p) n"))\
                        .then_inc(raw_in[slot], 16)
            for t in range(KT):
                sp.wait_ge(result_ready, t + 1)
                sp.dma_start(out[:, t * 256:(t + 1) * 256], tile(sq2, t)).then_inc(out_done, 16)
            sp.wait_ge(out_done, 16 * KT)

        @block.gpsimd
        def _(pool):
            with pool.Fori(0, N_CHUNKS // RING) as r:
                for slot in range(RING):
                    pool.wait_ge(hi_ready, r * RING + (slot + 1))
                    nc.gpsimd.tensor_tensor(wlo[slot][:, :], raw[slot][:, :], whi[slot][:, :].bitcast(F32),
                                            ALU.subtract).then_inc(lo_ready, 1)

        @block.tensor
        def _(pe):
            class Cursor:
                atom = 0

            def weights(lay, base, n):
                chunk, at = divmod(Cursor.atom, CHUNK_ATOMS)
                opens = at == 0
                assert at + n <= CHUNK_ATOMS
                if opens:
                    pe.wait_ge(lo_ready, base(lay, chunk) + 1)
                Cursor.atom += n
                cols = slice(at * P, (at + n) * P)
                return whi[chunk % RING][:, cols], wlo[chunk % RING][:, cols], opens

            def product(out_ap, hi_act, lo_act, k_tiles, lay, base, wait_k=None):
                for k in range(k_tiles):
                    w_hi, w_lo, opens = weights(lay, base, 1)
                    if wait_k is not None:
                        wait_k(k)
                    first = nc.tensor.matmul(out_ap, w_hi, hi_act(k), start=(k == 0), stop=False)
                    if opens:
                        first.then_inc(slots_used, 1)
                    nc.tensor.matmul(out_ap, w_hi, lo_act(k), start=False, stop=False)
                    last = nc.tensor.matmul(out_ap, w_lo, hi_act(k), start=False, stop=(k == k_tiles - 1))
                return last

            nc.tensor.sem_inc(slots_used, FREE_SLOTS)
            nc.tensor.sem_inc(pv_done, 2)
            pe.wait_ge(start_in, 64)

            with pe.Fori(0, DEPTH) as lay:
                Cursor.atom = 0

                def base(lay, chunk):
                    return lay * LAYER_CHUNKS + chunk

                def open_bank(t):
                    n = TILE_NO[t]
                    pe.wait_ge(tiles_out, lay * TILES_PER_LAYER + n + 1)
                    return bank[n % N_BANKS]

                def out_of_bank(t, extra=0):
                    pe.wait_ge(tiles_out, lay * TILES_PER_LAYER + (FREE_BANKS + TILE_NO[t] + 1))

                def normed(name, hi, lo, n):
                    first = NORM_FIRST[name]
                    return (lambda k: tile(hi, k), lambda k: tile(lo, k),
                            lambda k: pe.wait_ge(nlo_ready, lay * NORM_TILES + (first + k + 1)))

                act_of = {
                    "u": (xa_hi, xa_lo, 8), "gl": (xa_hi, xa_lo, 8), "cq": (xa_hi, xa_lo, 8),
                    "ckv": (xa_hi, xa_lo, 8), "kr": (xa_hi, xa_lo, 8), "fl": (xa_hi, xa_lo, 8),
                    "fq": (xa_hi, xa_lo, 8), "fk": (xa_hi, xa_lo, 8), "g": (xa_hi, xa_lo, 8),
                    "qn": (cn_hi, cn_lo, 3), "qr": (cn_hi, cn_lo, 3),
                    "kn": (cn_hi[:, 768:], cn_lo[:, 768:], 2),
                    "wo": (xb_hi, xb_lo, 8), "hg": (xa_hi, xa_lo, 8), "hu": (xa_hi, xa_lo, 8),
                    "dn": (h_hi, h_lo, HALF_T), "pg": (xb_hi, xb_lo, 8), "pp": (p_hi, p_lo, 2),
                }

                def gemm(t):
                    kind, j = t[0], t[-1]
                    if t in SHARED:
                        return
                    b = open_bank(t)
                    if kind == "ss":
                        n = {"mix": 8, "q": 3, "kv": 2, "ffn": 8, "ple": 8}[j]
                        for k in range(n):
                            pe.wait_ge(sq_ready, lay * NORM_TILES + (NORM_FIRST[j] + k + 1))
                            src = tile(sqx, k) if j in ("mix", "ffn", "ple") else tile(c_sq, k)
                            last = nc.tensor.matmul(b[:, 0:256], ones[:, 0:128], src, start=(k == 0), stop=(k == n - 1))
                    elif kind == "col":
                        pe.wait_ge(rstd_ready, lay * N_NORMS + (NORM_NO[j] + 1))
                        row = rstd_x if j == "mix" else rstd_kv
                        for m in range(2):
                            last = nc.tensor.matmul(b[:, m:m + 1], row[0:1, m * P:(m + 1) * P], ones[0:1, 0:1],
                                                    start=True, stop=True)
                    elif kind in ("wa", "wx"):
                        pe.wait_ge(xclo_ready, lay * 1 + 1)
                        last = product(b[:, 0:256], lambda k: tile(xc_hi, j), lambda k: tile(xc_lo, j), 1, lay, base)
                    elif kind in ("rotk", "rotq"):
                        out_of_bank(("kr", 0) if kind == "rotk" else ("qr", j))
                        src = krz if kind == "rotk" else tile(qr, j)
                        last = nc.tensor.matmul(b[:, 0:256], C("rot"), src, start=True, stop=True)
                    elif kind in ("fv", "vm"):
                        b2 = open_bank((kind, 1))
                        hi, lo, kts = (xa_hi, xa_lo, 8) if kind == "fv" else (cn_hi[:, 768:], cn_lo[:, 768:], 2)
                        for half in range(2):
                            for k in range(kts):
                                w_hi, w_lo, opens = weights(lay, base, 2)
                                for m, bm in enumerate((b, b2)):
                                    o = bm[:, half * 256:half * 256 + 256]
                                    tok_hi = hi[:, k * 256 + m * P:k * 256 + (m + 1) * P]
                                    tok_lo = lo[:, k * 256 + m * P:k * 256 + (m + 1) * P]
                                    one = nc.tensor.matmul(o, tok_hi, w_hi, start=(k == 0), stop=False)
                                    if opens and m == 0:
                                        one.then_inc(slots_used, 1)
                                    nc.tensor.matmul(o, tok_hi, w_lo, start=False, stop=False)
                                    last = nc.tensor.matmul(o, tok_lo, w_hi, start=False, stop=(k == kts - 1))
                        last.then_inc(gemm_done, 2)
                        return
                    else:
                        if kind == "y":
                            hi, lo = branch_in[t[1]]
                            n = 4
                            if j == 0:
                                if t[1] == 0:
                                    pe.wait_ge(lrulo_ready, lay * 4 + 4)
                                else:
                                    pe.wait_ge(olo_ready, lay * PAIRS + 4 * t[1])
                        else:
                            hi, lo, n = act_of[kind]
                        wait_k = None
                        if t == ("u", 0):
                            wait_k = normed("mix", hi, lo, n)[2]
                        elif t == ("kn", 0):
                            pe.wait_ge(nlo_ready, lay * NORM_TILES + NORM_FIRST["ffn"])
                        elif t == ("wo", 0):
                            wait_k = lambda k: pe.wait_ge(mlo_ready, lay * 8 + (k + 1))
                        elif t == ("hg", 0, 0):
                            wait_k = normed("ffn", hi, lo, n)[2]
                        elif kind == "dn" and j == 0:
                            wait_k = lambda k: pe.wait_ge(hlo_ready, lay * FF_T + (t[1] * HALF_T + k + 1))
                        elif t == ("pg", 0):
                            wait_k = normed("ple", hi, lo, n)[2]
                        elif t == ("pp", 0):
                            pe.wait_ge(plo_ready, lay + 1)
                        last = product(b[:, 0:256], lambda k: tile(hi, k), lambda k: tile(lo, k), n, lay, base, wait_k)
                    last.then_inc(gemm_done, 1)

                def scores(kind, u):
                    U = (0 if kind == "mla" else 16) + u
                    h, qb = u // 2, u % 2
                    r, nk = 64 * (h % 2), P * (qb + 1)
                    rows, q_cols = slice(r, r + 64), slice(qb * P, (qb + 1) * P)
                    pe.wait_ge(lg_done, lay * UNITS + U + 1)
                    o = s_bank[u % 2][:, 0:nk]
                    if kind == "mla":
                        if u == 0:
                            pe.wait_ge(mla_ready, lay + 1)
                        nc.tensor.matmul(o, tile(qn, h // 2)[rows, q_cols], tile(kn, h // 2)[rows, 0:nk],
                                         start=True, stop=False)
                        last = nc.tensor.matmul(o, tile(qr, h // 4)[rows, q_cols],
                                                tile(krm, (h // 2) % 2)[rows, 0:nk], start=False, stop=True)
                    else:
                        if u == 0:
                            out_of_bank(("fk", 3))
                            pe.wait_ge(decay_ready, lay + 1)
                        if qb == 0:
                            pe.wait_ge(lh_ready, lay * HEADS + h + 1)
                        nc.tensor.matmul(o, tile(fq, h // 2)[rows, q_cols], tile(fk, h // 2)[rows, 0:nk],
                                         start=True, stop=False)
                        last = nc.tensor.matmul(o, tile(lh, h % 2)[rows, q_cols], rk[rows, 0:nk],
                                                start=False, stop=True)
                    last.then_inc(s_done, 1)

                def turn(kind, u):
                    U = (0 if kind == "mla" else 16) + u
                    pe.wait_ge(p_done, lay * UNITS + U + 1)
                    pe.wait_ge(pt_done, lay * UNITS + U + 1)
                    for kb in range(u % 2 + 1):
                        last = nc.tensor.transpose(t_bank[:, kb * P:(kb + 1) * P],
                                                   tile(pr, u % 2)[:, kb * P:(kb + 1) * P], ident)
                    last.then_inc(t_done, 1)

                def values(kind, u):
                    U = (0 if kind == "mla" else 16) + u
                    h, qb = u // 2, u % 2
                    pair = U // 4
                    if u % 4 == 0:
                        pe.wait_ge(o_out, lay * PAIRS + pair + 1)
                    pe.wait_ge(pt_done, lay * UNITS + U + 2)
                    v = vm if kind == "mla" else vf
                    r = 64 * (h % 2)
                    cols = (pair % 2) * 256 + qb * P
                    for kb in range(qb + 1):
                        last = nc.tensor.matmul(o_bank[r:r + 64, cols:cols + P],
                                                v[:, kb * 512 + h * 64:kb * 512 + (h + 1) * 64],
                                                tile(pt, u % 2)[:, kb * P:(kb + 1) * P],
                                                start=(kb == 0), stop=(kb == qb))
                    last.then_inc(pv_done, 1)

                for t in HEAD_TILES:
                    gemm(t)
                for kind, fill in (("mla", MLA_FILL), ("fox", FOX_FILL)):
                    for i in range(17):
                        if i:
                            turn(kind, i - 1)
                        if i < 16:
                            scores(kind, i)
                            gemm(fill[i])
                        if i:
                            values(kind, i - 1)
                for t in MID_TILES + TAIL_TILES:
                    gemm(t)
                Cursor.atom = -(-LAYER_ATOMS // CHUNK_ATOMS) * CHUNK_ATOMS
                while Cursor.atom < LAYER_CHUNKS * CHUNK_ATOMS:
                    w_hi, w_lo, _ = weights(lay, base, CHUNK_ATOMS)
                    nc.tensor.matmul(t_bank[:, 0:256], w_hi[:, 0:P], tile(xb_hi, 0), start=True, stop=True)\
                        .then_inc(slots_used, 1)

            Cursor.atom = 0

            def base2(lay, chunk):
                return FIRST_CHUNK2 + chunk

            def open2(t):
                n = FIRST_TILE2 + TILE_NO2[t]
                pe.wait_ge(tiles_out, n + 1)
                return bank[n % N_BANKS]

            norm_tiles = 0
            splits_before = {("pool",): 0}
            act_tiles = 0

            def gemm2(t):
                nonlocal norm_tiles, act_tiles
                kind = t[0]
                if kind == "v" and t[1]:
                    return
                b = open2(t)
                if kind == "ss":
                    wide = t[1:] in ((0, 0), (0, 1), (1, 0))
                    o = b[:, 0:512] if wide else b[:, 0:256]
                    for k in range(KT):
                        pe.wait_ge(sq2_ready, norm_tiles + k + 1)
                        src = sq2[:, k * 512:(k + 1) * 512] if wide else sq2[:, k * 512 + 256:(k + 1) * 512]
                        last = nc.tensor.matmul(o, ones[:, 0:128], src, start=(k == 0), stop=(k == KT - 1))
                    norm_tiles += KT
                elif kind == "ada":
                    if t[1:] == (0, 0):
                        pe.wait_ge(silu_ready, 1)
                    for k in range(KT):
                        w_hi, w_lo, opens = weights(0, base2, 2)
                        s4 = silu_c[:, k * P:(k + 1) * P]
                        one = nc.tensor.matmul(b[:, 0:256], s4, w_hi, start=(k == 0), stop=False)
                        if opens:
                            one.then_inc(slots_used, 1)
                        last = nc.tensor.matmul(b[:, 0:256], s4, w_lo, start=False, stop=(k == KT - 1))
                elif kind == "turn":
                    g = t[1] * ADA_GROUPS + t[2]
                    pe.wait_ge(tiles_out, FIRST_TILE2 + FREE_BANKS + TILE_NO2[("ada", t[1], 4 * t[2] + 3)] + 1)
                    for i in range(8):
                        last = nc.tensor.transpose(b[:, 4 * i:4 * i + 4],
                                                   rows[0:4, (g % 2) * 1024 + i * P:(g % 2) * 1024 + (i + 1) * P],
                                                   ident[0:4, 0:4])
                elif kind == "pool":
                    if t[1] % 2 == 0:
                        pe.wait_ge(m_split, t[1] + 2)
                    g = t[1] // 2
                    last = product(b[:, 0:512], lambda k: tile(m_hi, 2 * g + k, 512),
                                   lambda k: tile(m_lo, 2 * g + k, 512), 2, 0, base2)
                elif kind in ("w1", "w2"):
                    l = t[1]
                    first_split = {0: 8, 1: 24}[l]

                    def part(a):
                        return (lambda k: tile(a, k, 512)) if l == 0 else (lambda k: side(a, k, 1))

                    o = b[:, 0:512] if l == 0 else b[:, 0:256]
                    if kind == "w1":
                        wait_k = (lambda k: pe.wait_ge(m_split, first_split + k + 1)) if t[2:] == (0, 0) else None
                        last = product(o, part(m_hi), part(m_lo), KT, 0, base2, wait_k)
                    else:
                        done = (l * QUARTERS + t[2]) * QT
                        wait_k = (lambda k: pe.wait_ge(act2_lo, done + k + 1)) if t[3] == 0 else None
                        last = product(o, part(hid_hi), part(hid_lo), QT, 0, base2, wait_k)
                elif kind == "q":
                    wait_k = (lambda k: pe.wait_ge(m_split, 16 + k + 1)) if t[1] == 0 else None
                    last = product(b[:, 0:256], lambda k: side(m_hi, k, 1), lambda k: side(m_lo, k, 1), KT, 0, base2,
                                   wait_k)
                elif kind == "k":
                    last = product(b[:, 0:512], lambda k: tile(m_hi, k, 512), lambda k: tile(m_lo, k, 512), KT, 0,
                                   base2)
                elif kind in ("qss", "kss"):
                    n = t[1] + (8 if kind == "kss" else 0)
                    w = 256 if kind == "qss" else 512
                    pe.wait_ge(hsq_ready, n + 1)
                    last = nc.tensor.matmul(b[:, 0:w], ones[:, 0:128], tile(hsq, n % 2, 512)[:, 0:w], start=True,
                                            stop=True)
                elif kind in ("qrot", "krot"):
                    n = t[1] + (8 if kind == "krot" else 0)
                    pe.wait_ge(hn_ready, n + 1)
                    src = tile(q2, t[1]) if kind == "qrot" else side(k2, t[1], 1)
                    last = nc.tensor.matmul(b[:, 0:256], C2("rot"), src, start=True, stop=True)
                elif kind == "v":
                    banks = [b] + [open2(("v", m)) for m in range(1, 4)]
                    for half in range(2):
                        for k in range(KT):
                            w_hi, w_lo, opens = weights(0, base2, 2)
                            for m in range(4):
                                o = banks[m][:, half * 256:half * 256 + 256]
                                tok_hi = m_hi[:, k * 512 + m * P:k * 512 + (m + 1) * P]
                                tok_lo = m_lo[:, k * 512 + m * P:k * 512 + (m + 1) * P]
                                one = nc.tensor.matmul(o, tok_hi, w_hi, start=(k == 0), stop=False)
                                if opens and m == 0:
                                    one.then_inc(slots_used, 1)
                                nc.tensor.matmul(o, tok_hi, w_lo, start=False, stop=False)
                                last = nc.tensor.matmul(o, tok_lo, w_hi, start=False, stop=(k == KT - 1))
                    last.then_inc(gemm_done, 4)
                    return
                elif kind == "o":
                    wait_k = (lambda k: pe.wait_ge(o2_lo, k + 1)) if t[1] == 0 else None
                    last = product(b[:, 0:256], lambda k: tile(oh_hi, k), lambda k: tile(oh_lo, k), KT, 0, base2,
                                   wait_k)
                last.then_inc(gemm_done, 1)

            def scores2(u):
                h_, qb = u // 2, u % 2
                if u == 0:
                    pe.wait_ge(qkv_ready, 1)
                if u >= 2:
                    pe.wait_ge(exp2_done, u - 1)
                nc.tensor.matmul(s_bank[u % 2][:, :], tile(q2, h_)[:, qb * P:(qb + 1) * P],
                                 tile(k2, h_ // 2, 512), start=True, stop=True).then_inc(s2_done, 1)

            def turn2(u):
                pe.wait_ge(p2_done, u + 1)
                if u >= 1:
                    pe.wait_ge(pt2_done, u)
                for kb in range(4):
                    last = nc.tensor.transpose(t_bank[:, kb * P:(kb + 1) * P],
                                               tile(pr2, u % 2, 512)[:, kb * P:(kb + 1) * P], ident)
                last.then_inc(t2_done, 1)

            def values2(u):
                h_, qb = u // 2, u % 2
                if qb == 0 and h_ >= 2:
                    pe.wait_ge(o2_out, h_ - 1)
                pe.wait_ge(pt2_done, u + 1)
                o = o_banks2[h_ % 2][:, qb * P:(qb + 1) * P]
                for kb in range(4):
                    kv = h_ // 2
                    last = nc.tensor.matmul(o, v2[:, kb * 512 + kv * P:kb * 512 + (kv + 1) * P],
                                            tile(pt2, u % 2, 512)[:, kb * P:(kb + 1) * P], start=(kb == 0),
                                            stop=(kb == 3))
                last.then_inc(pv2_done, 1)

            for t in TILES2:
                if t == ("o", 0):
                    for i in range(18):
                        if i < 16:
                            scores2(i)
                        if 1 <= i < 17:
                            turn2(i - 1)
                        if i >= 2:
                            values2(i - 2)
                gemm2(t)

        @block.scalar
        def _(act):
            sc = nc.scalar

            class Split:
                chunk = 0

            def split(lay, base, chunk):
                g = base(lay, chunk)
                act.wait_ge(slots_used, g + 1)
                act.wait_ge(raw_in[chunk % RING], (base(lay, chunk - chunk % RING) // RING) * 16 + 16
                            if isinstance(g, int) else lay * (LAYER_CHUNKS // RING * 16) + (chunk // RING + 1) * 16)
                sc.activation(whi[chunk % RING][:, :], raw[chunk % RING][:, :], ACT.Copy).then_inc(hi_ready, 1)

            def ahead(lay, base, chunk):
                while Split.chunk <= chunk + AHEAD:
                    split(lay, base, Split.chunk)
                    Split.chunk += 1

            act.wait_ge(start_in, 64)
            sc.copy(stat[:, 8:9], ones[:, 0:1]).then_inc(pt_done, 1)
            for chunk in range(AHEAD):
                split(0, lambda lay, c: c, chunk)

            with act.Fori(0, DEPTH) as lay:
                Split.chunk = AHEAD

                def base(lay, chunk):
                    return lay * LAYER_CHUNKS + chunk

                def moved_out(t):
                    ahead(lay, base, last_chunk(ATOM_SPAN[t]))
                    act.wait_ge(tiles_out, lay * TILES_PER_LAYER + (FREE_BANKS + TILE_NO[t] + 1))

                def norm(name, src, sq, g, hi, ready):
                    first = NORM_FIRST[name]
                    for k in range({"mix": 8, "q": 3, "kv": 2, "ffn": 8, "ple": 8}[name]):
                        ready(k)
                        sc.activation(sq(k), src(k), ACT.Square).then_inc(sq_ready, 1)
                        sc.activation(hi(k), src(k), ACT.Copy, scale=Cp(g, k)).then_inc(nhi_ready, 1)

                def root(name):
                    moved_out(("ss", name))
                    sc.activation(yt, yt, ACT.Sqrt).then_inc(sd_ready, 1)

                def exp(kind, u):
                    U = (0 if kind == "mla" else 16) + u
                    act.wait_ge(lg_done, lay * UNITS + U + 3)
                    nk = P * (u % 2 + 1)
                    sc.activation(tile(pr, u % 2)[:, 0:nk], tile(lg, u % 2)[:, 0:nk], ACT.Exp, scale=-1.0,
                                  bias=nmax[u % 2], accum_out=rsum[u % 2]).then_inc(exp_done, 1)

                def move_turned(kind, u):
                    U = (0 if kind == "mla" else 16) + u
                    act.wait_ge(t_done, lay * UNITS + U + 1)
                    act.wait_ge(pv_done, lay * UNITS + U + 1)
                    nk = P * (u % 2 + 1)
                    sc.activation(tile(pt, u % 2)[:, 0:nk], t_bank[:, 0:nk], ACT.Copy).then_inc(pt_done, 1)

                def attended(kind, pair):
                    act.wait_ge(o_out, lay * PAIRS + pair + 3)
                    hi = mo_hi if kind == "mla" else fo_hi
                    sc.activation(tile(hi, pair % 4), o32, ACT.Copy).then_inc(ohi_ready, 1)

                def decay_mask(h):
                    sc.activation(tile(lh, h % 2), lq, ACT.Copy, scale=C("onehot")[:, h:h + 1]).then_inc(lh_ready, 1)

                def of_tile(t):
                    kind, j = t[0], t[-1]
                    if kind == "g":
                        moved_out(t)
                        g = tile(gt, j % 2)
                        sc.activation(g, g, ACT.Tanh, scale=0.5, bias=hgb[:, t[1] * 8 + j:t[1] * 8 + j + 1])\
                            .then_inc(gate_tanh, 1)
                    elif kind == "hg":
                        moved_out(t)
                        sc.activation(tile(th, j % 2), tile(gt, j % 2), ACT.Tanh, scale=0.5).then_inc(gate_tanh, 1)
                    elif kind == "hu":
                        act.wait_ge(hid_ready, lay * FF_T + (t[1] * HALF_T + j + 1))
                        sc.activation(tile(h_hi, j), tile(hid, j % 2), ACT.Copy).then_inc(hhi_ready, 1)
                    elif kind == "y" and t[1] == 2:
                        act.wait_ge(merged_ready, lay * 8 + j + 1)
                        sc.activation(tile(xb_hi, j), tile(merged, j), ACT.Copy, scale=0.5).then_inc(mhi_ready, 1)
                    elif kind == "pg":
                        moved_out(t)
                        sc.activation(tile(gt, j % 2), tile(gt, j % 2), ACT.Tanh, scale=0.5).then_inc(gate_tanh, 1)

                def keep_ahead(t):
                    ahead(lay, base, last_chunk(ATOM_SPAN[t]))

                act.wait_ge(par_ready, lay + 1)
                norm("mix", lambda k: tile(x, k), lambda k: tile(sqx, k), "mix_g", lambda k: tile(xa_hi, k),
                     lambda k: act.wait_ge(x_ready, lay * 8 + k + 1))
                act.wait_ge(lam_abs, lay + 1)
                sc.activation(small[:, 4:8], small[:, 0:4], ACT.Exp, scale=-1.0).then_inc(lam_exp, 1)
                root("mix")
                for j in range(4):
                    keep_ahead(("u", j))
                    moved_out(("u", j))
                    sc.activation(tile(xc, j), u_pad[:, j * 259:j * 259 + 256], ACT.Identity,
                                  scale=Cp("conv_w", j), bias=Cp("conv_b", j)).then_inc(xc_begun, 1)
                for j in range(4):
                    keep_ahead(("gl", j))
                    moved_out(("gl", j))
                    sc.activation(tile(tr, j), tile(gl, j), ACT.Square).then_inc(gl_sq, 1)
                act.wait_ge(xc_done, lay + 1)
                sc.activation(xc_hi, xc, ACT.Copy).then_inc(xchi_ready, 1)
                act.wait_ge(gl_inner, lay + 1)
                sc.activation(tr, tr, ACT.Tanh, scale=GELU_C).then_inc(gl_tanh, 1)
                for j in range(3):
                    keep_ahead(("cq", j))
                    moved_out(("cq", j))
                    sc.activation(tile(c_sq, j), tile(c_raw, j), ACT.Square).then_inc(sq_ready, 1)
                    sc.activation(tile(cn_hi, j), tile(c_raw, j), ACT.Copy, scale=Cp("q_g", j)).then_inc(nhi_ready, 1)
                for j in range(2):
                    keep_ahead(("ckv", j))
                    moved_out(("ckv", j))
                    if j == 0:
                        act.wait_ge(gemm_done, lay * N_TILES + TILE_NO[("ss", "q")] + 1)
                    sc.activation(tile(c_sq, j), tile(c_raw, 3 + j), ACT.Square).then_inc(sq_ready, 1)
                    sc.activation(tile(cn_hi, 3 + j), tile(c_raw, 3 + j), ACT.Copy, scale=Cp("kv_g", j))\
                        .then_inc(nhi_ready, 1)
                keep_ahead(("kr", 0))
                root("q")
                root("kv")
                keep_ahead(("wx", 3))
                moved_out(("wx", 3))
                act.wait_ge(m2sp_ready, lay + 1)
                sc.activation(tr, tr, ACT.Tanh).then_inc(lru_act, 1)
                sc.activation(ti, ti, ACT.Tanh).then_inc(lru_act, 1)
                sc.drain()
                for j in range(4):
                    sc.activation(tile(tr, j), tile(tr, j), ACT.Tanh, scale=m2sp[:, j:j + 1], bias=m2sp[:, j:j + 1])\
                        .then_inc(lru_act, 1)
                sc.drain()
                sc.activation(sq_lru, tr, ACT.Sqrt, scale=-1.0).then_inc(lru_act, 1)
                done = 0
                for t in HEAD_TILES[TILE_NO[("rotk", 0)]:]:
                    keep_ahead(t)
                    if t in (("kn", 0), ("qn", 0), ("qn", 3), ("rotq", 1)):
                        act.wait_ge(lru_done, lay * 4 + done + 1)
                        sc.activation(tile(lru_hi, done), tile(xc, done), ACT.Copy).then_inc(lruhi_ready, 1)
                        done += 1
                for kind, fill in (("mla", MLA_FILL), ("fox", FOX_FILL)):
                    if kind == "fox":
                        decay_mask(0)
                    for i in range(17):
                        if i:
                            move_turned(kind, i - 1)
                        if i < 16:
                            exp(kind, i)
                            if kind == "fox" and i % 2 == 0 and i // 2 + 1 < HEADS:
                                decay_mask(i // 2 + 1)
                            if kind == "mla" and i == 1:
                                act.wait_ge(fl_abs, lay + 1)
                                sc.activation(f_den, f_ab, ACT.Exp, scale=-1.0).then_inc(fl_exp, 1)
                            keep_ahead(fill[i])
                            of_tile(fill[i])
                        if i and i % 4 == 0:
                            attended(kind, (i - 1) // 4 + (0 if kind == "mla" else 4))
                act.wait_ge(pv_done, lay * UNITS + UNITS + 2)
                act.dma_start(p_raw, p_in[bass.ds(lay, 1)].rearrange("a p n -> (a p) n")).then_inc(ple_in, 16)
                for t in MID_TILES:
                    keep_ahead(t)
                    of_tile(t)
                for n in range(8):
                    keep_ahead(("wo", n))
                norm("ffn", lambda k: tile(x, k), lambda k: tile(sqx, k), "ffn_g", lambda k: tile(xa_hi, k),
                     lambda k: moved_out(("wo", k)))
                root("ffn")
                for t in TAIL_TILES[9:9 + 60]:
                    if t == ("hg", 1, 0):
                        act.wait_ge(ple_in, lay * 16 + 16)
                        sc.activation(p_hi, p_raw, ACT.Copy).then_inc(phi_ready, 1)
                    keep_ahead(t)
                    of_tile(t)
                norm("ple", lambda k: tile(x, k), lambda k: tile(sqx, k), "ple_g", lambda k: tile(xb_hi, k),
                     lambda k: moved_out(("dn", 1, k)))
                root("ple")
                for t in TAIL_TILES[-16:]:
                    keep_ahead(t)
                    of_tile(t)
                ahead(lay, base, LAYER_CHUNKS - 1)

            Split.chunk = AHEAD

            def base2(lay, chunk):
                return FIRST_CHUNK2 + chunk

            def ahead2(t):
                ahead(0, base2, min((ATOM_SPAN2[t][1] - 1) // CHUNK_ATOMS, -(-B2_ATOMS // CHUNK_ATOMS) - 1 - AHEAD))

            def moved_out2(t):
                ahead2(t)
                act.wait_ge(tiles_out, FIRST_TILE2 + FREE_BANKS + TILE_NO2[t] + 1)

            def root2(t):
                moved_out2(t)
                wide = t[1:] in ((0, 0), (0, 1), (1, 0))
                a = var2[:, 0:512] if wide else var2[:, 256:512]
                sc.activation(a, a, ACT.Sqrt).then_inc(sd2_ready, 1)

            def squares2(both, ready):
                for k in range(KT):
                    ready(k)
                    c = slice(k * 512, (k + 1) * 512) if both else slice(k * 512 + 256, (k + 1) * 512)
                    sc.activation(sq2[:, c], h[:, c], ACT.Square).then_inc(sq2_ready, 1)

            scaled_before = 0

            def modulate_tile(l, i, t, dst):
                act.wait_ge(scaled2, scaled_before + t + 1)
                for s in sides(l, i):
                    last = sc.activation(dst(t, s), side(tmp, t % 2, s), ACT.Identity, scale=gain_col(l, i, t, s),
                                         bias=mod_col(l, SH1 if i == 0 else SH2, t, s))
                last.then_inc(m_act, 1)

            def modulated(l, i):
                nonlocal scaled_before
                for t in range(KT):
                    modulate_tile(l, i, t, lambda t, s: side(m_hi, t, s))
                scaled_before += KT

            def hidden2(l):
                n = l * MLP_T
                for q in range(QUARTERS):
                    for j in range(QT):
                        moved_out2(("w1", l, q, j))
                        if l == 0:
                            sc.activation(tile(hid_hi, j, 512), tile(tmp, j % 2, 512), ACT.Square).then_inc(act2_hi, 1)
                        else:
                            sc.activation(side(hid_hi, j, 1), side(tmp, j % 2, 1), ACT.Square).then_inc(act2_hi, 1)
                    for n_ in range(KT):
                        ahead2(("w2", l, q, n_))

            act.wait_ge(x_ready, 8 + 8 * DEPTH)
            act.dma_start(h.rearrange("p (t n) -> p t n", n=512)[:, :, 0:256],
                          ctx_in.rearrange("p (t n) -> p t n", n=256)).then_inc(late_in, 16)
            act.dma_start(const2, const2_in).then_inc(late_in, 16)
            for k in range(KT):
                sc.activation(side(sq2, k, 1), tile(x, k), ACT.Square).then_inc(sq2_ready, 1)
            sc.activation(svec[:, 0:16], par2[:, PAR2["cc"]:PAR2["cc"] + 16], ACT.Tanh, scale=0.5)\
                .then_inc(silu_act, 1)
            root2(("ss", "first"))
            act.wait_ge(silu_act, 2)
            s4 = silu_c.rearrange("p (k n) -> p k n", n=P)
            sc.activation(s4[:, :, 0:2], svec[:, 16:32].rearrange("p (k s) -> p k s", s=2), ACT.Copy)\
                .then_inc(silu_act, 1)
            for t in ada_tiles():
                ahead2(t)
            act.wait_ge(late_in, 32)
            squares2(True, lambda k: act.wait_ge(h_ready, k + 1))
            root2(("ss", 0, 0))
            pad3 = padded.rearrange("p (b s n) -> p b s n", b=2, s=2)
            modulate_tile(0, 0, 0, lambda t, s: pad3[:, t % 2, s, 8:264])
            for t in range(KT):
                if t + 1 < KT:
                    modulate_tile(0, 0, t + 1, lambda t, s: pad3[:, t % 2, s, 8:264])
                act.wait_ge(pooled, t + 1)
                sc.activation(tile(m_hi, t, 512), tile(tmp, t % 2, 512), ACT.Copy).then_inc(pooled_hi, 1)
            scaled_before += KT
            squares2(True, lambda k: moved_out2(("pool", k)))
            root2(("ss", 0, 1))
            modulated(0, 1)
            hidden2(0)
            squares2(True, lambda k: moved_out2(("w2", 0, QUARTERS - 1, k)))
            root2(("ss", 1, 0))
            modulated(1, 0)
            for name, n, w, first in (("q", 8, 256, 0), ("k", KV_HEADS, 512, 8)):
                for t in staggered(name, n):
                    ahead2(t)
                    j = t[1]
                    if t[0] == name:
                        moved_out2(t)
                        src = tile(q2, j) if name == "q" else tile(k2, j, 512)
                        if first + j >= 2:
                            m = first + j - 2
                            old = ("qss", m) if m < 8 else ("kss", m - 8)
                            act.wait_ge(gemm_done, FIRST_GEMM2 + TILE_NO2[old] + 1)
                        sc.activation(tile(hsq, (first + j) % 2, 512)[:, 0:w], src, ACT.Square).then_inc(hsq_ready, 1)
                    elif t[0] == name + "ss":
                        moved_out2(t)
                        sc.activation(var2[:, 0:w], var2[:, 0:w], ACT.Sqrt).then_inc(hsd_ready, 1)
            ahead2(("v", 3))

            def exp2(u):
                act.wait_ge(max2_done, u + 1)
                sc.activation(tile(pr2, u % 2, 512), s_bank[u % 2][:, :], ACT.Exp, scale=-1.0, bias=nmax[u % 2],
                              accum_out=rsum[u % 2]).then_inc(exp2_done, 1)

            def move2(u):
                act.wait_ge(t2_done, u + 1)
                if u >= 2:
                    act.wait_ge(pv2_done, u - 1)
                sc.activation(tile(pt2, u % 2, 512), t_bank[:, :], ACT.Copy).then_inc(pt2_done, 1)

            for i in range(18):
                if i < 16:
                    exp2(i)
                if 1 <= i < 17:
                    move2(i - 1)
                if i >= 3 and i % 2 == 1:
                    hd = (i - 3) // 2
                    act.wait_ge(o2_out, hd + 1)
                    sc.activation(tile(oh_hi, hd), o32b, ACT.Copy).then_inc(o2_hi, 1)
            squares2(False, lambda k: moved_out2(("o", k)))
            root2(("ss", 1, 1))
            modulated(1, 1)
            hidden2(1)
            squares2(False, lambda k: moved_out2(("w2", 1, QUARTERS - 1, k)))
            root2(("ss", "last"))

        @block.vector
        def _(dve):
            v = nc.vector

            def low_part(lo, value, hi, scale=None):
                if scale is None:
                    return v.tensor_tensor(lo, value, hi.bitcast(F32), ALU.subtract)
                return v.scalar_tensor_tensor(out=lo, in0=value, scalar=scale, in1=hi.bitcast(F32),
                                              op0=ALU.mult, op1=ALU.subtract)

            def half_log1p(y, s, s2, p):
                v.tensor_scalar(s, y, 2.0, None, ALU.add)
                v.drain()
                v.reciprocal(s2, s)
                v.drain()
                v.tensor_tensor(s, y, s2, ALU.mult)
                v.drain()
                v.tensor_tensor(s2, s, s, ALU.mult)
                v.drain()
                v.tensor_scalar(p, s2, 1.0 / 15, None, ALU.mult)
                for d in (13, 11, 9, 7, 5, 3):
                    v.drain()
                    v.scalar_tensor_tensor(out=p, in0=p, scalar=1.0 / d, in1=s2, op0=ALU.add, op1=ALU.mult)
                v.drain()
                v.scalar_tensor_tensor(out=p, in0=p, scalar=1.0, in1=s, op0=ALU.add, op1=ALU.mult)
                v.drain()

            dve.wait_ge(start_in, 64)
            v.memset(eps_col, EPS)
            v.memset(stat[:, 10:11], 0.0).then_inc(tiles_out, FREE_BANKS)
            v.memset(stat[:, 11:12], 0.0).then_inc(lg_done, 2)
            v.memset(stat[:, 12:13], 0.0).then_inc(o_out, 2)
            v.memset(stat[:, 13:14], 0.0).then_inc(x_ready, 8)

            with dve.Fori(0, DEPTH) as lay:
                def arrived(t, drain=False):
                    if drain:
                        v.drain()
                    dve.wait_ge(gemm_done, lay * N_TILES + TILE_NO[t] + 1)
                    return bank[TILE_NO[t] % N_BANKS]

                def left(instr, t):
                    instr.then_inc(tiles_out, 1 if t != TILES[-1] else 1 + TILES_PER_LAYER - N_TILES)

                def scaled(t, dst, rstd, factor=None):
                    b = arrived(t)[:, 0:256]
                    if factor is None:
                        left(v.tensor_tensor(dst, b, rstd, ALU.mult), t)
                    else:
                        left(v.scalar_tensor_tensor(out=dst, in0=b, scalar=factor, in1=rstd, op0=ALU.mult,
                                                    op1=ALU.mult), t)

                def norm_lo(name, src, g, hi, lo, n):
                    for k in range(n):
                        dve.wait_ge(nhi_ready, lay * NORM_TILES + NORM_FIRST[name] + k + 1)
                        low_part(lo(k), src(k), hi(k), Cp(g, k)).then_inc(nlo_ready, 1)

                def norm_rstd(name, dst, n):
                    b = arrived(("ss", name))[:, 0:256]
                    left(v.tensor_scalar(yt, b, 1.0 / n, EPS, ALU.mult, ALU.add), ("ss", name))
                    dve.wait_ge(sd_ready, lay * N_NORMS + NORM_NO[name] + 1)
                    v.reciprocal(dst, yt).then_inc(rstd_ready, 1)
                    v.drain()

                def logits(kind, u):
                    U = (0 if kind == "mla" else 16) + u
                    nk = P * (u % 2 + 1)
                    mask = C("mask_" + kind)[:, 256 - nk:256]
                    dve.wait_ge(s_done, lay * UNITS + U + 1)
                    v.memset(stat[:, 20:21], 0.0)
                    v.tensor_tensor_reduce(out=tile(lg, u % 2)[:, 0:nk], in0=s_bank[u % 2][:, 0:nk], in1=mask,
                                           scale=1.0, scalar=3.0e38, op0=ALU.add, op1=ALU.min,
                                           accum_out=nmax[u % 2]).then_inc(lg_done, 1)

                def normalise(kind, u):
                    U = (0 if kind == "mla" else 16) + u
                    nk = P * (u % 2 + 1)
                    dve.wait_ge(exp_done, lay * UNITS + U + 1)
                    v.reciprocal(rinv, rsum[u % 2])
                    v.drain()
                    p = tile(pr, u % 2)[:, 0:nk]
                    v.tensor_scalar(p, p, rinv, None, ALU.mult).then_inc(p_done, 1)

                def pair_out(kind, pair):
                    v.drain()
                    dve.wait_ge(pv_done, lay * UNITS + (pair * 4 + 4 + 2))
                    v.tensor_copy(o32, o_bank[:, (pair % 2) * 256:(pair % 2) * 256 + 256]).then_inc(o_out, 1)

                def pair_lo(kind, pair):
                    dve.wait_ge(ohi_ready, lay * PAIRS + pair + 1)
                    hi, lo = (mo_hi, mo_lo) if kind == "mla" else (fo_hi, fo_lo)
                    low_part(tile(lo, pair % 4), o32, tile(hi, pair % 4)).then_inc(olo_ready, 1)

                def lru_core(j):
                    T, I, X, R = tile(tr, j), tile(ti, j), tile(xc, j), tile(rec, j % 2)
                    if j == 0:
                        dve.wait_ge(lru_act, lay * 7 + 7)
                    v.tensor_scalar(R, T, -1.0, 1.0, ALU.mult, ALU.add)
                    v.drain()
                    v.reciprocal(R, R)
                    v.scalar_tensor_tensor(out=I, in0=I, scalar=1.0, in1=X, op0=ALU.add, op1=ALU.mult)
                    v.drain()
                    v.scalar_tensor_tensor(out=T, in0=T, scalar=1.0, in1=R, op0=ALU.add, op1=ALU.mult)
                    v.tensor_tensor(I, I, R, ALU.mult)
                    v.drain()
                    v.tensor_tensor(I, I, tile(sq_lru, j), ALU.mult)
                    v.drain()
                    v.tensor_tensor_scan(X, T, I, 0.0, ALU.mult, ALU.add)
                    v.drain()
                    v.scalar_tensor_tensor(out=X, in0=X, scalar=0.5, in1=tile(gl, j), op0=ALU.mult, op1=ALU.mult)\
                        .then_inc(lru_done, 1)

                def lru_lo_part(j):
                    dve.wait_ge(lruhi_ready, lay * 4 + j + 1)
                    low_part(tile(lru_lo, j), tile(xc, j), tile(lru_hi, j)).then_inc(lrulo_ready, 1)

                def hidden_lo(half, j):
                    dve.wait_ge(hhi_ready, lay * FF_T + half * HALF_T + j + 1)
                    low_part(tile(h_lo, j), tile(hid, j % 2), tile(h_hi, j)).then_inc(hlo_ready, 1)

                def merged_lo(n):
                    dve.wait_ge(mhi_ready, lay * 8 + n + 1)
                    low_part(tile(xb_lo, n), tile(merged, n), tile(xb_hi, n), 0.5).then_inc(mlo_ready, 1)

                def of_tile(t):
                    kind, j = t[0], t[-1]
                    if kind == "g":
                        b = arrived(t, drain=True)[:, 0:256]
                        left(v.tensor_tensor(tile(gt, j % 2), b, rstd_x, ALU.mult), t)
                    elif kind == "y":
                        b = arrived(t)[:, 0:256]
                        dve.wait_ge(gate_tanh, lay * N_GATES + gate_no(("g", t[1], j)) + 1)
                        if t[1] == 0:
                            left(v.scalar_tensor_tensor(out=tile(merged, j), in0=tile(gt, j % 2), scalar=1.0, in1=b,
                                                        op0=ALU.add, op1=ALU.mult), t)
                        else:
                            left(v.scalar_tensor_tensor(out=yt, in0=tile(gt, j % 2), scalar=1.0, in1=b,
                                                        op0=ALU.add, op1=ALU.mult), t)
                            v.drain()
                            ins = v.tensor_tensor(tile(merged, j), tile(merged, j), yt, ALU.add)
                            if t[1] == 2:
                                ins.then_inc(merged_ready, 1)
                                if j:
                                    merged_lo(j - 1)
                    elif kind == "fl":
                        b = arrived(t)[:, 0:256]
                        left(v.tensor_tensor(f_z, b, rstd_x, ALU.mult), t)
                        v.drain()
                        v.tensor_scalar(f_z, f_z, Cp("bf"), -1.0, ALU.add, ALU.mult)
                        v.drain()
                        v.scalar_tensor_tensor(out=f_ab, in0=f_z, scalar=-1.0, in1=f_z, op0=ALU.mult, op1=ALU.max)\
                            .then_inc(fl_abs, 1)
                    elif kind == "fq":
                        scaled(t, tile(fq, j), rstd_x, -FOX_SCALE)
                    elif kind == "fk":
                        scaled(t, tile(fk, j), rstd_x)
                    elif kind in ("wo", "dn"):
                        b = arrived(t)[:, 0:256]
                        ins = v.tensor_tensor(tile(x, j), b, tile(x, j), ALU.add)
                        left(ins, t)
                    elif kind == "hg":
                        b = arrived(t, drain=True)[:, 0:256]
                        left(v.tensor_tensor(tile(gt, j % 2), b, rstd_x, ALU.mult), t)
                        if j:
                            hidden_lo(t[1], j - 1)
                    elif kind == "hu":
                        b = arrived(t)[:, 0:256]
                        left(v.tensor_tensor(ut, b, rstd_x, ALU.mult), t)
                        dve.wait_ge(gate_tanh, lay * N_GATES + gate_no(("hg", t[1], j)) + 1)
                        g = tile(gt, j % 2)
                        v.scalar_tensor_tensor(out=g, in0=tile(th, j % 2), scalar=1.0, in1=g, op0=ALU.add,
                                               op1=ALU.mult)
                        v.drain()
                        v.scalar_tensor_tensor(out=tile(hid, j % 2), in0=g, scalar=0.5, in1=ut, op0=ALU.mult,
                                               op1=ALU.mult).then_inc(hid_ready, 1)
                    elif kind == "pg":
                        b = arrived(t, drain=True)[:, 0:256]
                        left(v.tensor_tensor(tile(gt, j % 2), b, rstd_x, ALU.mult), t)
                    elif kind == "pp":
                        b = arrived(t)[:, 0:256]
                        dve.wait_ge(gate_tanh, lay * N_GATES + gate_no(("pg", j)) + 1)
                        left(v.scalar_tensor_tensor(out=yt, in0=tile(gt, j % 2), scalar=1.0, in1=b, op0=ALU.add,
                                                    op1=ALU.mult), t)
                        v.drain()
                        v.scalar_tensor_tensor(out=tile(x, j), in0=yt, scalar=0.5, in1=tile(x, j), op0=ALU.mult,
                                               op1=ALU.add).then_inc(x_ready, 1)

                v.tensor_copy(cur, par[:, bass.ds(lay * NPAR, NPAR)])
                v.drain()
                v.tensor_scalar(hgb, cur[:, PAR["gate_b"]:PAR["gate_b"] + 24], 0.5, None, ALU.mult)\
                    .then_inc(par_ready, 1)
                lam = cur[:, PAR["lam"]:PAR["lam"] + 4]
                v.scalar_tensor_tensor(out=small[:, 0:4], in0=lam, scalar=-1.0, in1=lam, op0=ALU.mult, op1=ALU.max)\
                    .then_inc(lam_abs, 1)
                v.memset(u_pad.rearrange("p (j n) -> p j n", n=259)[:, :, 0:3], 0.0)
                norm_lo("mix", lambda k: tile(x, k), "mix_g", lambda k: tile(xa_hi, k), lambda k: tile(xa_lo, k), 8)
                norm_rstd("mix", rstd_x, D)
                dve.wait_ge(lam_exp, lay + 1)
                half_log1p(small[:, 4:8], small[:, 8:12], small[:, 12:16], small[:, 16:20])
                v.tensor_scalar(small[:, 20:24], lam, -1.0, 0.0, ALU.mult, ALU.max)
                v.drain()
                v.scalar_tensor_tensor(out=small[:, 16:20], in0=small[:, 16:20], scalar=2.0, in1=small[:, 20:24],
                                       op0=ALU.mult, op1=ALU.add)
                v.drain()
                v.tensor_scalar(m2sp, small[:, 16:20], -2.0, None, ALU.mult).then_inc(m2sp_ready, 1)
                for j in range(4):
                    b = arrived(("u", j))[:, 0:256]
                    left(v.tensor_tensor(u_pad[:, j * 259 + 3:(j + 1) * 259], b, rstd_x, ALU.mult), ("u", j))
                for j in range(4):
                    scaled(("gl", j), tile(gl, j), rstd_x)
                v.drain()
                dve.wait_ge(xc_begun, lay * 4 + 4)
                for kk in range(1, CONV):
                    if kk > 1:
                        v.drain()
                    for j in range(4):
                        last = v.scalar_tensor_tensor(out=tile(xc, j), in0=u_pad[:, j * 259 + kk:j * 259 + kk + 256],
                                                      scalar=Cp("conv_w", 4 * kk + j), in1=tile(xc, j),
                                                      op0=ALU.mult, op1=ALU.add)
                last.then_inc(xc_done, 1)
                dve.wait_ge(gl_sq, lay * 4 + 4)
                v.tensor_scalar(tr, tr, 0.044715, 1.0, ALU.mult, ALU.add)
                v.drain()
                v.tensor_tensor(tr, tr, gl, ALU.mult).then_inc(gl_inner, 1)
                dve.wait_ge(xchi_ready, lay + 1)
                low_part(xc_lo, xc, xc_hi).then_inc(xclo_ready, 1)
                dve.wait_ge(gl_tanh, lay + 1)
                v.scalar_tensor_tensor(out=gl, in0=tr, scalar=1.0, in1=gl, op0=ALU.add, op1=ALU.mult)
                v.drain()
                for j in range(3):
                    scaled(("cq", j), tile(c_raw, j), rstd_x)
                for j in range(2):
                    scaled(("ckv", j), tile(c_raw, 3 + j), rstd_x)
                scaled(("kr", 0), krz, rstd_x)
                v.drain()
                norm_lo("q", lambda k: tile(c_raw, k), "q_g", lambda k: tile(cn_hi, k), lambda k: tile(cn_lo, k), 3)
                norm_rstd("q", rstd_q, 384)
                norm_lo("kv", lambda k: tile(c_raw, 3 + k), "kv_g", lambda k: tile(cn_hi, 3 + k),
                        lambda k: tile(cn_lo, 3 + k), 2)
                norm_rstd("kv", rstd_kv, 256)
                b = arrived(("col", "mix"))
                left(v.tensor_copy(rcol[:, 0:2], b[:, 0:2]), ("col", "mix"))
                v.drain()
                for kind, dst, bias in (("wa", tr, "ba"), ("wx", ti, "bx")):
                    for j in range(4):
                        b = arrived((kind, j))[:, 0:256]
                        left(v.tensor_scalar(tile(dst, j), b, Cp(bias, j), 0.5, ALU.add, ALU.mult), (kind, j))

                def rotate(t, z):
                    b = arrived(t)[:, 0:256]
                    left(v.tensor_tensor(yt, b, C("sin"), ALU.mult), t)
                    v.tensor_tensor(z, z, C("cos"), ALU.mult)
                    v.drain()
                    return v.tensor_tensor(z, z, yt, ALU.add)

                rotate(("rotk", 0), krz)
                v.drain()
                for s in range(2):
                    v.tensor_scalar(tile(krm, s), krz, C("sub")[:, s:s + 1], None, ALU.mult)
                for m in range(2):
                    b = arrived(("fv", m))
                    left(v.tensor_scalar(tile(vf, m, 512), b[:, :], rcol[:, m:m + 1], None, ALU.mult), ("fv", m))
                b = arrived(("col", "kv"))
                left(v.tensor_copy(rcol[:, 2:4], b[:, 0:2]), ("col", "kv"))
                v.drain()
                for m in range(2):
                    b = arrived(("vm", m))
                    left(v.tensor_scalar(tile(vm, m, 512), b[:, :], rcol[:, 2 + m:3 + m], None, ALU.mult), ("vm", m))
                lru_core(0)
                for j in range(4):
                    scaled(("kn", j), tile(kn, j), rstd_kv)
                lru_core(1)
                lru_lo_part(0)
                for j in range(4):
                    scaled(("qn", j), tile(qn, j), rstd_q, -MLA_SCALE)
                lru_core(2)
                lru_lo_part(1)
                for j in range(2):
                    scaled(("qr", j), tile(qr, j), rstd_q, -MLA_SCALE)
                v.drain()
                for j in range(2):
                    last = rotate(("rotq", j), tile(qr, j))
                    v.drain()
                v.memset(stat[:, 17:18], 0.0).then_inc(mla_ready, 1)
                lru_core(3)
                lru_lo_part(2)

                for kind, fill in (("mla", MLA_FILL), ("fox", FOX_FILL)):
                    first_pair = 0 if kind == "mla" else 4
                    for i in range(17):
                        if i < 16:
                            logits(kind, i)
                            normalise(kind, i)
                        if kind == "mla" and i == 0:
                            lru_lo_part(3)
                        if i < 16:
                            of_tile(fill[i])
                        if kind == "mla" and i == 2:
                            dve.wait_ge(fl_exp, lay + 1)
                            half_log1p(f_den, f_s, f_s2, f_p)
                            v.tensor_scalar(f_z, f_z, 0.0, None, ALU.max)
                            v.drain()
                            v.scalar_tensor_tensor(out=f_p, in0=f_p, scalar=2.0, in1=f_z, op0=ALU.mult, op1=ALU.add)
                            v.drain()
                            v.tensor_tensor_scan(f_z, ones, f_p, 0.0, ALU.mult, ALU.subtract)
                            v.drain()
                            for r in (0, 64):
                                v.tensor_copy(rk[r:r + 32], f_z[r:r + 32])
                                v.memset(rk[r + 32:r + 64], 1.0)
                                v.memset(lq[r:r + 32], 1.0)
                                v.tensor_scalar(lq[r + 32:r + 64], f_z[r + 32:r + 64], -1.0, None, ALU.mult)
                            v.drain()
                            v.memset(stat[:, 18:19], 0.0).then_inc(decay_ready, 1)
                        if i and i % 4 == 0:
                            pair_out(kind, first_pair + (i - 1) // 4)
                            pair_lo(kind, first_pair + (i - 1) // 4)
                for t in MID_TILES:
                    of_tile(t)
                merged_lo(7)
                for n in range(8):
                    of_tile(("wo", n))
                norm_lo("ffn", lambda k: tile(x, k), "ffn_g", lambda k: tile(xa_hi, k), lambda k: tile(xa_lo, k), 8)
                norm_rstd("ffn", rstd_x, D)
                for half in range(2):
                    for j in range(HALF_T):
                        of_tile(("hg", half, j))
                        of_tile(("hu", half, j))
                    hidden_lo(half, HALF_T - 1)
                    if half == 1:
                        dve.wait_ge(phi_ready, lay + 1)
                        low_part(p_lo, p_raw, p_hi).then_inc(plo_ready, 1)
                    for n in range(8):
                        of_tile(("dn", half, n))
                norm_lo("ple", lambda k: tile(x, k), "ple_g", lambda k: tile(xb_hi, k), lambda k: tile(xb_lo, k), 8)
                norm_rstd("ple", rstd_x, D)
                for t in TAIL_TILES[-16:]:
                    of_tile(t)

            def arrived2(t):
                dve.wait_ge(gemm_done, FIRST_GEMM2 + TILE_NO2[t] + 1)
                return bank[(FIRST_TILE2 + TILE_NO2[t]) % N_BANKS]

            roots = 0

            def norm_rstd2(t):
                nonlocal roots
                b = arrived2(t)
                wide = t[1:] in ((0, 0), (0, 1), (1, 0))
                w = 512 if wide else 256
                a = slice(0, 512) if wide else slice(256, 512)
                v.drain()
                v.tensor_scalar(var2[:, a], b[:, 0:w], 1.0 / D, EPS, ALU.mult, ALU.add).then_inc(tiles_out, 1)
                roots += 1
                dve.wait_ge(sd2_ready, roots)
                v.reciprocal(rstd2[:, a], var2[:, a])
                v.drain()

            def scale_tile(l, i, t):
                a = slice(0, 512) if len(sides(l, i)) == 2 else slice(256, 512)
                v.tensor_tensor(tile(tmp, t % 2, 512)[:, a], tile(h, t, 512)[:, a], rstd2[:, a], ALU.mult)\
                    .then_inc(scaled2, 1)

            acted = 0

            def modulated(l, i):
                nonlocal acted
                a = slice(0, 512) if len(sides(l, i)) == 2 else slice(256, 512)
                for t in range(KT):
                    scale_tile(l, i, t)
                    v.drain()
                    for s in sides(l, i):
                        v.tensor_scalar(side(m32, 0, s), side(tmp, t % 2, s), gain_col(l, i, t, s),
                                        mod_col(l, SH1 if i == 0 else SH2, t, s), ALU.mult, ALU.add)
                    v.drain()
                    dve.wait_ge(m_act, acted + t + 1)
                    low_part(tile(m_lo, t, 512)[:, a], m32[:, a], tile(m_hi, t, 512)[:, a]).then_inc(m_split, 1)
                acted += KT

            def add_gated(t, n, col, s_list, whole):
                b = arrived2(t)
                for s in s_list:
                    src = b[:, s * 256:(s + 1) * 256] if whole else b[:, 0:256]
                    last = v.scalar_tensor_tensor(out=side(h, n, s), in0=src, scalar=col(s), in1=side(h, n, s),
                                                  op0=ALU.mult, op1=ALU.add)
                last.then_inc(tiles_out, 1)

            def hidden2(l):
                a = slice(0, 512) if l == 0 else slice(256, 512)
                w = 512 if l == 0 else 256

                for q in range(QUARTERS):
                    for j in range(QT + 2):
                        if j < QT:
                            b = arrived2(("w1", l, q, j))
                        if j >= 2:
                            dve.wait_ge(act2_hi, (l * QUARTERS + q) * QT + j - 1)
                        v.drain()
                        if j < QT:
                            v.tensor_scalar(tile(tmp, j % 2, 512)[:, a], b[:, 0:w], 0.0, None, ALU.max)\
                                .then_inc(tiles_out, 1)
                        if 1 <= j <= QT:
                            r = tile(tmp, (j - 1) % 2, 512)[:, a]
                            v.tensor_tensor(tile(squares, (j - 1) % 2, 512)[:, a], r, r, ALU.mult)
                        if j >= 2:
                            low_part(tile(hid_lo, j - 2, 512)[:, a], tile(squares, j % 2, 512)[:, a],
                                     tile(hid_hi, j - 2, 512)[:, a]).then_inc(act2_lo, 1)
                    v.drain()
                    for n in range(KT):
                        add_gated(("w2", l, q, n), n, lambda s: mod_col(l, G2, n, s), (0, 1) if l == 0 else (1,),
                                  l == 0)
                    v.drain()

            v.memset(silu_c.bitcast(F32), 0.0)
            dve.wait_ge(silu_act, 1)
            v.scalar_tensor_tensor(out=svec[:, 16:32], in0=svec[:, 0:16], scalar=1.0,
                                   in1=par2[:, PAR2["cc"]:PAR2["cc"] + 16], op0=ALU.add, op1=ALU.mult)
            v.drain()
            v.tensor_scalar(svec[:, 16:32], svec[:, 16:32], 0.5, None, ALU.mult).then_inc(silu_act, 1)
            v.tensor_scalar(qg_scaled, par2[:, PAR2["q_g"]:PAR2["q_g"] + 1], -GQA_SCALE, None, ALU.mult)
            norm_rstd2(("ss", "first"))
            dve.wait_ge(silu_act, 3)
            s4 = silu_c.rearrange("p (k n) -> p k n", n=P)
            low_part(s4[:, :, 2:4], svec[:, 16:32].rearrange("p (k s) -> p k s", s=2), s4[:, :, 0:2])\
                .then_inc(silu_ready, 1)
            dve.wait_ge(late_in, 32)
            for t in range(KT):
                v.scalar_tensor_tensor(out=side(h, t, 1), in0=tile(x, t),
                                       scalar=par2[:, PAR2["first_g"] + t:PAR2["first_g"] + t + 1],
                                       in1=rstd2[:, 256:512], op0=ALU.mult, op1=ALU.mult).then_inc(h_ready, 1)
            for t in ada_tiles():
                if t[0] == "ada":
                    n, i = t[1] * ADA_GROUPS + t[2] // 4, t[2] % 4
                    at = (n % 2) * 1024 + i * 256
                    v.drain()
                    v.tensor_copy(rows[0:4, at:at + 256], arrived2(t)[0:4, 0:256]).then_inc(tiles_out, 1)
                else:
                    n = t[1] * ADA_GROUPS + t[2]
                    v.tensor_copy(turned, arrived2(t)[:, 0:32]).then_inc(tiles_out, 1)
                    v.drain()
                    t4 = turned.rearrange("p (i a s) -> p i a s", a=2, s=2)
                    m = mod[:, n * 16:(n + 1) * 16].rearrange("p (i s) -> p i s", s=2)
                    v.tensor_tensor(m, t4[:, :, 0, :], t4[:, :, 1, :], ALU.add)
                    v.drain()
                    at = PAR2["ada_b"] + n * 8
                    for s in range(2):
                        v.tensor_tensor(m[:, :, s], m[:, :, s], par2[:, at:at + 8], ALU.add)
            v.drain()
            mods = mod.rearrange("p (l k t s) -> p l k t s", l=DEPTH, k=6, s=2)
            gains = gain.rearrange("p (l i t s) -> p l i t s", l=DEPTH, i=2, s=2)
            for l in range(DEPTH):
                for i in range(2):
                    at = PAR2["norm_g"] + (l * 2 + i) * 8
                    for s in range(2):
                        v.scalar_tensor_tensor(out=gains[:, l, i, :, s], in0=mods[:, l, SC1 if i == 0 else SC2, :, s],
                                               scalar=1.0, in1=par2[:, at:at + 8], op0=ALU.add, op1=ALU.mult)
            pg2 = pool_gate.rearrange("p (t s) -> p t s", s=2)
            for s in range(2):
                v.tensor_tensor(pg2[:, :, s], mods[:, 0, G1, :, s], par2[:, PAR2["pool_scale"]:PAR2["pool_scale"] + 8],
                                ALU.mult)
            v.drain()
            pad4 = padded.rearrange("p (b s n) -> p b s n", b=2, s=2)
            v.memset(padded, 0.0)
            norm_rstd2(("ss", 0, 0))
            sums = [a.rearrange("p (s n) -> p s n", s=2) for a in (sum_a, sum_b)]
            scale_tile(0, 0, 0)
            for t in range(KT):
                v.drain()
                if t + 1 < KT:
                    if t >= 1:
                        dve.wait_ge(pooled_hi, t)
                    scale_tile(0, 0, t + 1)
                dve.wait_ge(m_act, t + 1)
                a = pad4[:, t % 2]
                src, reach = a, 1
                lo_, hi_ = 1, 272
                v.tensor_tensor(sums[0][:, :, 1:272], a[:, :, 0:271], a[:, :, 1:272], ALU.add)
                cur_, edge = 0, 1
                for step in range(t // 2):
                    d = 1 << step
                    lo_, hi_ = lo_ + d, hi_ - d
                    v.drain()
                    v.tensor_tensor(sums[1 - cur_][:, :, lo_:hi_], sums[cur_][:, :, lo_ - d:hi_ - d],
                                    sums[cur_][:, :, lo_ + d:hi_ + d], ALU.add)
                    cur_ = 1 - cur_
                v.drain()
                w = sums[cur_][:, :, 8:264]
                inv = C2("inv_count")[:, (t // 2) * 256:(t // 2 + 1) * 256]
                for s in range(2):
                    v.tensor_tensor(w[:, s], w[:, s], inv, ALU.mult)
                v.drain()
                v.tensor_tensor(tile(tmp, t % 2, 512).rearrange("p (s n) -> p s n", s=2), w, a[:, :, 8:264],
                                ALU.subtract).then_inc(pooled, 1)
                dve.wait_ge(pooled_hi, t + 1)
                low_part(tile(m_lo, t, 512), tile(tmp, t % 2, 512), tile(m_hi, t, 512)).then_inc(m_split, 1)
            acted += KT
            for t in range(KT):
                add_gated(("pool", t), t, lambda s: pool_gate[:, 2 * t + s:2 * t + s + 1], (0, 1), True)
            norm_rstd2(("ss", 0, 1))
            modulated(0, 1)
            hidden2(0)
            norm_rstd2(("ss", 1, 0))
            modulated(1, 0)
            for name, n, w, first in (("q", 8, 256, 0), ("k", KV_HEADS, 512, 8)):
                for t in staggered(name, n):
                    j = t[1]
                    z = tile(q2, j) if name == "q" else tile(k2, j, 512)
                    g = qg_scaled if name == "q" else par2[:, PAR2["k_g"]:PAR2["k_g"] + 1]
                    b = arrived2(t)
                    if t[0] == name:
                        v.tensor_copy(z, b[:, 0:w]).then_inc(tiles_out, 1)
                    elif t[0] == name + "ss":
                        v.drain()
                        v.tensor_scalar(var2[:, 0:w], b[:, 0:w], 1.0 / P, EPS, ALU.mult, ALU.add)\
                            .then_inc(tiles_out, 1)
                        dve.wait_ge(hsd_ready, first + j + 1)
                        v.reciprocal(rstd2[:, 0:w], var2[:, 0:w])
                        v.drain()
                        v.scalar_tensor_tensor(out=z, in0=z, scalar=g, in1=rstd2[:, 0:w], op0=ALU.mult, op1=ALU.mult)\
                            .then_inc(hn_ready, 1)
                    else:
                        if name == "k":
                            z = side(k2, j, 1)
                        v.drain()
                        v.tensor_tensor(m32[:, 0:256], b[:, 0:256], C2("sin"), ALU.mult).then_inc(tiles_out, 1)
                        v.tensor_tensor(z, z, C2("cos"), ALU.mult)
                        v.drain()
                        v.tensor_tensor(z, z, m32[:, 0:256], ALU.add)
            for m in range(4):
                b = arrived2(("v", m))
                v.tensor_copy(tile(v2, m, 512), b[:, :]).then_inc(tiles_out, 1)
            v.drain()
            v.memset(stat[:, 19:20], 0.0).then_inc(qkv_ready, 1)

            def maximum2(u):
                dve.wait_ge(s2_done, u + 1)
                v.tensor_reduce(out=nmax[u % 2], in_=s_bank[u % 2][:, :], axis=AXX, op=ALU.min).then_inc(max2_done, 1)

            def normalise2(u):
                dve.wait_ge(exp2_done, u + 1)
                v.reciprocal(rinv, rsum[u % 2])
                v.drain()
                p = tile(pr2, u % 2, 512)
                v.tensor_scalar(p, p, rinv, None, ALU.mult).then_inc(p2_done, 1)

            for i in range(18):
                if i < 16:
                    maximum2(i)
                if i < 16:
                    normalise2(i)
                if i >= 3 and i % 2 == 1:
                    hd = (i - 3) // 2
                    dve.wait_ge(pv2_done, 2 * hd + 2)
                    v.drain()
                    v.tensor_copy(o32b, o_banks2[hd % 2][:, 0:256]).then_inc(o2_out, 1)
                    dve.wait_ge(o2_hi, hd + 1)
                    v.drain()
                    low_part(tile(oh_lo, hd), o32b, tile(oh_hi, hd)).then_inc(o2_lo, 1)
            for n in range(KT):
                add_gated(("o", n), n, lambda s: mod_col(1, G1, n, s), (1,), False)
            norm_rstd2(("ss", 1, 1))
            modulated(1, 1)
            hidden2(1)
            norm_rstd2(("ss", "last"))
            for t in range(KT):
                v.scalar_tensor_tensor(out=tile(sq2, t), in0=side(h, t, 1),
                                       scalar=par2[:, PAR2["final_g"] + t:PAR2["final_g"] + t + 1],
                                       in1=rstd2[:, 256:512], op0=ALU.mult, op1=ALU.mult).then_inc(result_ready, 1)


def kernel(**inputs):
    import concourse.bacc as bacc
    from concourse.bass_utils import run_bass_kernel_spmd

    a = {k: np.asarray(v) for k, v in inputs.items()}
    const, const2 = shape_constants()
    par, par2 = pack_parameters(a)
    arrays = {
        "stream": pack_stream(a),
        "x": token_minor(a["x"][0]),
        "ctx": token_minor(a["ctx_2"][0]),
        "p": np.stack([token_minor(a["p"][l, 0]) for l in range(DEPTH)]),
        "par": par,
        "par2": par2,
        "const": const,
        "const2": const2,
    }
    nc = bacc.Bacc("TRN2", target_bir_lowering=False, num_devices=1)
    ins = [nc.dram_tensor(f"in_{n}", list(v.shape), F32, kind="ExternalInput").ap() for n, v in arrays.items()]
    out = nc.dram_tensor("out_0", [P, KT * S], F32, kind="ExternalOutput").ap()
    build(nc, ins, out)
    r = run_bass_kernel_spmd(nc, [{f"in_{n}": v for n, v in arrays.items()}], core_ids=[0])
    got = r.results[0]["out_0"]
    return np.ascontiguousarray(np.asarray(got).reshape(P, KT, S).transpose(2, 1, 0).reshape(1, S, D))
```

```python
from contextlib import ExitStack

import numpy as np

import concourse.bass as bass
from concourse import mybir

F32 = mybir.dt.float32
F32R = mybir.dt.float32r
ALU = mybir.AluOpType
ACT = mybir.ActivationFunctionType
AXX = mybir.AxisListType.X

P = 128
D = 1024
S = 256
DEPTH = 2
KT = D // P
LRU_T = 512 // P
CONV = 4
Q_LORA_T = 384 // P
KV_LORA_T = 256 // P
HEADS = 8
D_FF = 2816
FF_T = D_FF // P
HALF_T = FF_T // 2
PLE_T = 256 // P
EPS = 1e-6
MLA_SCALE = 96.0 ** -0.5
FOX_SCALE = 64.0 ** -0.5
GELU_C = (2.0 / np.pi) ** 0.5
BIG = 1.0e30

CHUNK_ATOMS = 10
RING = 4
CH = CHUNK_ATOMS * P
AHEAD = 3

PAR = {}
_n = 0
for _name, _w in (("mix_g", 8), ("gate_b", 24), ("conv_w", 16), ("conv_b", 4), ("ba", 4), ("bx", 4), ("lam", 4),
                  ("q_g", 3), ("kv_g", 2), ("ffn_g", 8), ("ple_g", 8), ("bf", 1)):
    PAR[_name] = _n
    _n += _w
NPAR = _n

ATOMS_OF = {"ss": 0, "u": 8, "gl": 8, "cq": 8, "ckv": 8, "kr": 8, "col": 0, "wa": 1, "wx": 1, "rotk": 0,
            "fv": 32, "vm": 8, "kn": 2, "qn": 3, "qr": 3, "rotq": 0, "fl": 8, "fq": 8, "fk": 8, "g": 8, "y": 4,
            "wo": 8, "hg": 8, "hu": 8, "dn": 11, "pg": 8, "pp": 2, "ada": 16, "turn": 0}
BRANCH_TILES = [[t for n in range(8) for t in (("g", b, n), ("y", b, n))] for b in range(3)]
HEAD_TILES = (
    [("ss", "mix")] + [("u", j) for j in range(4)] + [("gl", j) for j in range(4)]
    + [("cq", j) for j in range(3)] + [("ckv", j) for j in range(2)] + [("kr", 0)]
    + [("ss", "q"), ("ss", "kv"), ("col", "mix")]
    + [("wa", j) for j in range(4)] + [("wx", j) for j in range(4)]
    + [("rotk", 0), ("fv", 0), ("fv", 1), ("col", "kv"), ("vm", 0), ("vm", 1)]
    + [("kn", j) for j in range(4)] + [("qn", j) for j in range(4)] + [("qr", 0), ("qr", 1)]
    + [("rotq", 0), ("rotq", 1)])
ADA_TILES = DEPTH * 6 * D // 256
LAYER_ADA = 20


def with_modulation(tiles, places, first, start=0, end=None):
    out, n = [], first
    for t in tiles:
        for _ in range(places.get(t, 0)):
            out += [("turn", n // 2 - 1)] if n % 2 == 0 and n > start else []
            out.append(("ada", n))
            n += 1
        out += [("turn", n // 2 - 1)] if t == end else []
        out.append(t)
    return out, n


MLA_FILL = [("fl", 0)] + [("fq", j) for j in range(4)] + [("fk", j) for j in range(4)] + BRANCH_TILES[0][:7]
FOX_FILL = BRANCH_TILES[0][7:] + BRANCH_TILES[1][:7]
MID_TILES = BRANCH_TILES[1][7:] + BRANCH_TILES[2]
TAIL_TILES = (
    [("wo", n) for n in range(8)] + [("ss", "ffn")]
    + [t for h in range(2) for t in [u for j in range(HALF_T) for u in (("hg", h, j), ("hu", h, j))]
       + [("dn", h, n) for n in range(8)]]
    + [("ss", "ple")] + [t for n in range(8) for t in (("pg", n), ("pp", n))])
HEAD_TILES, _n = with_modulation(HEAD_TILES, {("ss", "mix"): 2, ("ss", "q"): 1, ("ss", "kv"): 1, ("qn", 0): 1,
                                              ("rotq", 0): 1}, 0, end=("rotq", 1))
MID_TILES, _n = with_modulation(MID_TILES, {("g", 2, j): 1 for j in (0, 2, 4, 6)}, _n, _n)
TAIL_TILES, _n = with_modulation(TAIL_TILES, {("ss", "ffn"): 2, ("hg", 0, 3): 1, ("hg", 0, 5): 1, ("hg", 0, 7): 1,
                                              ("hg", 1, 3): 1, ("hg", 1, 5): 1, ("hg", 1, 7): 1, ("ss", "ple"): 2}, _n, end=("pg", 4))
assert _n == LAYER_ADA
FF_TILES = TAIL_TILES[TAIL_TILES.index(("hg", 0, 0)):TAIL_TILES.index(("dn", 1, 0))]
PLE_TILES = TAIL_TILES[TAIL_TILES.index(("ss", "ple")) + 1:]
TILES = HEAD_TILES + MLA_FILL + FOX_FILL + MID_TILES + TAIL_TILES
TILE_NO = {t: i for i, t in enumerate(TILES)}
N_TILES = len(TILES)
N_BANKS = 4
TILES_PER_LAYER = -(-N_TILES // N_BANKS) * N_BANKS


def modulation_before(tiles):
    out, run = {}, []
    for t in tiles:
        if t[0] in ("ada", "turn"):
            run.append(t)
        else:
            out[t], run = run, []
    return out


BEFORE = modulation_before(TILES)
SHARED = {("fv", 1), ("vm", 1)}


def first_atoms():
    at, out = 0, {}
    for t in TILES:
        if t in SHARED:
            out[t] = (out[(t[0], 0)][0], out[(t[0], 0)][1])
            continue
        out[t] = (at, at + ATOMS_OF[t[0]])
        at += ATOMS_OF[t[0]]
    return out, at


ATOM_SPAN, LAYER_ATOMS = first_atoms()
LAYER_CHUNKS = -(-LAYER_ATOMS // (CHUNK_ATOMS * RING)) * RING


def last_chunk(span):
    return max(span[1] - 1, 0) // CHUNK_ATOMS


MOD_T = 6 * D // P
MLP_T = 4 * D // P
QUARTERS = 4
QT = MLP_T // QUARTERS
KV_HEADS = 4
B2_ATOMS_ADA = (ADA_TILES - DEPTH * LAYER_ADA) * 2 * KT
B2 = {}
_at = 0
for _name, _n in (("ada", B2_ATOMS_ADA), ("pool", 16), ("mlp0", 2 * MLP_T * KT), ("q", 64), ("k", 32), ("v", 32),
                  ("o", 64), ("mlp1", 2 * MLP_T * KT)):
    B2[_name] = _at
    _at += _n
B2_ATOMS = _at
B2_CHUNKS = -(-B2_ATOMS // (CHUNK_ATOMS * RING)) * RING
N_CHUNKS = DEPTH * LAYER_CHUNKS + B2_CHUNKS

def mlp_tiles(l):
    return [t for q in range(QUARTERS) for t in [("w1", l, q, j) for j in range(QT)] + [("w2", l, q, n) for n in range(KT)]]


Q_TILES = [t for j in range(9) for t in ([("q", j)] if j < 8 else []) + ([("qrot", j - 1)] if j else [])]
K_TILES = [t for j in range(KV_HEADS + 1) for t in ([("k", j)] if j < KV_HEADS else [])
           + ([("kss", j - 1)] if j else []) + ([("krot", j - 2)] if 2 <= j < KV_HEADS else [])]
V_TILES = [("v", m) for m in range(4)]
LATE_ROTATIONS = [("krot", j) for j in range(KV_HEADS - 2, KV_HEADS)]


ATOMS_OF2 = {"ada": 16, "pool": 2, "w1": 8, "w2": 8, "q": 8, "k": 8, "v": 32, "o": 8}
TILES2 = (
    [("ss", "first")]
    + [("ss", 0, 0)] + [("pool", t) for t in range(KT)]
    + [("ss", 0, 1)] + mlp_tiles(0)
    + [("ss", 1, 0)] + Q_TILES + K_TILES + V_TILES + LATE_ROTATIONS
    + [("o", n) for n in range(KT)]
    + [("ss", 1, 1)] + mlp_tiles(1) + [("ss", "last")])
TILES2, _n = with_modulation(TILES2, {("ss", "first"): 2, ("ss", 0, 0): 2, ("pool", 0): 2,
                                      ("ss", 0, 1): 2}, DEPTH * LAYER_ADA, DEPTH * LAYER_ADA,
                             ("w1", 0, 0, 0))
assert _n == ADA_TILES
BEFORE2 = modulation_before(TILES2)
TILE_NO2 = {t: i for i, t in enumerate(TILES2)}


def second_spans():
    at, out = 0, {}
    for t in TILES2:
        n = 0 if t[0] == "v" and t[1] else ATOMS_OF2.get(t[0], 0)
        if t[0] == "v" and t[1]:
            out[t] = out[("v", 0)]
            continue
        out[t] = (at, at + n)
        at += n
    assert at == B2_ATOMS, (at, B2_ATOMS)
    return out


ATOM_SPAN2 = second_spans()
FIRST_CHUNK2 = DEPTH * LAYER_CHUNKS
FIRST_TILE2 = DEPTH * TILES_PER_LAYER
FIRST_GEMM2 = DEPTH * N_TILES
SH1, SC1, G1, SH2, SC2, G2 = range(6)
GQA_SCALE = float(P) ** -0.5

PAR2 = {}
_n = 0
for _name, _w in (("cc", 16), ("ada_b", 96), ("norm_g", 32), ("pool_scale", 8), ("q_g", 1), ("k_g", 1),
                  ("final_g", 8), ("first_g", 8)):
    PAR2[_name] = _n
    _n += _w
NPAR2 = _n

CONST = {}
_n = 0
for _name, _w in (("ident", 128), ("ones", 256), ("mask_mla", 256), ("mask_fox", 256), ("cos", 256), ("sin", 256),
                  ("rot", 128), ("onehot", 8), ("sub", 2)):
    CONST[_name] = (_n, _w)
    _n += _w
NCONST = _n
CONST2 = {}
_n = 0
for _name, _w in (("cos", 256), ("sin", 256), ("rot", 128), ("inv_count", 4 * 256)):
    CONST2[_name] = (_n, _w)
    _n += _w
NCONST2 = _n


def shape_constants():
    c = np.zeros((P, NCONST), np.float32)

    def put(dst, table, name, value):
        at, w = table[name]
        dst[:, at:at + w] = value

    put(c, CONST, "ident", np.eye(P))
    put(c, CONST, "ones", 1.0)
    i = np.arange(P)
    for name, seen in (("mask_mla", i[:, None] // 64 >= i[None, :] // 64), ("mask_fox", i[:, None] >= i[None, :])):
        m = np.zeros((P, 256), np.float32)
        m[:, P:] = np.where(seen, 0.0, BIG)
        put(c, CONST, name, m)
    pos = np.arange(S, dtype=np.float32)
    inv = (np.float32(10000.0) ** (-np.arange(0, 32, 2, dtype=np.float32) / np.float32(32))).astype(np.float32)
    ang = pos[None, :] * inv[i % 16][:, None]
    put(c, CONST, "cos", np.cos(ang))
    put(c, CONST, "sin", np.sin(ang))

    def rotation(width):
        r = np.zeros((P, P), np.float32)
        for m in range(P):
            if m % (2 * width) < width:
                r[m + width, m] = -1.0
            else:
                r[m - width, m] = 1.0
        return r

    put(c, CONST, "rot", rotation(16))
    onehot = np.zeros((P, 8), np.float32)
    for base in (0, 32, 64, 96):
        onehot[base:base + 8] = np.eye(8)
    put(c, CONST, "onehot", onehot)
    put(c, CONST, "sub", np.stack([(i // 32) % 2 == 0, (i // 32) % 2 == 1], 1))
    d = np.zeros((P, NCONST2), np.float32)
    half = 64
    inv = (np.float32(10000.0) ** (-np.arange(0, half, 2, dtype=np.float32) / np.float32(half))).astype(np.float32)
    grid = np.where(i[:, None] < 64, (pos // 64)[None, :], (pos % 64)[None, :]).astype(np.float32)
    ang = grid * inv[i % 32][:, None]
    put(d, CONST2, "cos", np.cos(ang))
    put(d, CONST2, "sin", np.sin(ang))
    put(d, CONST2, "rot", rotation(32))
    t = np.arange(S)
    counts = [1.0 / (np.clip(t + w - w // 2, 0, S) - np.clip(t - w // 2, 0, S)) for w in (2, 4, 8, 16)]
    put(d, CONST2, "inv_count", np.concatenate(counts)[None, :])
    return c.astype(np.float32), d.astype(np.float32)


def tile_columns(w, k_tiles, col):
    return [w[k * P:(k + 1) * P, col:col + P] for k in range(k_tiles)]


def wide_columns(w, k_tiles, cols, width=2):
    return [w[k * P:(k + 1) * P, c + P * i:c + P * (i + 1)]
            for c in range(0, cols, width * P) for k in range(k_tiles) for i in range(width)]


def modulation_atoms(a, n):
    layer, n = divmod(n, 6 * D // 256)
    return wide_columns(a["ada_w_2"][layer][:, n * 256:(n + 1) * 256], KT, 256)


def layer_atoms(a, lay):
    w_in = a["w_in"][lay]
    o_cq, o_ckv, o_fq = 1024, 1408, 1696
    o_fk, o_fv, o_fl, o_g = o_fq + 512, o_fq + 1024, o_fq + 1536, o_fq + 1544
    w_kr = np.tile(w_in[:, o_ckv + 256:o_fq], (1, 4))
    w_fl = np.zeros((D, P), np.float32)
    for base in (0, 32, 64, 96):
        w_fl[:, base:base + 8] = w_in[:, o_fl:o_g]
    wuq = a["mla_wuq"][lay].reshape(384, HEADS, 96)
    wukv = a["mla_wukv"][lay].reshape(256, HEADS, 128)
    w_qn = wuq[:, :, :64].reshape(384, 512)
    w_qr = wuq[:, [0, 2, 1, 3, 4, 6, 5, 7], 64:].reshape(384, 256)
    w_kn = wukv[:, :, :64].reshape(256, 512)
    w_vm = wukv[:, :, 64:].reshape(256, 512)

    def pair_diagonal(w, j):
        d = np.zeros((P, P), np.float32)
        d[:64, :64] = w[2 * j]
        d[64:, 64:] = w[2 * j + 1]
        return [d]

    out = []
    for t in TILES:
        if t in SHARED or t[0] == "turn":
            continue
        kind, j = t[0], t[-1]
        if kind == "ada":
            out += modulation_atoms(a, lay * LAYER_ADA + j)
        if kind in ("u", "gl", "cq", "ckv", "fq", "fk"):
            base = {"u": 0, "gl": 512, "cq": o_cq, "ckv": o_ckv, "fq": o_fq, "fk": o_fk}[kind]
            out += tile_columns(w_in, KT, base + j * P)
        elif kind == "kr":
            out += tile_columns(w_kr, KT, 0)
        elif kind == "fl":
            out += tile_columns(w_fl, KT, 0)
        elif kind == "wa":
            out += pair_diagonal(a["lru_wa"][lay], j)
        elif kind == "wx":
            out += pair_diagonal(a["lru_wx"][lay], j)
        elif kind == "fv":
            out += wide_columns(w_in[:, o_fv:o_fv + 512], KT, 512)
        elif kind == "vm":
            out += wide_columns(w_vm, KV_LORA_T, 512)
        elif kind == "kn":
            out += tile_columns(w_kn, KV_LORA_T, j * P)
        elif kind == "qn":
            out += tile_columns(w_qn, Q_LORA_T, j * P)
        elif kind == "qr":
            out += tile_columns(w_qr, Q_LORA_T, j * P)
        elif kind == "g":
            out += tile_columns(w_in, KT, o_g + t[1] * D + j * P)
        elif kind == "y":
            out += tile_columns(a[("w_br_a", "w_br_b", "w_br_c")[t[1]]][lay], 4, j * P)
        elif kind == "wo":
            out += tile_columns(a["w_o"][lay], KT, j * P)
        elif kind == "hg":
            out += tile_columns(a["w_gate_up"][lay], KT, (t[1] * HALF_T + j) * P)
        elif kind == "hu":
            out += tile_columns(a["w_gate_up"][lay], KT, D_FF + (t[1] * HALF_T + j) * P)
        elif kind == "dn":
            out += tile_columns(a["w_down"][lay][t[1] * HALF_T * P:], HALF_T, j * P)
        elif kind == "pg":
            out += tile_columns(a["w_ple_gate"][lay], KT, j * P)
        elif kind == "pp":
            out += tile_columns(a["w_ple"][lay], PLE_T, j * P)
    assert len(out) == LAYER_ATOMS
    return out


def second_atoms(a):
    out = []
    qkv = a["attn_w_qkv_2"][0]
    for t in TILES2:
        kind, j = t[0], t[-1]
        if kind == "ada":
            out += modulation_atoms(a, j)
        elif kind == "pool":
            out += tile_columns(a["pool_w_2"][0, j // 2], 2, j % 2 * P)
        elif kind == "w1":
            out += tile_columns(a["mlp_w1_2"][t[1]], KT, (t[2] * QT + j) * P)
        elif kind == "w2":
            out += tile_columns(a["mlp_w2_2"][t[1]][t[2] * QT * P:], QT, j * P)
        elif kind == "q":
            out += tile_columns(qkv, KT, j * P)
        elif kind == "k":
            out += tile_columns(qkv, KT, D + j * P)
        elif kind == "v" and j == 0:
            out += wide_columns(qkv[:, D + D // 2:], KT, D // 2)
        elif kind == "o":
            out += tile_columns(a["attn_w_o_2"][0], KT, j * P)
    assert len(out) == B2_ATOMS
    return out


def pack_stream(a):
    stream = np.zeros((N_CHUNKS, P, CHUNK_ATOMS, P), np.float32)
    first = 0
    for atoms, chunks in [(layer_atoms(a, l), LAYER_CHUNKS) for l in range(DEPTH)] + [(second_atoms(a), B2_CHUNKS)]:
        for n, atom in enumerate(atoms):
            stream[first + n // CHUNK_ATOMS, :, n % CHUNK_ATOMS] = atom
        first += chunks
    return stream.reshape(N_CHUNKS, P, CH)


def columns(v):
    return np.ascontiguousarray(np.asarray(v).reshape(-1, P).T)


def pack_parameters(a):
    par = np.zeros((P, DEPTH, NPAR), np.float32)
    for l in range(DEPTH):
        def put(name, v):
            c = columns(v)
            par[:, l, PAR[name]:PAR[name] + c.shape[1]] = c
        for name, src in (("mix_g", "mix_norm"), ("gate_b", "gate_b"), ("conv_w", "conv_w"), ("conv_b", "conv_b"),
                          ("ba", "lru_ba"), ("bx", "lru_bx"), ("lam", "lru_lambda"), ("q_g", "mla_q_norm"),
                          ("kv_g", "mla_kv_norm"), ("ffn_g", "ffn_norm"), ("ple_g", "ple_norm")):
            put(name, a[src][l])
        for base in (0, 32, 64, 96):
            par[base:base + 8, l, PAR["bf"]] = a["fox_bf"][l]
    par2 = np.zeros((P, NPAR2), np.float32)

    def put2(name, v, at=0):
        c = columns(v)
        par2[:, PAR2[name] + at:PAR2[name] + at + c.shape[1]] = c
    cc = np.stack([columns(a["c_ctx_2"]), columns(a["c_2"])], 2).reshape(P, 16)
    par2[:, PAR2["cc"]:PAR2["cc"] + 16] = cc
    put2("ada_b", a["ada_b_2"])
    put2("norm_g", a["norm_g_2"])
    put2("pool_scale", a["pool_scale_2"])
    put2("q_g", a["attn_q_g_2"])
    put2("k_g", a["attn_k_g_2"])
    put2("final_g", a["final_g_2"])
    put2("first_g", a["final_norm"])
    return par.reshape(P, DEPTH * NPAR), par2


def token_minor(x):
    t, f = x.shape
    return np.ascontiguousarray(x.T.reshape(f // P, P, t).transpose(1, 0, 2).reshape(P, (f // P) * t))


NORM_FIRST = {"mix": 0, "q": 8, "kv": 11, "ffn": 13, "ple": 21}
NORM_TILES = 29
NORM_NO = {"mix": 0, "q": 1, "kv": 2, "ffn": 3, "ple": 4}
N_NORMS = 5
UNITS = 32
PAIRS = 8
FREE_BANKS = N_BANKS
FREE_SLOTS = 3


def build(nc, ins, out):
    stream, x_in, ctx_in, p_in, par_in, par2_in, const_in, const2_in = ins
    ctx = ExitStack()
    with ctx:
        def sem(name):
            return ctx.enter_context(nc.semaphore(name))

        raw = [ctx.enter_context(nc.sbuf_tensor(f"raw{i}", [P, CH], F32)) for i in range(RING)]
        whi = [ctx.enter_context(nc.sbuf_tensor(f"whi{i}", [P, CH], F32R)) for i in range(RING)]
        wlo = [ctx.enter_context(nc.sbuf_tensor(f"wlo{i}", [P, CH], F32R)) for i in range(RING)]
        AR = ctx.enter_context(nc.sbuf_tensor("split_acts", [P, 16384], F32R))
        NAF = 21464
        AF = ctx.enter_context(nc.sbuf_tensor("acts", [P, NAF], F32))
        bank = [ctx.enter_context(nc.psum_tensor(f"bank{i}", [P, 512], F32)) for i in range(8)]
        o_bank, s_bank, t_bank = bank[4], [bank[5], bank[6]], bank[7]

        top = [NAF]
        low = [0]

        def keep(n):
            top[0] -= n
            return AF[:, top[0]:top[0] + n]

        def take(n):
            low[0] += n
            assert low[0] <= top[0], (low[0], top[0])
            return AF[:, low[0] - n:low[0]]

        const = keep(NCONST)
        par = keep(DEPTH * NPAR)
        par2 = keep(NPAR2)
        stat = keep(24)
        mod = keep(2 * DEPTH * MOD_T)

        def C(name):
            at, w = CONST[name]
            return const[:, at:at + w]

        ident, ones = C("ident"), C("ones")
        eps_col = stat[:, 0:1]
        nmax = [stat[:, 2:3], stat[:, 3:4]]
        rsum = [stat[:, 4:5], stat[:, 5:6]]
        rinv = stat[:, 6:7]

        x = take(2048)
        rstd_x = take(256)
        rstd_q = take(256)
        rstd_kv = take(256)
        rcol = take(4)
        ugl = take(2060)
        u_pad = ugl[:, 0:1036]
        sq_lru = ugl[:, 0:1024]
        gl = ugl[:, 1036:2060]
        merged = ugl[:, 0:2048]
        lru = take(3584)
        xc, tr, ti, rec = lru[:, 0:1024], lru[:, 1024:2048], lru[:, 2048:3072], lru[:, 3072:3584]
        sqx = lru[:, 0:2048]
        krm = take(512)
        qn, kn, qr, vm = take(1024), take(1024), take(512), take(1024)
        fqk = take(2048)
        fq, fk = fqk[:, 0:1024], fqk[:, 1024:2048]
        c_raw, c_sq = fqk[:, 0:1280], fqk[:, 1280:2048]
        p_raw = fqk[:, 0:512]
        vf = take(1024)
        rk, lq, lh = take(256), take(256), take(512)
        att = take(2048 - 256)
        lg, pr, pt, o32 = att[:, 0:512], att[:, 512:1024], att[:, 1024:1536], att[:, 1536:1792]
        krz = lg[:, 0:256]
        th, hid, ut = att[:, 0:512], att[:, 512:1024], att[:, 1024:1280]
        gt = take(512)
        yt = take(256)
        cur = take(NPAR)
        hgb = take(24)
        m2sp = take(4)
        small = take(24)
        f_z, f_ab, f_den, f_s = (ti[:, i * 256:(i + 1) * 256] for i in range(4))
        f_s2, f_p = rec[:, 0:256], rec[:, 256:512]

        def Cp(name, j=0):
            return cur[:, PAR[name] + j:PAR[name] + j + 1]

        xa_hi, xa_lo = AR[:, 0:2048], AR[:, 2048:4096]
        xb_hi, xb_lo = AR[:, 4096:6144], AR[:, 6144:8192]
        lru_hi, lru_lo = AR[:, 8192:9216], AR[:, 9216:10240]
        cn_hi, cn_lo = AR[:, 10240:11520], AR[:, 11520:12800]
        mo_hi, mo_lo = AR[:, 10240:11264], AR[:, 11264:12288]
        xc_hi, xc_lo = AR[:, 12800:13824], AR[:, 13824:14848]
        fo_hi, fo_lo = AR[:, 12800:13824], AR[:, 13824:14848]
        h_hi, h_lo = AR[:, 8192:8192 + HALF_T * 256], AR[:, 8192 + HALF_T * 256:8192 + 2 * HALF_T * 256]
        p_hi, p_lo = AR[:, 13824:14336], AR[:, 14336:14848]
        silu_c = AR[:, 14848:15872]
        rows = att[:, 1280:1792]
        turned = small[:, 0:16]
        svec = att[:, 0:32]
        branch_in = [(lru_hi, lru_lo), (mo_hi, mo_lo), (fo_hi, fo_lo)]

        def tile(a, t, n=256):
            return a[:, t * n:(t + 1) * n]

        low[0] = 2048
        h = take(4096)
        sq2 = take(4096)
        q2, k2 = sq2[:, 0:2048], sq2[:, 2048:4096]
        v2 = take(2048)
        pr2, pt2 = take(1024), take(1024)
        low[0] -= 2048
        rows2 = v2[:, 0:512]
        padded, sum_a, sum_b = take(1088), take(544), take(544)
        hsq = pr2
        tmp, squares, rstd2 = take(1024), take(1024), take(512)
        probs2 = (pr2[:, 0:512], pr2[:, 512:1024], tmp[:, 0:512])
        m32, var2 = squares[:, 0:512], squares[:, 512:1024]
        o32b = take(256)
        const2 = take(NCONST2)
        gain, pool_gate, turned2 = take(64), take(16), take(16)
        qcol, qrstd, qneg, peak = take(16), take(16), take(16), take(16)
        qg_scaled = take(1)
        m_hi, m_lo = AR[:, 0:4096], AR[:, 4096:8192]
        hid_hi, hid_lo = AR[:, 8192:12288], AR[:, 12288:16384]
        oh_hi, oh_lo = AR[:, 8192:10240], AR[:, 12288:14336]

        def C2(name):
            at, w = CONST2[name]
            return const2[:, at:at + w]

        def mod_col(l, part, t, s):
            i = (l * MOD_T + part * KT + t) * 2 + s
            return mod[:, i:i + 1]

        def gain_col(l, i, t, s):
            c = ((l * 2 + i) * KT + t) * 2 + s
            return gain[:, c:c + 1]

        o_banks2 = (o_bank, bank[(FIRST_TILE2 + TILE_NO2[("o", 3)]) % N_BANKS])

        def sides(l, i):
            return (1,) if (l, i) == (1, 1) else (0, 1)

        def side(a, t, s):
            return a[:, t * 512 + s * 256:t * 512 + (s + 1) * 256]

        raw_in = [sem(f"raw_in{i}") for i in range(RING)]
        hi_ready = sem("hi_ready")
        lo_ready = sem("lo_ready")
        slots_used = sem("slots_used")
        gemm_done = sem("gemm_done")
        tiles_out = sem("tiles_out")
        start_in, x_in_done, const_in_done = sem("start_in"), sem("x_in_done"), sem("const_in_done")
        x_ready = sem("x_ready")
        par_ready = sem("par_ready")
        nhi_ready = sem("nhi_ready")
        sum_ready = sem("sum_ready")
        nlo_ready = sem("nlo_ready")
        sd_ready = sem("sd_ready")
        rstd_ready = sem("rstd_ready")
        lam_abs, lam_exp, m2sp_ready = sem("lam_abs"), sem("lam_exp"), sem("m2sp_ready")
        xc_begun, xc_done = sem("xc_begun"), sem("xc_done")
        gl_sq, gl_inner, gl_tanh = sem("gl_sq"), sem("gl_inner"), sem("gl_tanh")
        xchi_ready, xclo_ready = sem("xchi_ready"), sem("xclo_ready")
        lru_act = sem("lru_act")
        lru_done, lruhi_ready, lrulo_ready = sem("lru_done"), sem("lruhi_ready"), sem("lrulo_ready")
        mla_ready = sem("mla_ready")
        fl_abs, fl_exp, decay_ready, lh_ready = sem("fl_abs"), sem("fl_exp"), sem("decay_ready"), sem("lh_ready")
        s_done, lg_done, exp_done = sem("s_done"), sem("lg_done"), sem("exp_done")
        p_done, t_done, pt_done, pv_done = sem("p_done"), sem("t_done"), sem("pt_done"), sem("pv_done")
        o_out, ohi_ready, olo_ready = sem("o_out"), sem("ohi_ready"), sem("olo_ready")
        gate_tanh = sem("gate_tanh")
        merged_ready, mhi_ready, mlo_ready = sem("merged_ready"), sem("mhi_ready"), sem("mlo_ready")
        hid_ready, hhi_ready, hlo_ready = sem("hid_ready"), sem("hhi_ready"), sem("hlo_ready")
        ple_in, phi_ready, plo_ready = sem("ple_in"), sem("phi_ready"), sem("plo_ready")
        late_in = sem("late_in")
        h_ready = sem("h_ready")
        sq2_ready = sem("sq2_ready")
        sum2_ready = sem("sum2_ready")
        sd2_ready = sem("sd2_ready")
        silu_act, silu_ready = sem("silu_act"), sem("silu_ready")
        scaled2, m_act, m_split = sem("scaled2"), sem("m_act"), sem("m_split")
        pooled, pooled_hi = sem("pooled"), sem("pooled_hi")
        act2_hi, act2_lo = sem("act2_hi"), sem("act2_lo")
        qcol_done, qms_ready, qsd_ready = sem("qcol_done"), sem("qms_ready"), sem("qsd_ready")
        hsq_ready, hsd_ready, hn_ready = sem("hsq_ready"), sem("hsd_ready"), sem("hn_ready")
        qkv_ready = sem("qkv_ready")
        s2_done, max2_done, exp2_done, p2_done = sem("s2_done"), sem("max2_done"), sem("exp2_done"), sem("p2_done")
        t2_done, pt2_done, pv2_done = sem("t2_done"), sem("pt2_done"), sem("pv2_done")
        o2_out, o2_hi, o2_lo = sem("o2_out"), sem("o2_hi"), sem("o2_lo")
        result_ready = sem("result_ready")
        out_done = sem("out_done")
        N_GATES = 24 + FF_T + 8

        def gate_no(t):
            if t[0] == "g":
                return t[1] * 8 + t[2]
            return 24 + t[1] * HALF_T + t[2] if t[0] == "hg" else 24 + FF_T + t[1]

        block = ctx.enter_context(nc.Block())

        @block.sync
        def _(sp):
            def fetch(slot, index):
                sp.dma_start(raw[slot][:, :], stream[index]).then_inc(raw_in[slot], 16)

            sp.dma_start(par2[:, :], par2_in).then_inc(start_in, 16)
            sp.dma_start(par[:, :], par_in).then_inc(start_in, 16)
            fetch(0, 0)
            sp.dma_start(x[:, :], x_in).then_inc(x_in_done, 16)
            fetch(1, 1)
            sp.dma_start(const[:, :], const_in).then_inc(const_in_done, 16)
            for slot in range(2, RING):
                fetch(slot, slot)
            with sp.Fori(1, N_CHUNKS // RING) as r:
                for slot in range(RING):
                    sp.wait_ge(lo_ready, r * RING + (slot - RING + 1))
                    sp.dma_start(raw[slot][:, :], stream[bass.ds(r * RING + slot, 1)].rearrange("a p n -> (a p) n"))\
                        .then_inc(raw_in[slot], 16)
            for t in range(KT):
                sp.wait_ge(result_ready, t + 1)
                sp.dma_start(out[:, t * 256:(t + 1) * 256], tile(sq2, t)).then_inc(out_done, 16)
            sp.wait_ge(out_done, 16 * KT)

        @block.gpsimd
        def _(pool):
            def lo_parts(slot, chunk):
                pool.wait_ge(hi_ready, chunk + 1)
                nc.gpsimd.tensor_tensor(wlo[slot][:, :], raw[slot][:, :], whi[slot][:, :].bitcast(F32),
                                        ALU.subtract).then_inc(lo_ready, 1)

            used = DEPTH * LAYER_CHUNKS + -(-B2_ATOMS // CHUNK_ATOMS)
            with pool.Fori(0, used // RING) as r:
                for slot in range(RING):
                    lo_parts(slot, r * RING + slot)
            for slot in range(used % RING):
                lo_parts(slot, used - used % RING + slot)

        @block.tensor
        def _(pe):
            class Cursor:
                atom = 0

            def weights(lay, base, n):
                chunk, at = divmod(Cursor.atom, CHUNK_ATOMS)
                opens = at == 0
                assert at + n <= CHUNK_ATOMS
                if opens:
                    pe.wait_ge(lo_ready, base(lay, chunk) + 1)
                Cursor.atom += n
                cols = slice(at * P, (at + n) * P)
                return whi[chunk % RING][:, cols], wlo[chunk % RING][:, cols], opens

            def product(out_ap, hi_act, lo_act, k_tiles, lay, base, wait_k=None):
                for k in range(k_tiles):
                    w_hi, w_lo, opens = weights(lay, base, 1)
                    if wait_k is not None:
                        wait_k(k)
                    first = nc.tensor.matmul(out_ap, w_hi, hi_act(k), start=(k == 0), stop=False)
                    if opens:
                        first.then_inc(slots_used, 1)
                    nc.tensor.matmul(out_ap, w_hi, lo_act(k), start=False, stop=False)
                    last = nc.tensor.matmul(out_ap, w_lo, hi_act(k), start=False, stop=(k == k_tiles - 1))
                return last

            def modulation(b, lay, base):
                for k in range(KT):
                    w_hi, w_lo, opens = weights(lay, base, 2)
                    s4 = silu_c[:, k * P:(k + 1) * P]
                    first = nc.tensor.matmul(b[:, 0:256], s4, w_hi, start=(k == 0), stop=False)
                    if opens:
                        first.then_inc(slots_used, 1)
                    last = nc.tensor.matmul(b[:, 0:256], s4, w_lo, start=False, stop=(k == KT - 1))
                return last

            def turn_rows(b, rows):
                for i in range(4):
                    last = nc.tensor.matmul(b[:, 4 * i:4 * i + 4], rows[0:4, i * P:(i + 1) * P], ident[0:4, 0:4],
                                            start=True, stop=True)
                return last

            nc.tensor.sem_inc(slots_used, FREE_SLOTS)
            nc.tensor.sem_inc(pv_done, 2)
            pe.wait_ge(silu_ready, 1)

            with pe.Fori(0, DEPTH) as lay:
                Cursor.atom = 0

                def base(lay, chunk):
                    return lay * LAYER_CHUNKS + chunk

                def open_bank(t):
                    n = TILE_NO[t]
                    pe.wait_ge(tiles_out, lay * TILES_PER_LAYER + n + 1)
                    return bank[n % N_BANKS]

                def out_of_bank(t, extra=0):
                    pe.wait_ge(tiles_out, lay * TILES_PER_LAYER + (FREE_BANKS + TILE_NO[t] + 1))

                def normed(name, hi, lo, n):
                    first = NORM_FIRST[name]
                    return (lambda k: tile(hi, k), lambda k: tile(lo, k),
                            lambda k: pe.wait_ge(nlo_ready, lay * NORM_TILES + (first + k + 1)))

                act_of = {
                    "u": (xa_hi, xa_lo, 8), "gl": (xa_hi, xa_lo, 8), "cq": (xa_hi, xa_lo, 8),
                    "ckv": (xa_hi, xa_lo, 8), "kr": (xa_hi, xa_lo, 8), "fl": (xa_hi, xa_lo, 8),
                    "fq": (xa_hi, xa_lo, 8), "fk": (xa_hi, xa_lo, 8), "g": (xa_hi, xa_lo, 8),
                    "qn": (cn_hi, cn_lo, 3), "qr": (cn_hi, cn_lo, 3),
                    "kn": (cn_hi[:, 768:], cn_lo[:, 768:], 2),
                    "wo": (xb_hi, xb_lo, 8), "hg": (xa_hi, xa_lo, 8), "hu": (xa_hi, xa_lo, 8),
                    "dn": (h_hi, h_lo, HALF_T), "pg": (xb_hi, xb_lo, 8), "pp": (p_hi, p_lo, 2),
                }

                def gemm(t):
                    kind, j = t[0], t[-1]
                    if t in SHARED:
                        return
                    b = open_bank(t)
                    if kind == "ada":
                        modulation(b, lay, base).then_inc(gemm_done, 1)
                        return
                    if kind == "turn":
                        out_of_bank(("ada", 2 * j + 1))
                        turn_rows(b, rows).then_inc(gemm_done, 1)
                        return
                    if kind == "ss":
                        pe.wait_ge(const_in_done, 16)
                        pe.wait_ge(sum_ready, lay * N_NORMS + (NORM_NO[j] + 1))
                        src = tile({"q": c_sq, "kv": rec}.get(j, sqx), 0)
                        last = nc.tensor.matmul(b[:, 0:256], ones[:, 0:128], src, start=True, stop=True)
                    elif kind == "col":
                        pe.wait_ge(rstd_ready, lay * N_NORMS + (NORM_NO[j] + 1))
                        row = rstd_x if j == "mix" else rstd_kv
                        for m in range(2):
                            last = nc.tensor.matmul(b[:, m:m + 1], row[0:1, m * P:(m + 1) * P], ones[0:1, 0:1],
                                                    start=True, stop=True)
                    elif kind in ("wa", "wx"):
                        pe.wait_ge(xclo_ready, lay * 1 + 1)
                        last = product(b[:, 0:256], lambda k: tile(xc_hi, j), lambda k: tile(xc_lo, j), 1, lay, base)
                    elif kind in ("rotk", "rotq"):
                        out_of_bank(("kr", 0) if kind == "rotk" else ("qr", j))
                        src = krz if kind == "rotk" else tile(qr, j)
                        last = nc.tensor.matmul(b[:, 0:256], C("rot"), src, start=True, stop=True)
                    elif kind in ("fv", "vm"):
                        b2 = open_bank((kind, 1))
                        hi, lo, kts = (xa_hi, xa_lo, 8) if kind == "fv" else (cn_hi[:, 768:], cn_lo[:, 768:], 2)
                        for half in range(2):
                            for k in range(kts):
                                w_hi, w_lo, opens = weights(lay, base, 2)
                                for m, bm in enumerate((b, b2)):
                                    o = bm[:, half * 256:half * 256 + 256]
                                    tok_hi = hi[:, k * 256 + m * P:k * 256 + (m + 1) * P]
                                    tok_lo = lo[:, k * 256 + m * P:k * 256 + (m + 1) * P]
                                    one = nc.tensor.matmul(o, tok_hi, w_hi, start=(k == 0), stop=False)
                                    if opens and m == 0:
                                        one.then_inc(slots_used, 1)
                                    nc.tensor.matmul(o, tok_hi, w_lo, start=False, stop=False)
                                    last = nc.tensor.matmul(o, tok_lo, w_hi, start=False, stop=(k == kts - 1))
                        last.then_inc(gemm_done, 2)
                        return
                    else:
                        if kind == "y":
                            hi, lo = branch_in[t[1]]
                            n = 4
                            if j == 0:
                                if t[1] == 0:
                                    pe.wait_ge(lrulo_ready, lay * 4 + 4)
                                else:
                                    pe.wait_ge(olo_ready, lay * PAIRS + 4 * t[1])
                        else:
                            hi, lo, n = act_of[kind]
                        wait_k = None
                        if t == ("u", 0):
                            wait_k = normed("mix", hi, lo, n)[2]
                        elif t == ("kn", 0):
                            pe.wait_ge(nlo_ready, lay * NORM_TILES + NORM_FIRST["ffn"])
                        elif t == ("wo", 0):
                            wait_k = lambda k: pe.wait_ge(mlo_ready, lay * 8 + (k + 1))
                        elif t == ("hg", 0, 0):
                            wait_k = normed("ffn", hi, lo, n)[2]
                        elif kind == "dn" and j == 0:
                            wait_k = lambda k: pe.wait_ge(hlo_ready, lay * FF_T + (t[1] * HALF_T + k + 1))
                        elif t == ("pg", 0):
                            wait_k = normed("ple", hi, lo, n)[2]
                        elif t == ("pp", 0):
                            pe.wait_ge(plo_ready, lay + 1)
                        last = product(b[:, 0:256], lambda k: tile(hi, k), lambda k: tile(lo, k), n, lay, base, wait_k)
                    last.then_inc(gemm_done, 1)

                def scores(kind, u):
                    U = (0 if kind == "mla" else 16) + u
                    h, qb = u // 2, u % 2
                    r, nk = 64 * (h % 2), P * (qb + 1)
                    rows, q_cols = slice(r, r + 64), slice(qb * P, (qb + 1) * P)
                    pe.wait_ge(lg_done, lay * UNITS + U + 1)
                    o = s_bank[u % 2][:, 0:nk]
                    if kind == "mla":
                        if u == 0:
                            pe.wait_ge(mla_ready, lay + 1)
                        nc.tensor.matmul(o, tile(qn, h // 2)[rows, q_cols], tile(kn, h // 2)[rows, 0:nk],
                                         start=True, stop=False)
                        last = nc.tensor.matmul(o, tile(qr, h // 4)[rows, q_cols],
                                                tile(krm, (h // 2) % 2)[rows, 0:nk], start=False, stop=True)
                    else:
                        if u == 0:
                            out_of_bank(("fk", 3))
                            pe.wait_ge(decay_ready, lay + 1)
                        if qb == 0:
                            pe.wait_ge(lh_ready, lay * HEADS + h + 1)
                        nc.tensor.matmul(o, tile(fq, h // 2)[rows, q_cols], tile(fk, h // 2)[rows, 0:nk],
                                         start=True, stop=False)
                        last = nc.tensor.matmul(o, tile(lh, h % 2)[rows, q_cols], rk[rows, 0:nk],
                                                start=False, stop=True)
                    last.then_inc(s_done, 1)

                def turn(kind, u):
                    U = (0 if kind == "mla" else 16) + u
                    pe.wait_ge(p_done, lay * UNITS + U + 1)
                    pe.wait_ge(pt_done, lay * UNITS + U + 1)
                    for kb in range(u % 2 + 1):
                        last = nc.tensor.transpose(t_bank[:, kb * P:(kb + 1) * P],
                                                   tile(pr, u % 2)[:, kb * P:(kb + 1) * P], ident)
                    last.then_inc(t_done, 1)

                def values(kind, u):
                    U = (0 if kind == "mla" else 16) + u
                    h, qb = u // 2, u % 2
                    pair = U // 4
                    if u % 4 == 0:
                        pe.wait_ge(o_out, lay * PAIRS + pair + 1)
                    pe.wait_ge(pt_done, lay * UNITS + U + 2)
                    v = vm if kind == "mla" else vf
                    r = 64 * (h % 2)
                    cols = (pair % 2) * 256 + qb * P
                    for kb in range(qb + 1):
                        last = nc.tensor.matmul(o_bank[r:r + 64, cols:cols + P],
                                                v[:, kb * 512 + h * 64:kb * 512 + (h + 1) * 64],
                                                tile(pt, u % 2)[:, kb * P:(kb + 1) * P],
                                                start=(kb == 0), stop=(kb == qb))
                    last.then_inc(pv_done, 1)

                for t in HEAD_TILES:
                    gemm(t)
                for kind, fill in (("mla", MLA_FILL), ("fox", FOX_FILL)):
                    for i in range(17):
                        if i:
                            turn(kind, i - 1)
                        if i < 16:
                            scores(kind, i)
                            gemm(fill[i])
                        if i:
                            values(kind, i - 1)
                for t in MID_TILES + TAIL_TILES:
                    gemm(t)
                Cursor.atom = -(-LAYER_ATOMS // CHUNK_ATOMS) * CHUNK_ATOMS
                while Cursor.atom < LAYER_CHUNKS * CHUNK_ATOMS:
                    w_hi, w_lo, _ = weights(lay, base, CHUNK_ATOMS)
                    nc.tensor.matmul(t_bank[:, 0:256], w_hi[:, 0:P], tile(xb_hi, 0), start=True, stop=True)\
                        .then_inc(slots_used, 1)

            Cursor.atom = 0

            def base2(lay, chunk):
                return FIRST_CHUNK2 + chunk

            def open2(t):
                n = FIRST_TILE2 + TILE_NO2[t]
                pe.wait_ge(tiles_out, n + 1)
                return bank[n % N_BANKS]

            norms = 0

            def gemm2(t):
                nonlocal norms
                kind = t[0]
                if kind == "v" and t[1]:
                    return
                b = open2(t)
                if kind == "ss":
                    wide = t[1:] in ((0, 0), (0, 1), (1, 0))
                    o = b[:, 0:512] if wide else b[:, 0:256]
                    norms += 1
                    pe.wait_ge(sum2_ready, norms)
                    src = sq2[:, 0:512] if wide else sq2[:, 256:512]
                    last = nc.tensor.matmul(o, ones[:, 0:128], src, start=True, stop=True)
                elif kind == "ada":
                    last = modulation(b, 0, base2)
                elif kind == "turn":
                    pe.wait_ge(tiles_out, FIRST_TILE2 + FREE_BANKS + TILE_NO2[("ada", 2 * t[1] + 1)] + 1)
                    last = turn_rows(b, rows2)
                elif kind == "pool":
                    if t[1] % 2 == 0:
                        pe.wait_ge(m_split, t[1] + 2)
                    g = t[1] // 2
                    last = product(b[:, 0:512], lambda k: tile(m_hi, 2 * g + k, 512),
                                   lambda k: tile(m_lo, 2 * g + k, 512), 2, 0, base2)
                elif kind in ("w1", "w2"):
                    l = t[1]
                    first_split = {0: 8, 1: 24}[l]

                    def part(a):
                        return (lambda k: tile(a, k, 512)) if l == 0 else (lambda k: side(a, k, 1))

                    o = b[:, 0:512] if l == 0 else b[:, 0:256]
                    if kind == "w1":
                        wait_k = (lambda k: pe.wait_ge(m_split, first_split + k + 1)) if t[2:] == (0, 0) else None
                        last = product(o, part(m_hi), part(m_lo), KT, 0, base2, wait_k)
                    else:
                        done = (l * QUARTERS + t[2]) * QT
                        wait_k = (lambda k: pe.wait_ge(act2_lo, done + k + 1)) if t[3] == 0 else None
                        last = product(o, part(hid_hi), part(hid_lo), QT, 0, base2, wait_k)
                elif kind == "q":
                    wait_k = (lambda k: pe.wait_ge(m_split, 16 + k + 1)) if t[1] == 0 else None
                    last = product(b[:, 0:256], lambda k: side(m_hi, k, 1), lambda k: side(m_lo, k, 1), KT, 0, base2,
                                   wait_k)
                elif kind == "k":
                    last = product(b[:, 0:512], lambda k: tile(m_hi, k, 512), lambda k: tile(m_lo, k, 512), KT, 0,
                                   base2)
                elif kind == "kss":
                    pe.wait_ge(hsq_ready, 8 + t[1] + 1)
                    last = nc.tensor.matmul(b[:, 0:512], ones[:, 0:128], tile(hsq, t[1] % 2, 512), start=True,
                                            stop=True)
                elif kind == "qrot":
                    pe.wait_ge(hsq_ready, t[1] + 1)
                    for qb in range(2):
                        c = 2 * t[1] + qb
                        col = nc.tensor.matmul(t_bank[:, c:c + 1], tile(hsq, t[1] % 2, 512)[:, qb * P:(qb + 1) * P],
                                               ones[:, 0:1], start=True, stop=True)
                    col.then_inc(qcol_done, 1)
                    pe.wait_ge(tiles_out, FIRST_TILE2 + FREE_BANKS + TILE_NO2[("q", t[1])] + 1)
                    last = nc.tensor.matmul(b[:, 0:256], C2("rot"), tile(q2, t[1]), start=True, stop=True)
                elif kind == "krot":
                    pe.wait_ge(hn_ready, t[1] + 1)
                    last = nc.tensor.matmul(b[:, 0:256], C2("rot"), side(k2, t[1], 1), start=True, stop=True)
                elif kind == "v":
                    banks = [b] + [open2(("v", m)) for m in range(1, 4)]
                    for half in range(2):
                        for k in range(KT):
                            w_hi, w_lo, opens = weights(0, base2, 2)
                            for m in range(4):
                                o = banks[m][:, half * 256:half * 256 + 256]
                                tok_hi = m_hi[:, k * 512 + m * P:k * 512 + (m + 1) * P]
                                tok_lo = m_lo[:, k * 512 + m * P:k * 512 + (m + 1) * P]
                                one = nc.tensor.matmul(o, tok_hi, w_hi, start=(k == 0), stop=False)
                                if opens and m == 0:
                                    one.then_inc(slots_used, 1)
                                nc.tensor.matmul(o, tok_hi, w_lo, start=False, stop=False)
                                last = nc.tensor.matmul(o, tok_lo, w_hi, start=False, stop=(k == KT - 1))
                    last.then_inc(gemm_done, 4)
                    return
                elif kind == "o":
                    wait_k = (lambda k: pe.wait_ge(o2_lo, k + 1)) if t[1] == 0 else None
                    last = product(b[:, 0:256], lambda k: tile(oh_hi, k), lambda k: tile(oh_lo, k), KT, 0, base2,
                                   wait_k)
                last.then_inc(gemm_done, 1)

            def scores2(u):
                h_, qb = u // 2, u % 2
                if u == 0:
                    pe.wait_ge(qkv_ready, 1)
                if u >= 2:
                    pe.wait_ge(exp2_done, u - 1)
                nc.tensor.matmul(s_bank[u % 2][:, :], tile(q2, h_)[:, qb * P:(qb + 1) * P],
                                 tile(k2, h_ // 2, 512), start=True, stop=True).then_inc(s2_done, 1)

            def turn2(u):
                pe.wait_ge(p2_done, u + 1)
                if u >= 1:
                    pe.wait_ge(pt2_done, u)
                for kb in range(4):
                    last = nc.tensor.transpose(t_bank[:, kb * P:(kb + 1) * P],
                                               probs2[u % 3][:, kb * P:(kb + 1) * P], ident)
                last.then_inc(t2_done, 1)

            def values2(u):
                h_, qb = u // 2, u % 2
                if qb == 0 and h_ >= 2:
                    pe.wait_ge(o2_out, h_ - 1)
                pe.wait_ge(pt2_done, u + 1)
                o = o_banks2[h_ % 2][:, qb * P:(qb + 1) * P]
                for kb in range(4):
                    kv = h_ // 2
                    last = nc.tensor.matmul(o, v2[:, kb * 512 + kv * P:kb * 512 + (kv + 1) * P],
                                            tile(pt2, u % 2, 512)[:, kb * P:(kb + 1) * P], start=(kb == 0),
                                            stop=(kb == 3))
                last.then_inc(pv2_done, 1)

            for t in TILES2:
                if t == ("o", 0):
                    for i in range(19):
                        if i < 16:
                            scores2(i)
                        if 2 <= i < 18:
                            turn2(i - 2)
                        if i >= 3:
                            values2(i - 3)
                gemm2(t)

        @block.scalar
        def _(act):
            sc = nc.scalar

            class Split:
                chunk = 0

            def split(lay, base, chunk):
                g = base(lay, chunk)
                act.wait_ge(slots_used, g + 1)
                act.wait_ge(raw_in[chunk % RING], (base(lay, chunk - chunk % RING) // RING) * 16 + 16
                            if isinstance(g, int) else lay * (LAYER_CHUNKS // RING * 16) + (chunk // RING + 1) * 16)
                sc.activation(whi[chunk % RING][:, :], raw[chunk % RING][:, :], ACT.Copy).then_inc(hi_ready, 1)

            def ahead(lay, base, chunk):
                while Split.chunk <= chunk + AHEAD:
                    split(lay, base, Split.chunk)
                    Split.chunk += 1

            act.wait_ge(start_in, 32)
            sc.copy(stat[:, 8:9], par2[:, 0:1]).then_inc(pt_done, 1)
            sc.activation(svec[:, 0:16], par2[:, PAR2["cc"]:PAR2["cc"] + 16], ACT.Tanh, scale=0.5)\
                .then_inc(silu_act, 1)
            act.wait_ge(silu_act, 2)
            s4 = silu_c.rearrange("p (k n) -> p k n", n=P)
            sc.activation(s4[:, :, 0:2], svec[:, 16:32].rearrange("p (k s) -> p k s", s=2), ACT.Copy)\
                .then_inc(silu_act, 1)
            for chunk in range(AHEAD):
                split(0, lambda lay, c: c, chunk)

            act.wait_ge(x_in_done, 16)
            with act.Fori(0, DEPTH) as lay:
                Split.chunk = AHEAD

                def base(lay, chunk):
                    return lay * LAYER_CHUNKS + chunk

                def moved_out(t):
                    ahead(lay, base, last_chunk(ATOM_SPAN[t]))
                    act.wait_ge(tiles_out, lay * TILES_PER_LAYER + (FREE_BANKS + TILE_NO[t] + 1))

                def norm(name, src, sq, g, hi, ready):
                    first = NORM_FIRST[name]
                    for k in range({"mix": 8, "q": 3, "kv": 2, "ffn": 8, "ple": 8}[name]):
                        ready(k)
                        sc.activation(sq(k), src(k), ACT.Square)
                        sc.activation(hi(k), src(k), ACT.Copy, scale=Cp(g, k)).then_inc(nhi_ready, 1)
                        if name == "mix" and k in (2, 5):
                            keep_ahead(("ada", k // 3))

                def root(name):
                    moved_out(("ss", name))
                    sc.activation(yt, yt, ACT.Sqrt).then_inc(sd_ready, 1)

                def exp(kind, u):
                    U = (0 if kind == "mla" else 16) + u
                    act.wait_ge(lg_done, lay * UNITS + U + 3)
                    nk = P * (u % 2 + 1)
                    sc.activation(tile(pr, u % 2)[:, 0:nk], tile(lg, u % 2)[:, 0:nk], ACT.Exp, scale=-1.0,
                                  bias=nmax[u % 2], accum_out=rsum[u % 2]).then_inc(exp_done, 1)

                def move_turned(kind, u):
                    U = (0 if kind == "mla" else 16) + u
                    act.wait_ge(t_done, lay * UNITS + U + 1)
                    act.wait_ge(pv_done, lay * UNITS + U + 1)
                    nk = P * (u % 2 + 1)
                    sc.activation(tile(pt, u % 2)[:, 0:nk], t_bank[:, 0:nk], ACT.Copy).then_inc(pt_done, 1)

                def attended(kind, pair):
                    act.wait_ge(o_out, lay * PAIRS + pair + 3)
                    hi = mo_hi if kind == "mla" else fo_hi
                    sc.activation(tile(hi, pair % 4), o32, ACT.Copy).then_inc(ohi_ready, 1)

                def decay_mask(h):
                    sc.activation(tile(lh, h % 2), lq, ACT.Copy, scale=C("onehot")[:, h:h + 1]).then_inc(lh_ready, 1)

                def of_tile(t):
                    kind, j = t[0], t[-1]
                    if kind == "g":
                        moved_out(t)
                        g = tile(gt, j % 2)
                        sc.activation(g, g, ACT.Tanh, scale=0.5, bias=hgb[:, t[1] * 8 + j:t[1] * 8 + j + 1])\
                            .then_inc(gate_tanh, 1)
                    elif kind == "hg":
                        moved_out(t)
                        sc.activation(tile(th, j % 2), tile(gt, j % 2), ACT.Tanh, scale=0.5).then_inc(gate_tanh, 1)
                    elif kind == "hu":
                        act.wait_ge(hid_ready, lay * FF_T + (t[1] * HALF_T + j + 1))
                        sc.activation(tile(h_hi, j), tile(hid, j % 2), ACT.Copy).then_inc(hhi_ready, 1)
                    elif kind == "y" and t[1] == 2:
                        act.wait_ge(merged_ready, lay * 8 + j + 1)
                        sc.activation(tile(xb_hi, j), tile(merged, j), ACT.Copy, scale=0.5).then_inc(mhi_ready, 1)
                    elif kind == "pg":
                        moved_out(t)
                        sc.activation(tile(gt, j % 2), tile(gt, j % 2), ACT.Tanh, scale=0.5).then_inc(gate_tanh, 1)

                def keep_ahead(t):
                    ahead(lay, base, last_chunk(ATOM_SPAN[t]))

                act.wait_ge(par_ready, lay + 1)
                norm("mix", lambda k: tile(x, k), lambda k: tile(sqx, k), "mix_g", lambda k: tile(xa_hi, k),
                     lambda k: act.wait_ge(x_ready, lay * 8 + k + 1))
                act.wait_ge(lam_abs, lay + 1)
                sc.activation(small[:, 4:8], small[:, 0:4], ACT.Exp, scale=-1.0).then_inc(lam_exp, 1)
                root("mix")
                for j in range(4):
                    keep_ahead(("u", j))
                    moved_out(("u", j))
                    sc.activation(tile(xc, j), u_pad[:, j * 259:j * 259 + 256], ACT.Identity,
                                  scale=Cp("conv_w", j), bias=Cp("conv_b", j)).then_inc(xc_begun, 1)
                for j in range(4):
                    keep_ahead(("gl", j))
                    moved_out(("gl", j))
                    sc.activation(tile(tr, j), tile(gl, j), ACT.Square).then_inc(gl_sq, 1)
                act.wait_ge(xc_done, lay + 1)
                sc.activation(xc_hi, xc, ACT.Copy).then_inc(xchi_ready, 1)
                act.wait_ge(gl_inner, lay + 1)
                sc.activation(tr, tr, ACT.Tanh, scale=GELU_C).then_inc(gl_tanh, 1)
                for j in range(3):
                    keep_ahead(("cq", j))
                    moved_out(("cq", j))
                    sc.activation(tile(c_sq, j), tile(c_raw, j), ACT.Square)
                    sc.activation(tile(cn_hi, j), tile(c_raw, j), ACT.Copy, scale=Cp("q_g", j)).then_inc(nhi_ready, 1)
                for j in range(2):
                    keep_ahead(("ckv", j))
                    moved_out(("ckv", j))
                    sc.activation(tile(rec, j), tile(c_raw, 3 + j), ACT.Square)
                    sc.activation(tile(cn_hi, 3 + j), tile(c_raw, 3 + j), ACT.Copy, scale=Cp("kv_g", j))\
                        .then_inc(nhi_ready, 1)
                keep_ahead(("kr", 0))
                root("q")
                root("kv")
                keep_ahead(("wx", 3))
                moved_out(("wx", 3))
                act.wait_ge(m2sp_ready, lay + 1)
                sc.activation(tr, tr, ACT.Tanh).then_inc(lru_act, 1)
                sc.activation(ti, ti, ACT.Tanh).then_inc(lru_act, 1)
                sc.drain()
                for j in range(4):
                    sc.activation(tile(tr, j), tile(tr, j), ACT.Tanh, scale=m2sp[:, j:j + 1], bias=m2sp[:, j:j + 1])\
                        .then_inc(lru_act, 1)
                sc.drain()
                sc.activation(sq_lru, tr, ACT.Sqrt, scale=-1.0).then_inc(lru_act, 1)
                done = 0
                for t in HEAD_TILES[TILE_NO[("rotk", 0)]:]:
                    keep_ahead(t)
                    if t in (("kn", 0), ("qn", 0), ("qn", 3)):
                        act.wait_ge(lru_done, lay * 4 + done + 1)
                        sc.activation(tile(lru_hi, done), tile(xc, done), ACT.Copy).then_inc(lruhi_ready, 1)
                        done += 1
                for kind, fill in (("mla", MLA_FILL), ("fox", FOX_FILL)):
                    if kind == "fox":
                        act.wait_ge(const_in_done, 16)
                        decay_mask(0)
                    for i in range(17):
                        if i:
                            move_turned(kind, i - 1)
                        if i < 16:
                            exp(kind, i)
                            if kind == "fox" and i % 2 == 0 and i // 2 + 1 < HEADS:
                                decay_mask(i // 2 + 1)
                            if kind == "mla" and i == 2:
                                act.wait_ge(lru_done, lay * 4 + 4)
                                sc.activation(tile(lru_hi, 3), tile(xc, 3), ACT.Copy).then_inc(lruhi_ready, 1)
                            if kind == "mla" and i == 1:
                                act.wait_ge(fl_abs, lay + 1)
                                sc.activation(f_den, f_ab, ACT.Exp, scale=-1.0).then_inc(fl_exp, 1)
                            keep_ahead(fill[i])
                            of_tile(fill[i])
                        if i and i % 4 == 0:
                            attended(kind, (i - 1) // 4 + (0 if kind == "mla" else 4))
                act.wait_ge(pv_done, lay * UNITS + UNITS + 2)
                act.dma_start(p_raw, p_in[bass.ds(lay, 1)].rearrange("a p n -> (a p) n")).then_inc(ple_in, 16)
                for t in MID_TILES:
                    keep_ahead(t)
                    of_tile(t)
                norm("ffn", lambda k: tile(x, k), lambda k: tile(sqx, k), "ffn_g", lambda k: tile(xa_hi, k),
                     lambda k: moved_out(("wo", k)))
                root("ffn")
                for t in FF_TILES:
                    if t == ("hg", 1, 0):
                        act.wait_ge(ple_in, lay * 16 + 16)
                        sc.activation(p_hi, p_raw, ACT.Copy).then_inc(phi_ready, 1)
                    keep_ahead(t)
                    of_tile(t)
                norm("ple", lambda k: tile(x, k), lambda k: tile(sqx, k), "ple_g", lambda k: tile(xb_hi, k),
                     lambda k: moved_out(("dn", 1, k)))
                root("ple")
                for t in PLE_TILES:
                    keep_ahead(t)
                    of_tile(t)
                ahead(lay, base, LAYER_CHUNKS - 1)

            Split.chunk = AHEAD

            def base2(lay, chunk):
                return FIRST_CHUNK2 + chunk

            def ahead2(t, margin=0):
                ahead(0, base2, margin + min((ATOM_SPAN2[t][1] - 1) // CHUNK_ATOMS, -(-B2_ATOMS // CHUNK_ATOMS) - 1 - AHEAD))

            def moved_out2(t):
                ahead2(t)
                act.wait_ge(tiles_out, FIRST_TILE2 + FREE_BANKS + TILE_NO2[t] + 1)

            def root2(t):
                moved_out2(t)
                wide = t[1:] in ((0, 0), (0, 1), (1, 0))
                a = var2[:, 0:512] if wide else var2[:, 256:512]
                sc.activation(a, a, ACT.Sqrt).then_inc(sd2_ready, 1)

            def squares2(both, ready):
                for k in range(KT):
                    ready(k)
                    c = slice(k * 512, (k + 1) * 512) if both else slice(k * 512 + 256, (k + 1) * 512)
                    sc.activation(sq2[:, c], h[:, c], ACT.Square).then_inc(sq2_ready, 1)

            scaled_before = 0
            split_before = KT

            def modulate_tile(l, i, t, dst, full=False):
                act.wait_ge(scaled2, scaled_before + t + 1)
                if full:
                    if t >= 2:
                        act.wait_ge(m_split, split_before + t - 1)
                    sc.activation(side(squares, t % 2, 0), side(tmp, t % 2, 0), ACT.Identity,
                                  scale=gain_col(l, i, t, 0), bias=mod_col(l, SH1 if i == 0 else SH2, t, 0))
                for s in sides(l, i):
                    last = sc.activation(dst(t, s), side(tmp, t % 2, s), ACT.Identity, scale=gain_col(l, i, t, s),
                                         bias=mod_col(l, SH1 if i == 0 else SH2, t, s))
                last.then_inc(m_act, 1)

            def modulated(l, i):
                nonlocal scaled_before, split_before
                for t in range(KT):
                    modulate_tile(l, i, t, lambda t, s: side(m_hi, t, s), 0 in sides(l, i))
                scaled_before += KT
                split_before += KT

            def hidden2(l):
                for q in range(QUARTERS):
                    for j in range(QT):
                        moved_out2(("w1", l, q, j))
                        if l == 0:
                            sc.activation(tile(hid_hi, j, 512), tile(tmp, j % 2, 512), ACT.Square).then_inc(act2_hi, 1)
                        else:
                            sc.activation(side(hid_hi, j, 1), side(tmp, j % 2, 1), ACT.Square).then_inc(act2_hi, 1)
                    if q < QUARTERS - 1:
                        for n in range(KT):
                            ahead2(("w2", l, q, n))

            act.wait_ge(x_ready, 8 + 8 * DEPTH)
            act.dma_start(h.rearrange("p (t n) -> p t n", n=512)[:, :, 0:256],
                          ctx_in.rearrange("p (t n) -> p t n", n=256)).then_inc(late_in, 16)
            act.dma_start(const2, const2_in).then_inc(late_in, 16)
            for k in range(KT):
                sc.activation(side(sq2, k, 1), tile(x, k), ACT.Square).then_inc(sq2_ready, 1)
            root2(("ss", "first"))
            act.wait_ge(late_in, 32)
            squares2(True, lambda k: act.wait_ge(h_ready, k + 1))
            root2(("ss", 0, 0))
            pad3 = padded.rearrange("p (b s n) -> p b s n", b=2, s=2)
            modulate_tile(0, 0, 0, lambda t, s: pad3[:, t % 2, s, 8:264])
            for t in range(KT):
                if t + 1 < KT:
                    modulate_tile(0, 0, t + 1, lambda t, s: pad3[:, t % 2, s, 8:264])
                act.wait_ge(pooled, t + 1)
                sc.activation(tile(m_hi, t, 512), tile(tmp, t % 2, 512), ACT.Copy).then_inc(pooled_hi, 1)
                if t == 0:
                    ahead2(("pool", KT - 1), -AHEAD)
            scaled_before += KT
            squares2(True, lambda k: moved_out2(("pool", k)))
            root2(("ss", 0, 1))
            modulated(0, 1)
            hidden2(0)
            squares2(True, lambda k: moved_out2(("w2", 0, QUARTERS - 1, k)))
            root2(("ss", 1, 0))
            modulated(1, 0)
            for j in range(8):
                ahead2(("q", j))
                if j >= 2:
                    act.wait_ge(qcol_done, j - 1)
                act.wait_ge(gemm_done, FIRST_GEMM2 + TILE_NO2[("q", j)] + 1)
                sc.activation(tile(hsq, j % 2, 512)[:, 0:256], bank[(FIRST_TILE2 + TILE_NO2[("q", j)]) % N_BANKS][:, 0:256],
                              ACT.Square).then_inc(hsq_ready, 1)
            act.wait_ge(qms_ready, 1)
            sc.activation(qcol, qcol, ACT.Sqrt).then_inc(qsd_ready, 1)
            for t in K_TILES:
                j = t[1]
                if t[0] == "k":
                    moved_out2(t)
                    if j < 2:
                        act.wait_ge(qcol_done, 6 + j + 1)
                    else:
                        act.wait_ge(gemm_done, FIRST_GEMM2 + TILE_NO2[("kss", j - 2)] + 1)
                    sc.activation(tile(hsq, j % 2, 512), tile(k2, j, 512), ACT.Square).then_inc(hsq_ready, 1)
                elif t[0] == "kss":
                    moved_out2(t)
                    sc.activation(var2, var2, ACT.Sqrt).then_inc(hsd_ready, 1)
            ahead2(("v", 3))

            def exp2(u):
                act.wait_ge(max2_done, u + 1)
                sc.activation(probs2[u % 3], s_bank[u % 2][:, :], ACT.Exp, scale=qneg[:, u:u + 1],
                              bias=peak[:, u:u + 1], accum_out=rsum[u % 2]).then_inc(exp2_done, 1)

            def move2(u):
                act.wait_ge(t2_done, u + 1)
                if u >= 2:
                    act.wait_ge(pv2_done, u - 1)
                sc.activation(tile(pt2, u % 2, 512), t_bank[:, :], ACT.Copy).then_inc(pt2_done, 1)

            for i in range(19):
                if i < 16:
                    exp2(i)
                if 2 <= i < 18:
                    move2(i - 2)
                if i >= 4 and i % 2 == 0:
                    hd = (i - 4) // 2
                    act.wait_ge(o2_out, hd + 1)
                    sc.activation(tile(oh_hi, hd), o32b, ACT.Copy).then_inc(o2_hi, 1)
            squares2(False, lambda k: moved_out2(("o", k)))
            root2(("ss", 1, 1))
            modulated(1, 1)
            hidden2(1)
            squares2(False, lambda k: moved_out2(("w2", 1, QUARTERS - 1, k)))
            root2(("ss", "last"))

        @block.vector
        def _(dve):
            v = nc.vector

            def low_part(lo, value, hi, scale=None):
                if scale is None:
                    return v.tensor_tensor(lo, value, hi.bitcast(F32), ALU.subtract)
                return v.scalar_tensor_tensor(out=lo, in0=value, scalar=scale, in1=hi.bitcast(F32),
                                              op0=ALU.mult, op1=ALU.subtract)

            def half_log1p(y, s, s2, p):
                half_log1p_ratio(y, s, s2)
                half_log1p_series(s, s2, p)

            def half_log1p_ratio(y, s, s2):
                v.tensor_scalar(s, y, 2.0, None, ALU.add)
                v.drain()
                v.reciprocal(s2, s)
                v.drain()
                v.tensor_tensor(s, y, s2, ALU.mult)
                v.drain()
                v.tensor_tensor(s2, s, s, ALU.mult)
                v.drain()

            def half_log1p_series(s, s2, p):
                v.tensor_scalar(p, s2, 1.0 / 15, None, ALU.mult)
                for d in (13, 11, 9, 7, 5, 3):
                    v.drain()
                    v.scalar_tensor_tensor(out=p, in0=p, scalar=1.0 / d, in1=s2, op0=ALU.add, op1=ALU.mult)
                v.drain()
                v.scalar_tensor_tensor(out=p, in0=p, scalar=1.0, in1=s, op0=ALU.add, op1=ALU.mult)
                v.drain()

            def take_modulation(t, b, rows, turned, columns):
                if t[0] == "ada":
                    at = t[1] % 2 * 256
                    v.tensor_copy(rows[0:4, at:at + 256], b[0:4, 0:256]).then_inc(tiles_out, 1)
                    return
                v.tensor_copy(turned, b[:, 0:16]).then_inc(tiles_out, 1)
                v.drain()
                t4 = turned.rearrange("p (i a s) -> p i a s", a=2, s=2)
                m = mod[:, columns(2 * t[1], 4)].rearrange("p (i s) -> p i s", s=2)
                v.tensor_tensor(m, t4[:, :, 0, :], t4[:, :, 1, :], ALU.add)
                v.drain()
                bias = par2[:, PAR2["ada_b"]:PAR2["ada_b"] + DEPTH * MOD_T][:, columns(2 * t[1], 2)]
                for s in range(2):
                    v.tensor_tensor(m[:, :, s], m[:, :, s], bias, ALU.add)
                v.drain()

            dve.wait_ge(start_in, 32)
            v.memset(eps_col, EPS)
            v.memset(stat[:, 10:11], 0.0).then_inc(tiles_out, FREE_BANKS)
            v.memset(stat[:, 11:12], 0.0).then_inc(lg_done, 2)
            v.memset(stat[:, 12:13], 0.0).then_inc(o_out, 2)
            v.memset(stat[:, 13:14], 0.0).then_inc(x_ready, 8)
            for k in range(KT):
                v.tensor_scalar(silu_c[:, k * P:(k + 1) * P], par2[:, 0:P], 0.0, None, ALU.mult)
            dve.wait_ge(silu_act, 1)
            v.scalar_tensor_tensor(out=svec[:, 16:32], in0=svec[:, 0:16], scalar=1.0,
                                   in1=par2[:, PAR2["cc"]:PAR2["cc"] + 16], op0=ALU.add, op1=ALU.mult)
            v.drain()
            v.tensor_scalar(svec[:, 16:32], svec[:, 16:32], 0.5, None, ALU.mult).then_inc(silu_act, 1)
            dve.wait_ge(silu_act, 3)
            s4 = silu_c.rearrange("p (k n) -> p k n", n=P)
            low_part(s4[:, :, 2:4], svec[:, 16:32].rearrange("p (k s) -> p k s", s=2), s4[:, :, 0:2])\
                .then_inc(silu_ready, 1)

            dve.wait_ge(x_in_done, 16)
            with dve.Fori(0, DEPTH) as lay:
                def arrived(t, drain=False):
                    for m in BEFORE[t]:
                        dve.wait_ge(gemm_done, lay * N_TILES + TILE_NO[m] + 1)
                        take_modulation(m, bank[TILE_NO[m] % N_BANKS], rows, turned,
                                        lambda n, w: bass.ds(lay * (LAYER_ADA * w) + n * w, 2 * w))
                    if drain:
                        v.drain()
                    dve.wait_ge(gemm_done, lay * N_TILES + TILE_NO[t] + 1)
                    return bank[TILE_NO[t] % N_BANKS]

                def left(instr, t):
                    instr.then_inc(tiles_out, 1 if t != TILES[-1] else 1 + TILES_PER_LAYER - N_TILES)

                def scaled(t, dst, rstd, factor=None):
                    b = arrived(t)[:, 0:256]
                    if factor is None:
                        left(v.tensor_tensor(dst, b, rstd, ALU.mult), t)
                    else:
                        left(v.scalar_tensor_tensor(out=dst, in0=b, scalar=factor, in1=rstd, op0=ALU.mult,
                                                    op1=ALU.mult), t)

                def norm_tile(name, k, src, g, hi, lo, sq, n):
                    if k:
                        v.drain()
                    dve.wait_ge(nhi_ready, lay * NORM_TILES + NORM_FIRST[name] + k + 1)
                    low_part(tile(lo, k), tile(src, k), tile(hi, k), Cp(g, k)).then_inc(nlo_ready, 1)
                    if k:
                        ins = v.tensor_tensor(tile(sq, 0), tile(sq, 0), tile(sq, k), ALU.add)
                        if k == n - 1:
                            ins.then_inc(sum_ready, 1)

                def ffn_norm(k):
                    norm_tile("ffn", k, x, "ffn_g", xa_hi, xa_lo, sqx, 8)

                def ple_norm(k):
                    norm_tile("ple", k, x, "ple_g", xb_hi, xb_lo, sqx, 8)

                def norm_rstd(name, dst, n):
                    b = arrived(("ss", name))[:, 0:256]
                    left(v.tensor_scalar(yt, b, 1.0 / n, EPS, ALU.mult, ALU.add), ("ss", name))
                    dve.wait_ge(sd_ready, lay * N_NORMS + NORM_NO[name] + 1)
                    v.reciprocal(dst, yt).then_inc(rstd_ready, 1)
                    v.drain()

                def logits(kind, u):
                    U = (0 if kind == "mla" else 16) + u
                    nk = P * (u % 2 + 1)
                    mask = C("mask_" + kind)[:, 256 - nk:256]
                    dve.wait_ge(s_done, lay * UNITS + U + 1)
                    v.memset(stat[:, 20:21], 0.0)
                    v.tensor_tensor_reduce(out=tile(lg, u % 2)[:, 0:nk], in0=s_bank[u % 2][:, 0:nk], in1=mask,
                                           scale=1.0, scalar=3.0e38, op0=ALU.add, op1=ALU.min,
                                           accum_out=nmax[u % 2]).then_inc(lg_done, 1)

                def normalise(kind, u):
                    U = (0 if kind == "mla" else 16) + u
                    nk = P * (u % 2 + 1)
                    dve.wait_ge(exp_done, lay * UNITS + U + 1)
                    v.reciprocal(rinv, rsum[u % 2])
                    v.drain()
                    p = tile(pr, u % 2)[:, 0:nk]
                    v.tensor_scalar(p, p, rinv, None, ALU.mult).then_inc(p_done, 1)

                def pair_out(kind, pair):
                    v.drain()
                    dve.wait_ge(pv_done, lay * UNITS + (pair * 4 + 4 + 2))
                    v.tensor_copy(o32, o_bank[:, (pair % 2) * 256:(pair % 2) * 256 + 256]).then_inc(o_out, 1)

                def pair_lo(kind, pair):
                    dve.wait_ge(ohi_ready, lay * PAIRS + pair + 1)
                    hi, lo = (mo_hi, mo_lo) if kind == "mla" else (fo_hi, fo_lo)
                    low_part(tile(lo, pair % 4), o32, tile(hi, pair % 4)).then_inc(olo_ready, 1)

                def lru_core(j):
                    T, I, X, R = tile(tr, j), tile(ti, j), tile(xc, j), tile(rec, j % 2)
                    if j == 0:
                        dve.wait_ge(lru_act, lay * 7 + 7)
                    v.tensor_scalar(R, T, -1.0, 1.0, ALU.mult, ALU.add)
                    v.drain()
                    v.reciprocal(R, R)
                    v.scalar_tensor_tensor(out=I, in0=I, scalar=1.0, in1=X, op0=ALU.add, op1=ALU.mult)
                    v.drain()
                    v.scalar_tensor_tensor(out=T, in0=T, scalar=1.0, in1=R, op0=ALU.add, op1=ALU.mult)
                    v.tensor_tensor(I, I, R, ALU.mult)
                    v.drain()
                    v.tensor_tensor(I, I, tile(sq_lru, j), ALU.mult)
                    v.drain()
                    v.tensor_tensor_scan(X, T, I, 0.0, ALU.mult, ALU.add)
                    v.drain()
                    v.scalar_tensor_tensor(out=X, in0=X, scalar=0.5, in1=tile(gl, j), op0=ALU.mult, op1=ALU.mult)\
                        .then_inc(lru_done, 1)

                def lru_lo_part(j):
                    dve.wait_ge(lruhi_ready, lay * 4 + j + 1)
                    low_part(tile(lru_lo, j), tile(xc, j), tile(lru_hi, j)).then_inc(lrulo_ready, 1)

                def hidden_lo(half, j):
                    dve.wait_ge(hhi_ready, lay * FF_T + half * HALF_T + j + 1)
                    low_part(tile(h_lo, j), tile(hid, j % 2), tile(h_hi, j)).then_inc(hlo_ready, 1)

                def merged_lo(n):
                    dve.wait_ge(mhi_ready, lay * 8 + n + 1)
                    low_part(tile(xb_lo, n), tile(merged, n), tile(xb_hi, n), 0.5).then_inc(mlo_ready, 1)

                def of_tile(t):
                    kind, j = t[0], t[-1]
                    if kind == "g":
                        b = arrived(t, drain=True)[:, 0:256]
                        left(v.tensor_tensor(tile(gt, j % 2), b, rstd_x, ALU.mult), t)
                    elif kind == "y":
                        b = arrived(t)[:, 0:256]
                        dve.wait_ge(gate_tanh, lay * N_GATES + gate_no(("g", t[1], j)) + 1)
                        if t[1] == 0:
                            left(v.scalar_tensor_tensor(out=tile(merged, j), in0=tile(gt, j % 2), scalar=1.0, in1=b,
                                                        op0=ALU.add, op1=ALU.mult), t)
                        else:
                            left(v.scalar_tensor_tensor(out=yt, in0=tile(gt, j % 2), scalar=1.0, in1=b,
                                                        op0=ALU.add, op1=ALU.mult), t)
                            v.drain()
                            ins = v.tensor_tensor(tile(merged, j), tile(merged, j), yt, ALU.add)
                            if t[1] == 2:
                                ins.then_inc(merged_ready, 1)
                                if j:
                                    merged_lo(j - 1)
                    elif kind == "fl":
                        b = arrived(t)[:, 0:256]
                        left(v.tensor_tensor(f_z, b, rstd_x, ALU.mult), t)
                        v.drain()
                        v.tensor_scalar(f_z, f_z, Cp("bf"), -1.0, ALU.add, ALU.mult)
                        v.drain()
                        v.scalar_tensor_tensor(out=f_ab, in0=f_z, scalar=-1.0, in1=f_z, op0=ALU.mult, op1=ALU.max)\
                            .then_inc(fl_abs, 1)
                    elif kind == "fq":
                        scaled(t, tile(fq, j), rstd_x, -FOX_SCALE)
                    elif kind == "fk":
                        scaled(t, tile(fk, j), rstd_x)
                    elif kind in ("wo", "dn"):
                        b = arrived(t)[:, 0:256]
                        ins = v.tensor_tensor(tile(x, j), b, tile(x, j), ALU.add)
                        left(ins, t)
                    elif kind == "hg":
                        b = arrived(t, drain=True)[:, 0:256]
                        left(v.tensor_tensor(tile(gt, j % 2), b, rstd_x, ALU.mult), t)
                        if j:
                            hidden_lo(t[1], j - 1)
                    elif kind == "hu":
                        b = arrived(t)[:, 0:256]
                        left(v.tensor_tensor(ut, b, rstd_x, ALU.mult), t)
                        dve.wait_ge(gate_tanh, lay * N_GATES + gate_no(("hg", t[1], j)) + 1)
                        g = tile(gt, j % 2)
                        v.scalar_tensor_tensor(out=g, in0=tile(th, j % 2), scalar=1.0, in1=g, op0=ALU.add,
                                               op1=ALU.mult)
                        v.drain()
                        v.scalar_tensor_tensor(out=tile(hid, j % 2), in0=g, scalar=0.5, in1=ut, op0=ALU.mult,
                                               op1=ALU.mult).then_inc(hid_ready, 1)
                    elif kind == "pg":
                        b = arrived(t, drain=True)[:, 0:256]
                        left(v.tensor_tensor(tile(gt, j % 2), b, rstd_x, ALU.mult), t)
                    elif kind == "pp":
                        b = arrived(t)[:, 0:256]
                        dve.wait_ge(gate_tanh, lay * N_GATES + gate_no(("pg", j)) + 1)
                        left(v.scalar_tensor_tensor(out=yt, in0=tile(gt, j % 2), scalar=1.0, in1=b, op0=ALU.add,
                                                    op1=ALU.mult), t)
                        v.drain()
                        v.scalar_tensor_tensor(out=tile(x, j), in0=yt, scalar=0.5, in1=tile(x, j), op0=ALU.mult,
                                               op1=ALU.add).then_inc(x_ready, 1)

                v.tensor_copy(cur, par[:, bass.ds(lay * NPAR, NPAR)])
                v.drain()
                v.tensor_scalar(hgb, cur[:, PAR["gate_b"]:PAR["gate_b"] + 24], 0.5, None, ALU.mult)\
                    .then_inc(par_ready, 1)
                lam = cur[:, PAR["lam"]:PAR["lam"] + 4]
                v.scalar_tensor_tensor(out=small[:, 0:4], in0=lam, scalar=-1.0, in1=lam, op0=ALU.mult, op1=ALU.max)\
                    .then_inc(lam_abs, 1)
                v.memset(u_pad.rearrange("p (j n) -> p j n", n=259)[:, :, 0:3], 0.0)
                for k in range(8):
                    norm_tile("mix", k, x, "mix_g", xa_hi, xa_lo, sqx, 8)
                norm_rstd("mix", rstd_x, D)
                dve.wait_ge(lam_exp, lay + 1)
                half_log1p(small[:, 4:8], small[:, 8:12], small[:, 12:16], small[:, 16:20])
                v.tensor_scalar(small[:, 20:24], lam, -1.0, 0.0, ALU.mult, ALU.max)
                v.drain()
                v.scalar_tensor_tensor(out=small[:, 16:20], in0=small[:, 16:20], scalar=2.0, in1=small[:, 20:24],
                                       op0=ALU.mult, op1=ALU.add)
                v.drain()
                v.tensor_scalar(m2sp, small[:, 16:20], -2.0, None, ALU.mult).then_inc(m2sp_ready, 1)
                for j in range(4):
                    b = arrived(("u", j))[:, 0:256]
                    left(v.tensor_tensor(u_pad[:, j * 259 + 3:(j + 1) * 259], b, rstd_x, ALU.mult), ("u", j))
                for j in range(4):
                    scaled(("gl", j), tile(gl, j), rstd_x)
                v.drain()
                dve.wait_ge(xc_begun, lay * 4 + 4)
                for kk in range(1, CONV):
                    if kk > 1:
                        v.drain()
                    for j in range(4):
                        last = v.scalar_tensor_tensor(out=tile(xc, j), in0=u_pad[:, j * 259 + kk:j * 259 + kk + 256],
                                                      scalar=Cp("conv_w", 4 * kk + j), in1=tile(xc, j),
                                                      op0=ALU.mult, op1=ALU.add)
                last.then_inc(xc_done, 1)
                dve.wait_ge(gl_sq, lay * 4 + 4)
                v.tensor_scalar(tr, tr, 0.044715, 1.0, ALU.mult, ALU.add)
                v.drain()
                v.tensor_tensor(tr, tr, gl, ALU.mult).then_inc(gl_inner, 1)
                dve.wait_ge(xchi_ready, lay + 1)
                low_part(xc_lo, xc, xc_hi).then_inc(xclo_ready, 1)
                dve.wait_ge(gl_tanh, lay + 1)
                v.scalar_tensor_tensor(out=gl, in0=tr, scalar=1.0, in1=gl, op0=ALU.add, op1=ALU.mult)
                v.drain()

                def q_norm(k):
                    norm_tile("q", k, c_raw, "q_g", cn_hi, cn_lo, c_sq, 3)

                def kv_norm(k):
                    norm_tile("kv", k, c_raw[:, 768:], "kv_g", cn_hi[:, 768:], cn_lo[:, 768:], rec, 2)

                for j in range(3):
                    scaled(("cq", j), tile(c_raw, j), rstd_x)
                    if j:
                        q_norm(j - 1)
                scaled(("ckv", 0), tile(c_raw, 3), rstd_x)
                q_norm(2)
                scaled(("ckv", 1), tile(c_raw, 4), rstd_x)
                kv_norm(0)
                scaled(("kr", 0), krz, rstd_x)
                kv_norm(1)
                norm_rstd("q", rstd_q, 384)
                norm_rstd("kv", rstd_kv, 256)
                b = arrived(("col", "mix"))
                left(v.tensor_copy(rcol[:, 0:2], b[:, 0:2]), ("col", "mix"))
                v.drain()
                for kind, dst, bias in (("wa", tr, "ba"), ("wx", ti, "bx")):
                    for j in range(4):
                        b = arrived((kind, j))[:, 0:256]
                        left(v.tensor_scalar(tile(dst, j), b, Cp(bias, j), 0.5, ALU.add, ALU.mult), (kind, j))

                def rotate(t, z):
                    b = arrived(t)[:, 0:256]
                    left(v.tensor_tensor(yt, b, C("sin"), ALU.mult), t)
                    v.tensor_tensor(z, z, C("cos"), ALU.mult)
                    v.drain()
                    return v.tensor_tensor(z, z, yt, ALU.add)

                dve.wait_ge(const_in_done, 16)
                rotate(("rotk", 0), krz)
                v.drain()
                for s in range(2):
                    v.tensor_scalar(tile(krm, s), krz, C("sub")[:, s:s + 1], None, ALU.mult)
                for m in range(2):
                    b = arrived(("fv", m))
                    left(v.tensor_scalar(tile(vf, m, 512), b[:, :], rcol[:, m:m + 1], None, ALU.mult), ("fv", m))
                b = arrived(("col", "kv"))
                left(v.tensor_copy(rcol[:, 2:4], b[:, 0:2]), ("col", "kv"))
                v.drain()
                for m in range(2):
                    b = arrived(("vm", m))
                    left(v.tensor_scalar(tile(vm, m, 512), b[:, :], rcol[:, 2 + m:3 + m], None, ALU.mult), ("vm", m))
                lru_core(0)
                for j in range(4):
                    scaled(("kn", j), tile(kn, j), rstd_kv)
                lru_core(1)
                lru_lo_part(0)
                for j in range(4):
                    scaled(("qn", j), tile(qn, j), rstd_q, -MLA_SCALE)
                lru_core(2)
                lru_lo_part(1)
                for j in range(2):
                    scaled(("qr", j), tile(qr, j), rstd_q, -MLA_SCALE)
                v.drain()
                for j in range(2):
                    last = rotate(("rotq", j), tile(qr, j))
                    v.drain()
                v.memset(stat[:, 17:18], 0.0).then_inc(mla_ready, 1)
                lru_lo_part(2)

                for kind, fill in (("mla", MLA_FILL), ("fox", FOX_FILL)):
                    first_pair = 0 if kind == "mla" else 4
                    for i in range(17):
                        if i < 16:
                            logits(kind, i)
                            normalise(kind, i)
                        if kind == "mla" and i == 1:
                            lru_core(3)
                        if kind == "mla" and i == 3:
                            lru_lo_part(3)
                        if i < 16:
                            of_tile(fill[i])
                        if kind == "mla" and i == 5:
                            dve.wait_ge(fl_exp, lay + 1)
                            half_log1p_ratio(f_den, f_s, f_s2)
                        if kind == "mla" and i == 7:
                            half_log1p_series(f_s, f_s2, f_p)
                        if kind == "mla" and i == 9:
                            v.tensor_scalar(f_z, f_z, 0.0, None, ALU.max)
                            v.drain()
                            v.scalar_tensor_tensor(out=f_p, in0=f_p, scalar=2.0, in1=f_z, op0=ALU.mult, op1=ALU.add)
                            v.drain()
                            v.tensor_tensor_scan(f_z, ones, f_p, 0.0, ALU.mult, ALU.subtract)
                            v.drain()
                            for r in (0, 64):
                                v.tensor_copy(rk[r:r + 32], f_z[r:r + 32])
                                v.memset(rk[r + 32:r + 64], 1.0)
                                v.memset(lq[r:r + 32], 1.0)
                                v.tensor_scalar(lq[r + 32:r + 64], f_z[r + 32:r + 64], -1.0, None, ALU.mult)
                            v.drain()
                            v.memset(stat[:, 18:19], 0.0).then_inc(decay_ready, 1)
                        if i and i % 4 == 0:
                            pair_out(kind, first_pair + (i - 1) // 4)
                            pair_lo(kind, first_pair + (i - 1) // 4)
                for t in MID_TILES:
                    if t[0] not in ("ada", "turn"):
                        of_tile(t)
                merged_lo(7)
                for n in range(8):
                    of_tile(("wo", n))
                    if n:
                        ffn_norm(n - 1)
                ffn_norm(7)
                norm_rstd("ffn", rstd_x, D)
                for half in range(2):
                    for j in range(HALF_T):
                        of_tile(("hg", half, j))
                        of_tile(("hu", half, j))
                    hidden_lo(half, HALF_T - 1)
                    if half == 1:
                        dve.wait_ge(phi_ready, lay + 1)
                        low_part(p_lo, p_raw, p_hi).then_inc(plo_ready, 1)
                    for n in range(8):
                        of_tile(("dn", half, n))
                        if half == 1 and n:
                            ple_norm(n - 1)
                ple_norm(7)
                norm_rstd("ple", rstd_x, D)
                for t in PLE_TILES:
                    if t[0] != "turn":
                        of_tile(t)

            def take_before2(t):
                while BEFORE2[t]:
                    m = BEFORE2[t].pop(0)
                    dve.wait_ge(gemm_done, FIRST_GEMM2 + TILE_NO2[m] + 1)
                    take_modulation(m, bank[(FIRST_TILE2 + TILE_NO2[m]) % N_BANKS], rows2, turned2,
                                    lambda n, w: slice(n * w, (n + 2) * w))

            def arrived2(t):
                take_before2(t)
                dve.wait_ge(gemm_done, FIRST_GEMM2 + TILE_NO2[t] + 1)
                return bank[(FIRST_TILE2 + TILE_NO2[t]) % N_BANKS]

            squared = 0

            def sum_square(t, k):
                nonlocal squared
                squared += 1
                if k:
                    v.drain()
                    a = slice(0, 512) if t[1:] in ((0, 0), (0, 1), (1, 0)) else slice(256, 512)
                    dve.wait_ge(sq2_ready, squared)
                    ins = v.tensor_tensor(tile(sq2, 0, 512)[:, a], tile(sq2, 0, 512)[:, a], tile(sq2, k, 512)[:, a],
                                          ALU.add)
                    if k == KT - 1:
                        ins.then_inc(sum2_ready, 1)

            roots = 0

            def norm_rstd2(t):
                nonlocal roots
                b = arrived2(t)
                wide = t[1:] in ((0, 0), (0, 1), (1, 0))
                w = 512 if wide else 256
                a = slice(0, 512) if wide else slice(256, 512)
                v.drain()
                v.tensor_scalar(var2[:, a], b[:, 0:w], 1.0 / D, EPS, ALU.mult, ALU.add).then_inc(tiles_out, 1)
                roots += 1
                dve.wait_ge(sd2_ready, roots)
                v.reciprocal(rstd2[:, a], var2[:, a])
                v.drain()

            def scale_tile(l, i, t):
                a = slice(0, 512) if len(sides(l, i)) == 2 else slice(256, 512)
                v.tensor_tensor(tile(tmp, t % 2, 512)[:, a], tile(h, t, 512)[:, a], rstd2[:, a], ALU.mult)\
                    .then_inc(scaled2, 1)

            acted = 0

            def modulated(l, i):
                nonlocal acted
                a = slice(0, 512) if len(sides(l, i)) == 2 else slice(256, 512)
                for t in range(KT + 1):
                    if t < KT:
                        scale_tile(l, i, t)
                    v.drain()
                    if t < KT:
                        v.tensor_scalar(side(squares, t % 2, 1), side(tmp, t % 2, 1), gain_col(l, i, t, 1),
                                        mod_col(l, SH1 if i == 0 else SH2, t, 1), ALU.mult, ALU.add)
                    if t:
                        dve.wait_ge(m_act, acted + t)
                        low_part(tile(m_lo, t - 1, 512)[:, a], tile(squares, (t - 1) % 2, 512)[:, a],
                                 tile(m_hi, t - 1, 512)[:, a]).then_inc(m_split, 1)
                acted += KT

            def add_gated(t, n, col, s_list, whole):
                b = arrived2(t)
                for s in s_list:
                    src = b[:, s * 256:(s + 1) * 256] if whole else b[:, 0:256]
                    last = v.scalar_tensor_tensor(out=side(h, n, s), in0=src, scalar=col(s), in1=side(h, n, s),
                                                  op0=ALU.mult, op1=ALU.add)
                last.then_inc(tiles_out, 1)

            def hidden2(l):
                after = ("ss", 1, 0) if l == 0 else ("ss", "last")
                a = slice(0, 512) if l == 0 else slice(256, 512)
                w = 512 if l == 0 else 256

                for q in range(QUARTERS):
                    for j in range(QT + 2):
                        if j < QT:
                            b = arrived2(("w1", l, q, j))
                        if j >= 2:
                            dve.wait_ge(act2_hi, (l * QUARTERS + q) * QT + j - 1)
                        v.drain()
                        if j < QT:
                            v.tensor_scalar(tile(tmp, j % 2, 512)[:, a], b[:, 0:w], 0.0, None, ALU.max)\
                                .then_inc(tiles_out, 1)
                        if 1 <= j <= QT:
                            r = tile(tmp, (j - 1) % 2, 512)[:, a]
                            v.tensor_tensor(tile(squares, (j - 1) % 2, 512)[:, a], r, r, ALU.mult)
                        if j >= 2:
                            low_part(tile(hid_lo, j - 2, 512)[:, a], tile(squares, j % 2, 512)[:, a],
                                     tile(hid_hi, j - 2, 512)[:, a]).then_inc(act2_lo, 1)
                    v.drain()
                    for n in range(KT):
                        add_gated(("w2", l, q, n), n, lambda s: mod_col(l, G2, n, s), (0, 1) if l == 0 else (1,),
                                  l == 0)
                        if q == QUARTERS - 1 and n:
                            sum_square(after, n - 1)
                    v.drain()
                sum_square(after, KT - 1)

            v.drain()
            v.tensor_scalar(qg_scaled, par2[:, PAR2["q_g"]:PAR2["q_g"] + 1], -GQA_SCALE, None, ALU.mult)
            for k in range(KT):
                sum_square(("ss", "first"), k)
            norm_rstd2(("ss", "first"))
            dve.wait_ge(late_in, 32)
            for t in range(KT):
                v.scalar_tensor_tensor(out=side(h, t, 1), in0=tile(x, t),
                                       scalar=par2[:, PAR2["first_g"] + t:PAR2["first_g"] + t + 1],
                                       in1=rstd2[:, 256:512], op0=ALU.mult, op1=ALU.mult).then_inc(h_ready, 1)
                if t:
                    sum_square(("ss", 0, 0), t - 1)
            sum_square(("ss", 0, 0), KT - 1)
            mods = mod.rearrange("p (l k t s) -> p l k t s", l=DEPTH, k=6, s=2)
            gains = gain.rearrange("p (l i t s) -> p l i t s", l=DEPTH, i=2, s=2)

            def norm_gains(l):
                for i in range(2):
                    at = PAR2["norm_g"] + (l * 2 + i) * 8
                    for s in range(2):
                        v.scalar_tensor_tensor(out=gains[:, l, i, :, s], in0=mods[:, l, SC1 if i == 0 else SC2, :, s],
                                               scalar=1.0, in1=par2[:, at:at + 8], op0=ALU.add, op1=ALU.mult)

            norm_gains(0)
            pg2 = pool_gate.rearrange("p (t s) -> p t s", s=2)
            for s in range(2):
                v.tensor_tensor(pg2[:, :, s], mods[:, 0, G1, :, s], par2[:, PAR2["pool_scale"]:PAR2["pool_scale"] + 8],
                                ALU.mult)
            v.drain()
            pad4 = padded.rearrange("p (b s n) -> p b s n", b=2, s=2)
            v.memset(padded, 0.0)
            norm_rstd2(("ss", 0, 0))
            sums = [a.rearrange("p (s n) -> p s n", s=2) for a in (sum_a, sum_b)]

            def pool_out(t):
                add_gated(("pool", t), t, lambda s: pool_gate[:, 2 * t + s:2 * t + s + 1], (0, 1), True)

            scale_tile(0, 0, 0)
            for t in range(KT):
                v.drain()
                if t + 1 < KT:
                    if t >= 1:
                        dve.wait_ge(pooled_hi, t)
                    scale_tile(0, 0, t + 1)
                dve.wait_ge(m_act, t + 1)
                a = pad4[:, t % 2]
                src, reach = a, 1
                lo_, hi_ = 1, 272
                v.tensor_tensor(sums[0][:, :, 1:272], a[:, :, 0:271], a[:, :, 1:272], ALU.add)
                cur_, edge = 0, 1
                for step in range(t // 2):
                    d = 1 << step
                    lo_, hi_ = lo_ + d, hi_ - d
                    v.drain()
                    v.tensor_tensor(sums[1 - cur_][:, :, lo_:hi_], sums[cur_][:, :, lo_ - d:hi_ - d],
                                    sums[cur_][:, :, lo_ + d:hi_ + d], ALU.add)
                    cur_ = 1 - cur_
                v.drain()
                w = sums[cur_][:, :, 8:264]
                inv = C2("inv_count")[:, (t // 2) * 256:(t // 2 + 1) * 256]
                for s in range(2):
                    v.tensor_tensor(w[:, s], w[:, s], inv, ALU.mult)
                v.drain()
                v.tensor_tensor(tile(tmp, t % 2, 512).rearrange("p (s n) -> p s n", s=2), w, a[:, :, 8:264],
                                ALU.subtract).then_inc(pooled, 1)
                dve.wait_ge(pooled_hi, t + 1)
                low_part(tile(m_lo, t, 512), tile(tmp, t % 2, 512), tile(m_hi, t, 512)).then_inc(m_split, 1)
                if t == 0:
                    take_before2(("pool", 0))
                if t % 2 and t > 2:
                    pool_out(t - 3)
                    pool_out(t - 2)
            acted += KT
            pool_out(KT - 2)
            pool_out(KT - 1)
            for k in range(KT):
                sum_square(("ss", 0, 1), k)
            norm_rstd2(("ss", 0, 1))
            modulated(0, 1)
            hidden2(0)
            norm_gains(1)
            norm_rstd2(("ss", 1, 0))
            modulated(1, 0)

            def rotate2(t, z):
                b = arrived2(t)
                v.drain()
                v.tensor_tensor(m32[:, 0:256], b[:, 0:256], C2("sin"), ALU.mult).then_inc(tiles_out, 1)
                v.tensor_tensor(z, z, C2("cos"), ALU.mult)
                v.drain()
                v.tensor_tensor(z, z, m32[:, 0:256], ALU.add)

            for t in Q_TILES:
                if t[0] == "q":
                    b = arrived2(t)
                    dve.wait_ge(hsq_ready, t[1] + 1)
                    v.tensor_scalar(tile(q2, t[1]), b[:, 0:256], qg_scaled, None, ALU.mult).then_inc(tiles_out, 1)
                else:
                    rotate2(t, tile(q2, t[1]))
            dve.wait_ge(qcol_done, 8)
            v.tensor_scalar(qcol, t_bank[:, 0:16], 1.0 / P, EPS, ALU.mult, ALU.add).then_inc(qms_ready, 1)
            dve.wait_ge(qsd_ready, 1)
            v.reciprocal(qrstd, qcol)
            v.drain()
            v.tensor_scalar(qneg, qrstd, -1.0, None, ALU.mult)
            for t in K_TILES + V_TILES + LATE_ROTATIONS:
                j = t[1]
                if t[0] == "k":
                    v.tensor_copy(tile(k2, j, 512), arrived2(t)[:, :]).then_inc(tiles_out, 1)
                elif t[0] == "kss":
                    b = arrived2(t)
                    v.drain()
                    v.tensor_scalar(var2, b[:, :], 1.0 / P, EPS, ALU.mult, ALU.add).then_inc(tiles_out, 1)
                    dve.wait_ge(hsd_ready, j + 1)
                    v.reciprocal(rstd2, var2)
                    v.drain()
                    z = tile(k2, j, 512)
                    v.scalar_tensor_tensor(out=z, in0=z, scalar=par2[:, PAR2["k_g"]:PAR2["k_g"] + 1], in1=rstd2,
                                           op0=ALU.mult, op1=ALU.mult).then_inc(hn_ready, 1)
                elif t[0] == "v":
                    v.tensor_copy(tile(v2, j, 512), arrived2(t)[:, :]).then_inc(tiles_out, 1)
                else:
                    rotate2(t, side(k2, j, 1))
            v.drain()
            v.memset(stat[:, 19:20], 0.0).then_inc(qkv_ready, 1)

            def maximum2(u):
                dve.wait_ge(s2_done, u + 1)
                v.tensor_reduce(out=nmax[u % 2], in_=s_bank[u % 2][:, :], axis=AXX, op=ALU.min)
                v.drain()
                v.tensor_tensor(peak[:, u:u + 1], nmax[u % 2], qrstd[:, u:u + 1], ALU.mult).then_inc(max2_done, 1)

            def normalise2(u):
                dve.wait_ge(exp2_done, u + 1)
                r = stat[:, 21 + u % 2:22 + u % 2]
                v.reciprocal(r, rsum[u % 2])
                v.drain()
                p = probs2[u % 3]
                v.tensor_scalar(p, p, r, None, ALU.mult).then_inc(p2_done, 1)

            for i in range(19):
                if i < 16:
                    maximum2(i)
                if 1 <= i < 17:
                    normalise2(i - 1)
                if i >= 4 and i % 2 == 0:
                    hd = (i - 4) // 2
                    dve.wait_ge(pv2_done, 2 * hd + 2)
                    v.drain()
                    v.tensor_copy(o32b, o_banks2[hd % 2][:, 0:256]).then_inc(o2_out, 1)
                    dve.wait_ge(o2_hi, hd + 1)
                    v.drain()
                    low_part(tile(oh_lo, hd), o32b, tile(oh_hi, hd)).then_inc(o2_lo, 1)
            for n in range(KT):
                add_gated(("o", n), n, lambda s: mod_col(1, G1, n, s), (1,), False)
                if n:
                    sum_square(("ss", 1, 1), n - 1)
            sum_square(("ss", 1, 1), KT - 1)
            norm_rstd2(("ss", 1, 1))
            modulated(1, 1)
            hidden2(1)
            norm_rstd2(("ss", "last"))
            for t in range(KT):
                v.scalar_tensor_tensor(out=tile(sq2, t), in0=side(h, t, 1),
                                       scalar=par2[:, PAR2["final_g"] + t:PAR2["final_g"] + t + 1],
                                       in1=rstd2[:, 256:512], op0=ALU.mult, op1=ALU.mult).then_inc(result_ready, 1)


def kernel(**inputs):
    import concourse.bacc as bacc
    from concourse.bass_utils import run_bass_kernel_spmd

    a = {k: np.asarray(v) for k, v in inputs.items()}
    const, const2 = shape_constants()
    par, par2 = pack_parameters(a)
    arrays = {
        "stream": pack_stream(a),
        "x": token_minor(a["x"][0]),
        "ctx": token_minor(a["ctx_2"][0]),
        "p": np.stack([token_minor(a["p"][l, 0]) for l in range(DEPTH)]),
        "par": par,
        "par2": par2,
        "const": const,
        "const2": const2,
    }
    nc = bacc.Bacc("TRN2", target_bir_lowering=False, num_devices=1)
    ins = [nc.dram_tensor(f"in_{n}", list(v.shape), F32, kind="ExternalInput").ap() for n, v in arrays.items()]
    out = nc.dram_tensor("out_0", [P, KT * S], F32, kind="ExternalOutput").ap()
    build(nc, ins, out)
    r = run_bass_kernel_spmd(nc, [{f"in_{n}": v for n, v in arrays.items()}], core_ids=[0])
    got = r.results[0]["out_0"]
    return np.ascontiguousarray(np.asarray(got).reshape(P, KT, S).transpose(2, 1, 0).reshape(1, S, D))
```
